# Optimizing a Trainium2 kernel written in Bass

```python
import math
import jax, jax.numpy as jnp
from jax import lax
import numpy as np

D_MODEL = 1024
BATCH = 1
SEQ = 1024
DEPTH = 1

CHUNK = 64
N_MIXERS = 4
EPS = 1e-6
GLA_HEADS = 4
GLA_DK = (D_MODEL // 2) // GLA_HEADS
GLA_DV = D_MODEL // GLA_HEADS
GLA_GATE_RANK = 16
GLA_TAU = 16.0
GLA_IN = 2 * GLA_HEADS * GLA_DK + 2 * GLA_HEADS * GLA_DV + GLA_GATE_RANK
POOL_WINDOWS = (2, 4, 8, 16)
POOL_GROUPS = len(POOL_WINDOWS)
POOL_GW = D_MODEL // POOL_GROUPS
SSD_DINNER = 2 * D_MODEL
SSD_HEADDIM = 64
SSD_HEADS = SSD_DINNER // SSD_HEADDIM
SSD_GROUPS = 4
SSD_HPG = SSD_HEADS // SSD_GROUPS
SSD_STATE = 128
SSD_CONV = 4
SSD_CONV_DIM = SSD_DINNER + 2 * SSD_GROUPS * SSD_STATE
SSD_IN = SSD_DINNER + SSD_CONV_DIM + SSD_HEADS
SB_HEADS = 16
SB_HEADDIM = D_MODEL // SB_HEADS
SB_QBLOCK = 128
FFN_DIM = 2816
FFN_CONV = 3


def rms_normalize(x):
    xf = x.astype(jnp.float32)
    y = xf * lax.rsqrt(jnp.mean(xf * xf, axis=-1, keepdims=True) + EPS)
    return y.astype(x.dtype)

def rmsnorm(x, w):
    return rms_normalize(x) * w

def causal_dwconv(u, w, b):
    K = w.shape[0]
    L = u.shape[1]
    up = jnp.pad(u, ((0, 0), (K - 1, 0), (0, 0)))
    out = up[:, K - 1:K - 1 + L] * w[K - 1] + b
    for k in range(K - 1):
        out = out + up[:, k:k + L] * w[k]
    return out

def to_chunks(a):
    b_, l_ = a.shape[:2]
    return jnp.moveaxis(a.reshape(b_, l_ // CHUNK, CHUNK, *a.shape[2:]), 1, 0)

def from_chunks(a):
    a = jnp.moveaxis(a, 0, 1)
    return a.reshape(a.shape[0], a.shape[1] * a.shape[2], *a.shape[3:])

def gla_mixer(h, w_in, w_gate2, b_gate, norm_w, w_out):
    b_, l_, _ = h.shape
    hk, hv = GLA_HEADS * GLA_DK, GLA_HEADS * GLA_DV
    proj = h @ w_in
    q, k, v, r, glr = jnp.split(proj, [hk, 2 * hk, 2 * hk + hv, 2 * hk + 2 * hv], axis=-1)
    q = q.reshape(b_, l_, GLA_HEADS, GLA_DK).astype(jnp.float32) * (GLA_DK ** -0.5)
    k = k.reshape(b_, l_, GLA_HEADS, GLA_DK).astype(jnp.float32)
    v = v.reshape(b_, l_, GLA_HEADS, GLA_DV).astype(jnp.float32)
    log_a = jax.nn.log_sigmoid((glr @ w_gate2 + b_gate).astype(jnp.float32)) / GLA_TAU
    log_a = log_a.reshape(b_, l_, GLA_HEADS, GLA_DK)
    qc, kc, vc, lac = to_chunks(q), to_chunks(k), to_chunks(v), to_chunks(log_a)
    g = jnp.cumsum(lac, axis=2)
    g_end = g[:, :, -1]
    k_dec = kc * jnp.exp(g_end[:, :, None] - g)

    def body(state, inp):
        q_c, kd_c, v_c, ge_c = inp
        state = state * jnp.exp(ge_c)[..., None] + jnp.einsum('bshk,bshv->bhkv', kd_c, v_c)
        o = jnp.einsum('bqhk,bhkv->bqhv', q_c, state)
        return state, o

    s0 = jnp.zeros((b_, GLA_HEADS, GLA_DK, GLA_DV), jnp.float32)
    _, o = lax.scan(body, s0, (qc, k_dec, vc, g_end))
    o = rms_normalize(from_chunks(o)).reshape(b_, l_, hv) * norm_w
    o = o.astype(h.dtype) * jax.nn.silu(r)
    return o @ w_out

def pool_mixer(h, w_grp, b_grp, scale):
    b_, l_, d_ = h.shape
    hf = h.astype(jnp.float32)
    cs = jnp.concatenate([jnp.zeros((b_, 1, d_), jnp.float32), jnp.cumsum(hf, axis=1)], axis=1)
    t1 = jnp.arange(1, l_ + 1, dtype=jnp.float32)
    outs = []
    for gi, win in enumerate(POOL_WINDOWS):
        sl = slice(gi * POOL_GW, (gi + 1) * POOL_GW)
        c = cs[..., sl]
        lower = jnp.concatenate([jnp.zeros((b_, win - 1, POOL_GW), jnp.float32), c[:, :l_ + 1 - win]], axis=1)
        mean = (c[:, 1:] - lower) / jnp.minimum(t1, float(win))[None, :, None]
        dlt = (mean - hf[..., sl]).astype(h.dtype)
        outs.append(dlt @ w_grp[gi] + b_grp[gi])
    return jnp.concatenate(outs, axis=-1) * scale

def ssd_mixer(h, w_in, conv_w, conv_b, dt_bias, a_log, d_skip, norm_w, w_out):
    b_, l_, _ = h.shape
    G, HG, P, N = SSD_GROUPS, SSD_HPG, SSD_HEADDIM, SSD_STATE
    proj = h @ w_in
    z, xbc, dt = jnp.split(proj, [SSD_DINNER, SSD_DINNER + SSD_CONV_DIM], axis=-1)
    xbc = jax.nn.silu(causal_dwconv(xbc, conv_w, conv_b))
    xs, bm, cm = jnp.split(xbc, [SSD_DINNER, SSD_DINNER + G * N], axis=-1)
    xs = xs.reshape(b_, l_, G, HG, P)
    bm = bm.reshape(b_, l_, G, N)
    cm = cm.reshape(b_, l_, G, N)
    dt = jax.nn.softplus((dt + dt_bias).astype(jnp.float32)).reshape(b_, l_, G, HG)
    a_h = -jnp.exp(a_log.astype(jnp.float32)).reshape(G, HG)
    causal = jnp.tril(jnp.ones((CHUNK, CHUNK), bool))

    def body(state, inp):
        x_c, b_c, c_c, dt_c = inp
        acs = jnp.cumsum(dt_c * a_h, axis=1)
        seg = acs[:, :, None] - acs[:, None, :]
        lmat = jnp.exp(jnp.where(causal[None, :, :, None, None], seg, -jnp.inf))
        xdt = x_c * dt_c[..., None]
        cb = jnp.einsum('btgn,bsgn->btsg', c_c, b_c)
        y = jnp.einsum('btsg,btsgh,bsghp->btghp', cb, lmat, xdt)
        y = y + jnp.einsum('btgn,bghpn,btgh->btghp', c_c, state, jnp.exp(acs))
        decay_end = jnp.exp(acs[:, -1:] - acs)
        state = state * jnp.exp(acs[:, -1])[..., None, None] + jnp.einsum('bsgn,bsgh,bsghp->bghpn', b_c, decay_end, xdt)
        return state, y

    s0 = jnp.zeros((b_, G, HG, P, N), jnp.float32)
    _, ys = lax.scan(body, s0, (to_chunks(xs), to_chunks(bm), to_chunks(cm), to_chunks(dt)))
    y = from_chunks(ys) + d_skip.reshape(G, HG)[..., None] * xs
    y = y.reshape(b_, l_, SSD_DINNER) * jax.nn.silu(z)
    y = rms_normalize(y.reshape(b_, l_, G, SSD_DINNER // G)).reshape(b_, l_, SSD_DINNER) * norm_w
    return y.astype(h.dtype) @ w_out

def sb_mixer(h, w_qkv, w_out):
    b_, l_, _ = h.shape
    q, k, v = jnp.split(h @ w_qkv, 3, axis=-1)
    q = q.reshape(b_, l_, SB_HEADS, SB_HEADDIM).transpose(0, 2, 1, 3) * (SB_HEADDIM ** -0.5)
    k = k.reshape(b_, l_, SB_HEADS, SB_HEADDIM).transpose(0, 2, 1, 3)
    v = v.reshape(b_, l_, SB_HEADS, SB_HEADDIM).transpose(0, 2, 1, 3)
    nb = l_ // SB_QBLOCK
    qb = jnp.moveaxis(q.reshape(b_, SB_HEADS, nb, SB_QBLOCK, SB_HEADDIM), 2, 0)
    starts = jnp.arange(nb, dtype=jnp.int32) * SB_QBLOCK
    key_pos = jnp.arange(l_, dtype=jnp.int32)

    def block(inp):
        q_i, start = inp
        zt = jnp.einsum('bhqd,bhkd->bhqk', q_i, k).astype(jnp.float32)
        qpos = start + jnp.arange(SB_QBLOCK, dtype=jnp.int32)
        mask = key_pos[None, :] < qpos[:, None]
        log_1mb = jnp.where(mask, jax.nn.log_sigmoid(-zt), 0.0)
        rc = lax.cumsum(log_1mb, axis=3, reverse=True)
        surv = jnp.concatenate([rc[..., 1:], jnp.zeros_like(rc[..., :1])], axis=-1)
        att = jnp.where(mask, jnp.exp(jax.nn.log_sigmoid(zt) + surv), 0.0)
        return jnp.einsum('bhqk,bhkd->bhqd', att.astype(v.dtype), v)

    o = lax.map(block, (qb, starts))
    o = jnp.moveaxis(o, 0, 2).reshape(b_, SB_HEADS, l_, SB_HEADDIM)
    o = o.transpose(0, 2, 1, 3).reshape(b_, l_, D_MODEL)
    return o @ w_out

def conv_ffn(h, w_up, conv_w, conv_b, w_down):
    u = causal_dwconv(h @ w_up, conv_w, conv_b)
    g, val = jnp.split(u, 2, axis=-1)
    return (jax.nn.silu(g) * val) @ w_down

def first_inputs(seed: int = 0) -> dict:
    key = jax.random.key(seed)
    ks = list(jax.random.split(key, 40))
    f32 = jnp.float32

    def nrm(i, shape, scale):
        return jax.random.normal(ks[i], shape, f32) * scale

    n_a = len(range(0, DEPTH, N_MIXERS))
    n_b = len(range(1, DEPTH, N_MIXERS))
    n_c = len(range(2, DEPTH, N_MIXERS))
    n_d = len(range(3, DEPTH, N_MIXERS))
    dt0 = jnp.exp(jax.random.uniform(ks[20], (n_c, SSD_HEADS), f32) * (math.log(0.1) - math.log(0.001)) + math.log(0.001))
    return {
        'x': nrm(0, (BATCH, SEQ, D_MODEL), 1.0),
        'mix_norm_w': 1.0 + nrm(1, (DEPTH, D_MODEL), 0.02),
        'ffn_norm_w': 1.0 + nrm(2, (DEPTH, D_MODEL), 0.02),
        'final_norm_w': 1.0 + nrm(3, (D_MODEL,), 0.02),
        'gla_w_in': nrm(4, (n_a, D_MODEL, GLA_IN), D_MODEL ** -0.5),
        'gla_w_gate2': nrm(5, (n_a, GLA_GATE_RANK, GLA_HEADS * GLA_DK), GLA_GATE_RANK ** -0.5),
        'gla_b_gate': nrm(6, (n_a, GLA_HEADS * GLA_DK), 0.1),
        'gla_norm_w': 1.0 + nrm(7, (n_a, GLA_HEADS * GLA_DV), 0.02),
        'gla_w_out': nrm(8, (n_a, GLA_HEADS * GLA_DV, D_MODEL), (GLA_HEADS * GLA_DV) ** -0.5),
        'pool_w': nrm(9, (n_b, POOL_GROUPS, POOL_GW, POOL_GW), POOL_GW ** -0.5),
        'pool_b': nrm(10, (n_b, POOL_GROUPS, POOL_GW), 0.02),
        'pool_scale': 1.0 + nrm(11, (n_b, D_MODEL), 0.02),
        'ssd_w_in': nrm(12, (n_c, D_MODEL, SSD_IN), D_MODEL ** -0.5),
        'ssd_conv_w': nrm(13, (n_c, SSD_CONV, SSD_CONV_DIM), SSD_CONV ** -0.5),
        'ssd_conv_b': nrm(14, (n_c, SSD_CONV_DIM), 0.02),
        'ssd_dt_bias': dt0 + jnp.log(-jnp.expm1(-dt0)),
        'ssd_a_log': jnp.log(jax.random.uniform(ks[15], (n_c, SSD_HEADS), f32, 1.0, 16.0)),
        'ssd_d': 1.0 + nrm(16, (n_c, SSD_HEADS), 0.02),
        'ssd_norm_w': 1.0 + nrm(17, (n_c, SSD_DINNER), 0.02),
        'ssd_w_out': nrm(18, (n_c, SSD_DINNER, D_MODEL), SSD_DINNER ** -0.5),
        'sb_w_qkv': nrm(19, (n_d, D_MODEL, 3 * D_MODEL), D_MODEL ** -0.5),
        'sb_w_out': nrm(21, (n_d, D_MODEL, D_MODEL), D_MODEL ** -0.5),
        'ffn_w_up': nrm(22, (DEPTH, D_MODEL, 2 * FFN_DIM), D_MODEL ** -0.5),
        'ffn_conv_w': nrm(23, (DEPTH, FFN_CONV, 2 * FFN_DIM), FFN_CONV ** -0.5),
        'ffn_conv_b': nrm(24, (DEPTH, 2 * FFN_DIM), 0.02),
        'ffn_w_down': nrm(25, (DEPTH, FFN_DIM, D_MODEL), FFN_DIM ** -0.5),
    }

def first_block(x, mix_norm_w, ffn_norm_w, final_norm_w,
              gla_w_in, gla_w_gate2, gla_b_gate, gla_norm_w, gla_w_out,
              pool_w, pool_b, pool_scale,
              ssd_w_in, ssd_conv_w, ssd_conv_b, ssd_dt_bias, ssd_a_log, ssd_d, ssd_norm_w, ssd_w_out,
              sb_w_qkv, sb_w_out,
              ffn_w_up, ffn_conv_w, ffn_conv_b, ffn_w_down):
    for i in range(DEPTH):
        m, j = i % N_MIXERS, i // N_MIXERS
        h = rmsnorm(x, mix_norm_w[i])
        if m == 0:
            y = gla_mixer(h, gla_w_in[j], gla_w_gate2[j], gla_b_gate[j], gla_norm_w[j], gla_w_out[j])
        elif m == 1:
            y = pool_mixer(h, pool_w[j], pool_b[j], pool_scale[j])
        elif m == 2:
            y = ssd_mixer(h, ssd_w_in[j], ssd_conv_w[j], ssd_conv_b[j], ssd_dt_bias[j], ssd_a_log[j],
                          ssd_d[j], ssd_norm_w[j], ssd_w_out[j])
        else:
            y = sb_mixer(h, sb_w_qkv[j], sb_w_out[j])
        x = x + y.astype(x.dtype)
        h = rmsnorm(x, ffn_norm_w[i])
        x = x + conv_ffn(h, ffn_w_up[i], ffn_conv_w[i], ffn_conv_b[i], ffn_w_down[i]).astype(x.dtype)
    return rmsnorm(x, final_norm_w)


D_RG = D_MODEL
RG_BLOCK_W = 256
RG_BLOCKS = D_RG // RG_BLOCK_W
CONV_W = 4
RG_C = 8.0
HG_EXPAND = 128
HG_HEADS = D_MODEL // HG_EXPAND
HG_DK = HG_EXPAND
HG_DV = D_MODEL // HG_HEADS
HG_CHUNK = 32
F_MIN = 1e-30
D_FF = 4 * D_MODEL
NORM_EPS = 1e-6
SPLIT_SIZES = (D_RG, D_RG, HG_HEADS * HG_DK, HG_HEADS * HG_DK, HG_HEADS * HG_DV, HG_HEADS * HG_DV, D_MODEL, D_MODEL)
D_IN = sum(SPLIT_SIZES)
SPLIT_POINTS = tuple(np.cumsum(SPLIT_SIZES)[:-1].tolist())


def rms_norm(x, gain):
    xf = x.astype(jnp.float32)
    y = xf * lax.rsqrt(jnp.mean(xf * xf, axis=-1, keepdims=True) + NORM_EPS)
    return (y * gain.astype(jnp.float32)).astype(x.dtype)

def causal_depthwise_conv(x, w, b):
    y = lax.conv_general_dilated(
        x, w[:, None, :].astype(x.dtype), window_strides=(1,),
        padding=((CONV_W - 1, 0),), dimension_numbers=('NWC', 'WIO', 'NWC'),
        feature_group_count=x.shape[-1])
    return y + b.astype(x.dtype)

def rg_lru(x, w_r, b_r, w_i, b_i, lam):
    B_, S_, _ = x.shape
    xf = x.astype(jnp.float32)
    xb = xf.reshape(B_, S_, RG_BLOCKS, RG_BLOCK_W)
    r = jax.nn.sigmoid(jnp.einsum('bsnj,njk->bsnk', xb, w_r.astype(jnp.float32)).reshape(B_, S_, D_RG) + b_r.astype(jnp.float32))
    i = jax.nn.sigmoid(jnp.einsum('bsnj,njk->bsnk', xb, w_i.astype(jnp.float32)).reshape(B_, S_, D_RG) + b_i.astype(jnp.float32))
    log_a = -RG_C * r * jax.nn.softplus(-lam.astype(jnp.float32))
    a = jnp.exp(log_a)
    u = jnp.sqrt(jnp.maximum(-jnp.expm1(2.0 * log_a), 0.0)) * (i * xf)

    def combine(left, right):
        a1, b1 = left
        a2, b2 = right
        return a1 * a2, a2 * b1 + b2

    _, h = lax.associative_scan(combine, (a, u), axis=1)
    return h.astype(x.dtype)

def hgrn2_chunkwise(q, k, log_f, v):
    B_, S_, H, DK = q.shape
    DV = v.shape[-1]
    n_chunks = S_ // HG_CHUNK

    def to_chunks(t):
        return t.reshape(B_, n_chunks, HG_CHUNK, H, t.shape[-1]).transpose(1, 0, 3, 2, 4)

    causal = jnp.tril(jnp.ones((HG_CHUNK, HG_CHUNK), dtype=bool))

    def step(state, chunk):
        qc, kc, lfc, vc = chunk
        cum = jnp.cumsum(lfc, axis=2)
        o_inter = jnp.einsum('bhtk,bhkv->bhtv', qc * jnp.exp(cum), state)
        rel = cum[:, :, :, None, :] - cum[:, :, None, :, :]
        decay = jnp.where(causal[:, :, None], jnp.exp(jnp.minimum(rel, 0.0)), 0.0)
        scores = jnp.einsum('bhtsk,bhsk->bhts', qc[:, :, :, None, :] * decay, kc)
        o_intra = jnp.einsum('bhts,bhsv->bhtv', scores, vc)
        last = cum[:, :, -1, :]
        k_to_end = kc * jnp.exp(jnp.minimum(last[:, :, None, :] - cum, 0.0))
        state = jnp.exp(last)[..., None] * state + jnp.einsum('bhsk,bhsv->bhkv', k_to_end, vc)
        return state, o_inter + o_intra

    state0 = jnp.zeros((B_, H, DK, DV), jnp.float32)
    _, o = lax.scan(step, state0, (to_chunks(q), to_chunks(k), to_chunks(log_f), to_chunks(v)))
    return o.transpose(1, 0, 3, 2, 4).reshape(B_, S_, H, DV)

def hybrid_mixer(h, lower_bound, w_in, conv_w, conv_b, w_r, b_r, w_i, b_i, lam, hg_norm, w_out):
    B_, S_, _ = h.shape
    proj = h @ w_in
    xa, ga, q, f, v, g, m_a, m_b = jnp.split(proj, SPLIT_POINTS, axis=-1)
    xa = causal_depthwise_conv(xa, conv_w, conv_b)
    y_a = rg_lru(xa, w_r, b_r, w_i, b_i, lam) * jax.nn.gelu(ga)
    qf = jax.nn.silu(q.astype(jnp.float32)).reshape(B_, S_, HG_HEADS, HG_DK)
    zf = f.astype(jnp.float32).reshape(B_, S_, HG_HEADS, HG_DK)
    lb = lower_bound.reshape(HG_HEADS, HG_DK)
    sig = jax.nn.sigmoid(zf)
    f_gate = lb + (1.0 - lb) * sig
    log_f = jnp.log(jnp.maximum(f_gate, F_MIN))
    kf = (1.0 - lb) * jax.nn.sigmoid(-zf)
    vf = v.astype(jnp.float32).reshape(B_, S_, HG_HEADS, HG_DV)
    o = rms_norm(hgrn2_chunkwise(qf, kf, log_f, vf), hg_norm)
    y_b = o.reshape(B_, S_, HG_HEADS * HG_DV).astype(h.dtype) * jax.nn.silu(g)
    y = jax.nn.sigmoid(m_a) * y_a + jax.nn.sigmoid(m_b) * y_b
    return y @ w_out

def second_inputs(seed: int = 0) -> dict:
    key = jax.random.key(seed)
    ks = jax.random.split(key, 20)
    f32 = jnp.float32
    nrm = lambda k, shape, scale: jax.random.normal(k, shape, f32) * scale
    a_c = jax.random.uniform(ks[10], (DEPTH, D_RG), f32, minval=0.9, maxval=0.999)
    a0 = a_c ** (1.0 / RG_C)
    lam = jnp.log(a0) - jnp.log1p(-a0)
    return {
        'x': jax.random.normal(ks[0], (BATCH, SEQ, D_MODEL), f32),
        'lb_logits': nrm(ks[1], (DEPTH, HG_HEADS * HG_DK), 0.1),
        'norm_mix': 1.0 + nrm(ks[2], (DEPTH, D_MODEL), 0.02),
        'w_in': nrm(ks[3], (DEPTH, D_MODEL, D_IN), D_MODEL ** -0.5),
        'conv_w': nrm(ks[4], (DEPTH, CONV_W, D_RG), CONV_W ** -0.5),
        'conv_b': nrm(ks[5], (DEPTH, D_RG), 0.02),
        'w_r': nrm(ks[6], (DEPTH, RG_BLOCKS, RG_BLOCK_W, RG_BLOCK_W), RG_BLOCK_W ** -0.5),
        'b_r': nrm(ks[7], (DEPTH, D_RG), 0.02),
        'w_i': nrm(ks[8], (DEPTH, RG_BLOCKS, RG_BLOCK_W, RG_BLOCK_W), RG_BLOCK_W ** -0.5),
        'b_i': nrm(ks[9], (DEPTH, D_RG), 0.02),
        'lam': lam,
        'hg_norm': 1.0 + nrm(ks[11], (DEPTH, HG_DV), 0.02),
        'w_out': nrm(ks[12], (DEPTH, D_MODEL, D_MODEL), D_MODEL ** -0.5),
        'norm_mlp': 1.0 + nrm(ks[13], (DEPTH, D_MODEL), 0.02),
        'w_up': nrm(ks[14], (DEPTH, D_MODEL, D_FF), D_MODEL ** -0.5),
        'w_down': nrm(ks[15], (DEPTH, D_FF, D_MODEL), D_FF ** -0.5),
        'norm_final': 1.0 + nrm(ks[16], (D_MODEL,), 0.02),
    }

def second_block(x, lb_logits, norm_mix, w_in, conv_w, conv_b, w_r, b_r, w_i, b_i, lam, hg_norm, w_out, norm_mlp, w_up, w_down, norm_final):
    sm = jax.nn.softmax(lb_logits.astype(jnp.float32), axis=0)
    lower_bounds = jnp.clip(jnp.cumsum(sm, axis=0) - sm[0], 0.0, 1.0)
    for l in range(DEPTH):
        h = rms_norm(x, norm_mix[l])
        x = x + hybrid_mixer(h, lower_bounds[l], w_in[l], conv_w[l], conv_b[l], w_r[l], b_r[l],
                             w_i[l], b_i[l], lam[l], hg_norm[l], w_out[l])
        h = rms_norm(x, norm_mlp[l])
        x = x + jnp.square(jax.nn.relu(h @ w_up[l])) @ w_down[l]
    return rms_norm(x, norm_final)


def setup_inputs(seed=0):
    out = dict(first_inputs(seed))
    for name, value in second_inputs(seed + 1).items():
        if name != "x":
            out[name + "_2"] = value
    return out


def reference(
    x, mix_norm_w, ffn_norm_w, final_norm_w, gla_w_in, gla_w_gate2, gla_b_gate, gla_norm_w,
    gla_w_out, pool_w, pool_b, pool_scale, ssd_w_in, ssd_conv_w, ssd_conv_b, ssd_dt_bias,
    ssd_a_log, ssd_d, ssd_norm_w, ssd_w_out, sb_w_qkv, sb_w_out, ffn_w_up, ffn_conv_w,
    ffn_conv_b, ffn_w_down, lb_logits_2, norm_mix_2, w_in_2, conv_w_2, conv_b_2, w_r_2, b_r_2,
    w_i_2, b_i_2, lam_2, hg_norm_2, w_out_2, norm_mlp_2, w_up_2, w_down_2, norm_final_2,
):
    x = first_block(
        x, mix_norm_w, ffn_norm_w, final_norm_w, gla_w_in, gla_w_gate2, gla_b_gate, gla_norm_w,
        gla_w_out, pool_w, pool_b, pool_scale, ssd_w_in, ssd_conv_w, ssd_conv_b, ssd_dt_bias,
        ssd_a_log, ssd_d, ssd_norm_w, ssd_w_out, sb_w_qkv, sb_w_out, ffn_w_up, ffn_conv_w,
        ffn_conv_b, ffn_w_down,
    )
    return second_block(
        x, lb_logits_2, norm_mix_2, w_in_2, conv_w_2, conv_b_2, w_r_2, b_r_2, w_i_2, b_i_2,
        lam_2, hg_norm_2, w_out_2, norm_mlp_2, w_up_2, w_down_2, norm_final_2,
    )


_drawn_inputs = setup_inputs


def setup_inputs(seed=0):
    import zlib

    import numpy as np

    out = dict(_drawn_inputs(seed))
    spreads = {}
    factors = {'ffn_norm_w': 3.472,
     'gla_norm_w': 4.319,
     'ffn_conv_b': 3.237,
     'norm_mix_2': 4.864,
     'b_r_2': 51.311,
     'b_i_2': 38.974,
     'hg_norm_2': 21.813,
     'norm_mlp_2': 14.046,
     'norm_final_2': 7.392,
     'conv_b_2': 5.218}
    for name, (base, spread) in spreads.items():
        noise = np.random.default_rng([zlib.crc32(name.encode()), seed]).standard_normal(out[name].shape)
        drawn = base * np.exp(spread * noise) if base else spread * noise
        out[name] = __import__('jax').numpy.asarray(drawn.astype(out[name].dtype))
    for name, factor in factors.items():
        out[name] = (out[name] * factor).astype(out[name].dtype)
    return out
```

```python
from contextlib import ExitStack

import concourse.bass as bass
from concourse import mybir

ALU = mybir.AluOpType
ACT = mybir.ActivationFunctionType
AX = mybir.AxisListType.X
F32 = mybir.dt.float32
F32R = mybir.dt.float32r
BF16 = mybir.dt.bfloat16
U8 = mybir.dt.uint8
ds = bass.ds

P = 128
SEQ = 1024
D = 1024
MT = SEQ // P
DOWN = 2 * MT
KT = D // P
HALF = 512
UNIT = 1024
EPS = 1e-6

GLA_HEADS, DK, DV, RANK, TAU, CHUNK = 4, 128, 256, 16, 16.0, 64
NCH = SEQ // CHUNK
GLA_IN = 2 * GLA_HEADS * DK + 2 * GLA_HEADS * DV + RANK
FFN_DIM = 2816
FT = FFN_DIM // P
HG_HEADS, HG_DV, LEVELS = 8, 128, 7
RG_C = 8.0
F_MIN = 1e-30
D_FF = 4096

C_FCW, C_FCB = 0, 3 * 2 * FT
C_BG = C_FCB + 2 * FT
C_GNW = C_BG + 4
C_CW = C_GNW + 8
C_CB = C_CW + 32
C_BR = C_CB + 8
C_BI = C_BR + 8
C_LAM = C_BI + 8
C_HGN = C_LAM + 8
C_LB = C_HGN + 1
C_END = C_LB + 8
ROWS = 4 * FT


def wait(eng, sem, value):
    if isinstance(value, int) and value <= 0:
        return
    eng.wait_ge(sem, value)


class Core:
    pass


class Stream:

    def __init__(self, sem, name, core, slots, first, per):
        self.slots, self.first, self.per, self.core = slots, first, per, core
        self.raw_in = [sem(f"{name}_raw_in{n}") for n in range(2)]
        self.hi_done = sem(f"{name}_hi_done")
        self.split = sem(f"{name}_split")
        self.used = sem(f"{name}_used")

    def number(self, it, pos):
        if isinstance(it, int) and it == 0:
            return pos, pos
        return self.first + pos, (it - 1) * self.per + self.first + pos

    def done(self, it, pos):
        return self.number(it, pos)[1] + 2

    def ready(self, it, pos):
        return self.number(it, pos)[1] + 1

    def slot(self, it, pos):
        n = self.number(it, pos)[0] % self.slots
        return self.core.whi[:, n, :], self.core.wlo[:, n, :]

    def load(self, sp, it, pos, source, dims):
        s, g = self.number(it, pos)
        wait(sp, self.split, g - 1)
        dst = self.core.raw[:, s % 2, :]
        if dims:
            dst = dst.rearrange("p (k n) -> p k n", k=dims)
        sp.dma_start(dst, source).then_inc(self.raw_in[s % 2], 16)

    def divide(self, pool, it, pos):
        s, g = self.number(it, pos)
        hi, lo = self.slot(it, pos)
        raw = self.core.raw[:, s % 2, :]
        if isinstance(g, int):
            arrived = 16 * (g // 2 + 1)
        else:
            arrived = (it - 1) * (8 * self.per) + 16 * (s // 2 + 1)
        pool.wait_ge(self.raw_in[s % 2], arrived)
        wait(pool, self.used, g - self.slots + 2)
        pool.tensor_tensor(hi, raw, self.core.zero[:, 0:1].broadcast_to([P, UNIT]), ALU.add)\
            .then_inc(self.hi_done, 1)
        pool.wait_ge(self.hi_done, g + 1)
        pool.tensor_tensor(lo, raw, hi.bitcast(F32), ALU.subtract).then_inc(self.split, 1)


def product(pe, out, a, b, first, last):
    (ah, al), (bh, bl) = a, b
    pe.matmul(out, ah, bh, start=first, stop=False)
    pe.matmul(out, ah, bl, start=False, stop=False)
    return pe.matmul(out, al, bh, start=False, stop=last)


def columns_tile(pe, core, st, it, pos, pair):
    _, g = st.number(it, pos)
    wait(pe, st.split, g + 1)
    hi, lo = (x.rearrange("p (k n) -> p k n", k=KT) for x in st.slot(it, pos))
    for half in range(2):
        cols = slice(half * HALF, (half + 1) * HALF)
        for k in range(KT):
            mm = product(pe, pair[:, cols], (hi[:, k, :], lo[:, k, :]),
                         (core.hhi[:, k, cols], core.hlo[:, k, cols]), k == 0, k == KT - 1)
    return mm


def down_tile(pe, core, m, half, parts, weights, bank):
    n = len(parts)
    rows, cols = slice(m * P, (m + 1) * P), slice(half * HALF, (half + 1) * HALF)
    for k, ((ah, al), (wh, wl)) in enumerate(zip(parts, weights)):
        mm = product(pe, bank, (ah[:, rows], al[:, rows]), (wh[:, cols], wl[:, cols]),
                     k == 0, k == n - 1)
    return mm


class Norm:
    def __init__(self, sem, name, core, xn, junk, row, ready=None):
        self.core, self.xn, self.junk, self.row, self.ready = core, xn, junk, row, ready
        self.row_in, self.squared, self.var, self.root, self.scaled, self.turned, self.hi, self.lo = (
            sem(f"{name}_{s}") for s in ("row_in", "squared", "var", "root", "scaled", "turned", "hi", "lo"))

    def pair(self, m):
        return self.core.DD if m % 2 == 0 else self.core.MM

    def scalar(self, act):
        c = self.core

        def square(m):
            if self.ready:
                act.wait_ge(*self.ready(m))
            act.activation(self.junk, c.X[:, m, :], ACT.Square, accum_out=c.ss[:, m:m + 1])\
                .then_inc(self.squared, 1)

        def root(m):
            act.wait_ge(self.var, m + 1)
            act.activation(c.sd[:, m:m + 1], c.ms[:, m:m + 1], ACT.Sqrt).then_inc(self.root, 1)

        def high(m):
            act.wait_ge(self.turned, m + 1)
            act.copy(c.hhi[:, :, m * P:(m + 1) * P],
                     self.pair(m).rearrange("p (k n) -> p k n", k=KT)).then_inc(self.hi, 1)

        for n in range(MT + 3):
            if n < MT:
                if n:
                    act.wait_ge(self.squared, n)
                square(n)
            if 1 <= n <= MT:
                root(n - 1)
            if n >= 3:
                high(n - 3)

    def vector(self, dve):
        c = self.core
        dve.wait_ge(self.row_in, 16)
        for n in range(MT + 3):
            if n < MT:
                dve.wait_ge(self.squared, n + 1)
                dve.tensor_scalar(c.ms[:, n:n + 1], c.ss[:, n:n + 1], 1.0 / D, EPS, ALU.mult,
                                  ALU.add).then_inc(self.var, 1)
            if 1 <= n <= MT:
                m = n - 1
                dve.wait_ge(self.root, m + 1)
                dve.reciprocal(c.rs[:, m:m + 1], c.sd[:, m:m + 1])
                dve.drain()
                wait(dve, self.turned, m - 1)
                dve.scalar_tensor_tensor(out=self.xn[:, m % 2, :], in0=c.X[:, m, :],
                                         scalar=c.rs[:, m:m + 1], in1=self.row, op0=ALU.mult,
                                         op1=ALU.mult).then_inc(self.scaled, 1)
            if n >= 3:
                m = n - 3
                dve.wait_ge(self.hi, m + 1)
                rows = slice(m * P, (m + 1) * P)
                dve.tensor_tensor(c.hlo[:, :, rows], self.pair(m).rearrange("p (k n) -> p k n", k=KT),
                                  c.hhi[:, :, rows].bitcast(F32), ALU.subtract).then_inc(self.lo, 1)

    def tensor(self, pe):
        for m in range(MT):
            pe.wait_ge(self.scaled, m + 1)
            wait(pe, self.lo, m - 1)
            for k in range(KT):
                mm = pe.transpose(self.pair(m)[:, k * P:(k + 1) * P],
                                  self.xn[:, m % 2, k * P:(k + 1) * P], self.core.ident[:, :])
            mm.then_inc(self.turned, 1)
        pe.wait_ge(self.lo, MT)


def down_product(pe, c, st, it, positions, parts, down_mm, down_add, before):
    pe.wait_ge(st.split, st.ready(it, positions[-1]))
    weights = [st.slot(it, pos) for pos in positions]
    for m in range(MT):
        for half in range(2):
            n = 2 * m + half
            pe.wait_ge(down_add, before * DOWN + max(n, 1))
            mm = down_tile(pe, c, m, half, parts, weights, c.DD[:, half * HALF:(half + 1) * HALF])
            if n < DOWN - 1:
                mm.then_inc(down_mm, 1)
    mm.then_inc(st.used, len(positions))


class RowNorm:

    def __init__(self, sem, name, core, junk, row):
        self.core, self.junk, self.row = core, junk, row
        self.row_in, self.squared, self.var, self.root, self.scaled = (
            sem(f"{name}_{s}") for s in ("row_in", "squared", "var", "root", "scaled"))

    def scalar(self, act):
        c = self.core
        for n in range(MT + 1):
            if n < MT:
                wait(act, self.squared, n)
                act.activation(self.junk, c.X[:, n, :], ACT.Square, accum_out=c.ss[:, n:n + 1])\
                    .then_inc(self.squared, 1)
            if n:
                act.wait_ge(self.var, n)
                act.activation(c.sd[:, n - 1:n], c.ms[:, n - 1:n], ACT.Sqrt).then_inc(self.root, 1)

    def vector(self, dve):
        c = self.core
        dve.wait_ge(self.row_in, 16)
        for n in range(MT + 1):
            if n < MT:
                dve.wait_ge(self.squared, n + 1)
                dve.tensor_scalar(c.ms[:, n:n + 1], c.ss[:, n:n + 1], 1.0 / D, EPS, ALU.mult,
                                  ALU.add).then_inc(self.var, 1)
            if n:
                m = n - 1
                dve.wait_ge(self.root, m + 1)
                dve.reciprocal(c.rs[:, m:m + 1], c.sd[:, m:m + 1])
                dve.drain()
                dve.scalar_tensor_tensor(out=c.X[:, m, :], in0=c.X[:, m, :], scalar=c.rs[:, m:m + 1],
                                         in1=self.row, op0=ALU.mult, op1=ALU.mult).then_inc(self.scaled, 1)


def add_down(dve, c, st, down_mm, down_add, it, pos, before):
    for m in range(MT):
        for half in range(2):
            n = 2 * m + half
            if n < DOWN - 1:
                dve.wait_ge(down_mm, before * (DOWN - 1) + n + 1)
            else:
                dve.wait_ge(st.used, st.done(it, pos))
            cols = slice(half * HALF, (half + 1) * HALF)
            dve.tensor_tensor(c.X[:, m, cols], c.X[:, m, cols], c.DD[:, cols], ALU.add)\
               .then_inc(down_add, 1)


class Program:
    def __init__(self, nc, ctx, a):
        self.nc, self.ctx, self.a = nc, ctx, a
        self.stage_sems = []
        c = self.core = Core()
        c.X = self.sb("X", [P, MT, D])
        c.hhi = self.sb("h_hi", [P, KT, SEQ], F32R)
        c.hlo = self.sb("h_lo", [P, KT, SEQ], F32R)
        c.raw = self.sb("w_raw", [P, 2, UNIT])
        c.zero = self.sb("zero", [P, 1])
        c.ident = self.sb("ident", [P, P])
        c.masks = self.sb("masks", [P, LEVELS, P // 2], U8)
        c.par = self.sb("params", [P, C_END])
        c.decay = self.sb("lru_decay", [P, 2, 8])
        c.lb = self.sb("lower_bound", [P, 2, 8])
        c.ss, c.ms, c.sd, c.rs = (self.sb(n, [P, MT]) for n in ("ss", "ms", "sd", "rs"))
        c.PA = self.ps("PA", [P, SEQ])
        c.PB = self.ps("PB", [P, SEQ])
        c.DD = self.ps("DD", [P, SEQ])
        c.MM = self.ps("MM", [P, SEQ])
        self.x_in = [ctx.enter_context(nc.semaphore(f"x_in{m}")) for m in range(MT)]

    def sb(self, name, shape, dt=F32):
        return self.ctx.enter_context(self.nc.sbuf_tensor(name, shape, dt))[:]

    def ps(self, name, shape):
        return self.ctx.enter_context(self.nc.psum_tensor(name, shape, F32))[:]

    def sem(self, name):
        handle = self.nc.alloc_semaphore(name)
        self.stage_sems.append(handle)
        return handle

    def end_stage(self):
        self.nc.clear_and_free_semaphores(self.stage_sems)
        self.nc.all_engine_barrier()
        self.stage_sems = []

    def split_slots(self, ctx, name, slots):
        c = self.core
        c.whi = ctx.enter_context(self.nc.sbuf_tensor(f"{name}_w_hi", [P, slots, UNIT], F32R))[:]
        c.wlo = ctx.enter_context(self.nc.sbuf_tensor(f"{name}_w_lo", [P, slots, UNIT], F32R))[:]

    def parameters(self):
        nc, c, a = self.nc, self.core, self.a
        with ExitStack() as ctx:
            rows = ctx.enter_context(nc.sbuf_tensor("param_rows", [P, 3, P], F32))[:]
            t = ctx.enter_context(nc.sbuf_tensor("param_temps", [P, 6, 8], F32))[:]
            maskf = ctx.enter_context(nc.sbuf_tensor("masks_in", [P, LEVELS, P // 2], F32))[:]
            s_rows, s_id, s_par, s_turn, s_zero = (self.sem(n) for n in (
                "rows_in", "ident_in", "params_ready", "params_turned", "rows_zeroed"))
            s_abs, s_exp, s_lb = self.sem("lam_abs"), self.sem("lam_exp"), self.sem("lb_exp")
            s_e = self.sem("lb_shifted")
            last = C_END - 2 * ROWS
            block = ctx.enter_context(nc.Block())

            @block.sync
            def _(sp):
                sp.dma_start(c.ident, a["ident"]).then_inc(s_id, 16)
                sp.dma_start(maskf, a["masks"]).then_inc(s_id, 16)
                taps = a["ffn_conv_w"][0].rearrange("t (f p) -> (t f) p", p=P)
                sp.dma_start(rows[0:ROWS, 0, :], taps[0:ROWS, :]).then_inc(s_rows, 16)
                sp.dma_start(rows[0:2 * FT, 1, :], taps[ROWS:3 * 2 * FT, :]).then_inc(s_rows, 16)
                sp.dma_start(rows[2 * FT:ROWS, 1, :],
                             a["ffn_conv_b"][0].rearrange("(f p) -> f p", p=P)).then_inc(s_rows, 16)
                n = 0
                for src in (
                    a["gla_b_gate"][0].rearrange("(f p) -> f p", p=P),
                    a["gla_norm_w"][0].rearrange("(f p) -> f p", p=P),
                    a["conv_w_2"][0].rearrange("t (f p) -> (t f) p", p=P),
                    a["conv_b_2"][0].rearrange("(f p) -> f p", p=P),
                    a["b_r_2"][0].rearrange("(f p) -> f p", p=P),
                    a["b_i_2"][0].rearrange("(f p) -> f p", p=P),
                    a["lam_2"][0].rearrange("(f p) -> f p", p=P),
                    a["hg_norm_2"],
                    a["lb_logits_2"][0].rearrange("(f p) -> f p", p=P),
                ):
                    k = src.shape[0]
                    sp.dma_start(rows[n:n + k, 2, :], src).then_inc(s_rows, 16)
                    n += k
                for m in range(MT):
                    sp.dma_start(c.X[:, m, :], a["x"][0, m * P:(m + 1) * P, :]).then_inc(self.x_in[m], 16)

            @block.tensor
            def _(pe):
                pe.wait_ge(s_id, 32)
                pe.wait_ge(s_rows, 16 * 12)
                for g in range(3):
                    k = ROWS if g < 2 else last
                    mm = pe.transpose(c.MM[:, g * ROWS:g * ROWS + k], rows[0:k, g, :], c.ident[0:k, 0:k])
                mm.then_inc(s_turn, 1)

            @block.scalar
            def _(act):
                act.wait_ge(s_abs, 1)
                act.activation(t[:, 1, :], t[:, 0, :], ACT.Exp, scale=-1.0).then_inc(s_exp, 1)
                act.wait_ge(s_e, 1)
                act.activation(t[:, 5, :], t[:, 4, :], ACT.Exp).then_inc(s_lb, 1)

            @block.vector
            def _(dve):
                def then(ins):
                    dve.drain()
                    return ins

                dve.memset(c.zero, 0.0)
                dve.wait_ge(s_id, 32)
                dve.tensor_copy(c.masks, maskf)
                dve.wait_ge(s_turn, 1)
                then(dve.tensor_copy(c.par, c.MM[:, 0:C_END]))
                lam, lbl = c.par[:, C_LAM:C_LAM + 8], c.par[:, C_LB:C_LB + 8]
                dve.tensor_scalar(t[:, 2, :], lam, -1.0, 0.0, ALU.mult, ALU.max)
                then(dve.tensor_scalar(t[:, 3, :], lam, 0.0, None, ALU.max))
                dve.tensor_tensor(t[:, 0, :], t[:, 2, :], t[:, 3, :], ALU.add).then_inc(s_abs, 1)
                dve.tensor_tensor(t[:, 4, :], lbl, lbl, ALU.subtract).then_inc(s_e, 1)
                dve.wait_ge(s_exp, 1)
                then(dve.tensor_scalar(t[:, 3, :], t[:, 1, :], 2.0, None, ALU.add))
                then(dve.reciprocal(t[:, 3, :], t[:, 3, :]))
                then(dve.tensor_tensor(t[:, 1, :], t[:, 1, :], t[:, 3, :], ALU.mult))
                then(dve.tensor_tensor(t[:, 3, :], t[:, 1, :], t[:, 1, :], ALU.mult))
                then(dve.tensor_scalar(t[:, 0, :], t[:, 3, :], 1.0 / 17, 1.0 / 15, ALU.mult, ALU.add))
                for d in (13, 11, 9, 7, 5, 3, 1):
                    then(dve.tensor_tensor(t[:, 0, :], t[:, 0, :], t[:, 3, :], ALU.mult))
                    then(dve.tensor_scalar(t[:, 0, :], t[:, 0, :], 1.0 / d, None, ALU.add))
                then(dve.tensor_tensor(t[:, 0, :], t[:, 0, :], t[:, 1, :], ALU.mult))
                then(dve.scalar_tensor_tensor(out=t[:, 0, :], in0=t[:, 0, :], scalar=2.0,
                                              in1=t[:, 2, :], op0=ALU.mult, op1=ALU.add))
                dve.tensor_scalar(c.decay[:, 0, :], t[:, 0, :], -RG_C, None, ALU.mult)
                dve.tensor_scalar(c.decay[:, 1, :], t[:, 0, :], RG_C, None, ALU.mult)
                dve.wait_ge(s_lb, 1)
                then(dve.reciprocal(t[:, 4, :], t[:, 5, :]))
                then(dve.tensor_tensor(t[:, 4, :], t[:, 4, :], t[:, 5, :], ALU.mult))
                then(dve.tensor_tensor(t[:, 5, :], t[:, 4, :], t[:, 4, :], ALU.subtract))
                then(dve.tensor_scalar(c.lb[:, 0, :], t[:, 5, :], 0.0, 1.0, ALU.max, ALU.min))
                dve.tensor_scalar(c.lb[:, 1, :], c.lb[:, 0, :], -1.0, 1.0, ALU.mult, ALU.add)\
                    .then_inc(s_par, 1)
                dve.wait_ge(s_par, 1)

    def gla(self):
        nc, c, a = self.nc, self.core, self.a
        W = a["gla_w_in"][0].rearrange("(k p) n -> p k n", p=P)
        WO = a["gla_w_out"][0].rearrange("(k p) n -> p k n", p=P)
        H = GLA_HEADS
        QC, KC, VC, RC = 0, H * DK, 2 * H * DK, 2 * H * DK + H * DV
        with ExitStack() as ctx:
            def sb(name, shape, dt=F32):
                return ctx.enter_context(nc.sbuf_tensor(name, shape, dt))[:]

            self.split_slots(ctx, "gla", 4)
            T1, T2, T3, Q = (sb(f"gla_{n}", [P, SEQ]) for n in ("t1", "t2", "t3", "q"))
            GLR = sb("gla_glr", [P, SEQ])
            V, R, Y = (sb(f"gla_{n}", [P, MT, DV]) for n in ("v", "r", "y"))
            KDT = sb("gla_kdT", [P, MT, DK])
            yhi, ylo = (sb(f"gla_y_{n}", [P, 2, SEQ], F32R) for n in ("hi", "lo"))
            keep = sb("gla_keep", [P, SEQ], BF16)
            G2 = sb("gla_gate2", [P, DK])
            S = sb("gla_state", [P, 2, DV])
            DEC = sb("gla_dec", [P, NCH])
            so, vo, qo, ro = (sb(f"gla_o_{n}", [P, MT]) for n in ("ss", "ms", "sd", "rs"))
            graw = Y.rearrange("p m v -> p (m v)")[:, 0:UNIT].rearrange("p (k n) -> p k n", k=KT)
            ghi, glo = (y[:, 0, :].rearrange("p (k n) -> p k n", k=KT) for y in (yhi, ylo))

            st = Stream(self.sem, "gla", c, 4, 8, 8)
            norm = Norm(self.sem, "gla_norm", c, V.rearrange("p (b m) v -> p b (m v)", b=2),
                        R[:, 0:4, :].rearrange("p m v -> p (m v)"), Q,
                        lambda m: (self.x_in[m], 16))
            s = {n: self.sem(f"gla_{n}") for n in (
                "graw_in", "g_hi", "g_lo", "glr_mm", "glr", "g2_zero", "g2_in",
                "gate_mm", "absd", "logd", "rel", "decay", "kd", "v_mm", "r_mm", "v", "q", "r", "kdt_mm", "kdt", "st_mm", "s", "o_mm",
                "o_sq", "o_ms", "o_sd", "y", "yt_mm", "y_hi", "y_lo", "down_mm", "down_add")}
            block = ctx.enter_context(nc.Block())
            ends = T3.rearrange("p (c t) -> p c t", t=CHUNK)[:, :, CHUNK - 1]

            def phases(eng, body):
                body(0)
                with eng.Fori(1, H) as h:
                    body(h)

            @block.sync
            def _(sp):
                sp.dma_start(norm.row, a["mix_norm_w"][0].partition_broadcast(P)).then_inc(norm.row_in, 16)
                sp.dma_start(graw, W[:, :, GLA_IN - P:GLA_IN]).then_inc(s["graw_in"], 16)

                def body(h):
                    if isinstance(h, int):
                        sp.wait_ge(s["g2_zero"], 1)
                    wait(sp, s["gate_mm"], h)
                    sp.dma_start(G2[P - RANK:P, :], a["gla_w_gate2"][0][:, ds(h * DK, DK)])\
                        .then_inc(s["g2_in"], 16)
                    st.load(sp, h, 0, W[:, :, ds(h * DK + KC, DK)], KT)
                    for k in range(2):
                        st.load(sp, h, 1 + k, W[:, 4 * k:4 * k + 4, ds(h * DV + VC, DV)], 4)
                    st.load(sp, h, 3, W[:, :, ds(h * DK + QC, DK)], KT)
                    for k in range(2):
                        st.load(sp, h, 4 + k, W[:, 4 * k:4 * k + 4, ds(h * DV + RC, DV)], 4)
                    for k in range(2):
                        st.load(sp, h, 6 + k, WO[:, ds(h * 2 + k, 1), :].rearrange("p k n -> p (k n)"), 0)
                phases(sp, body)

            @block.gpsimd
            def _(pool):
                pool.wait_ge(s["graw_in"], 16)
                pool.tensor_tensor(ghi, graw, c.zero[:, 0:1].unsqueeze(2).broadcast_to([P, KT, P]),
                                   ALU.add).then_inc(s["g_hi"], 1)
                pool.wait_ge(s["g_hi"], 1)
                pool.tensor_tensor(glo, graw, ghi.bitcast(F32), ALU.subtract).then_inc(s["g_lo"], 1)

                def body(h):
                    for pos in range(8):
                        st.divide(pool, h, pos)
                phases(pool, body)

            def rows_tiles(pe, h, pos, pairs, frees, half_mm):
                _, g = st.number(h, pos + 1)
                wait(pe, st.split, g + 1)
                parts = [[x.rearrange("p (k n) -> p k n", k=4) for x in st.slot(h, pos + u)] for u in range(2)]
                for n, (pair, (free, count)) in enumerate(zip(pairs, frees)):
                    wait(pe, free, count)
                    for q in range(4):
                        m = 4 * n + q
                        for k in range(KT):
                            wh, wl = parts[k // 4]
                            rows = slice(m * P, (m + 1) * P)
                            mm = product(pe, pair[:, q * DV:(q + 1) * DV],
                                         (c.hhi[:, k, rows], c.hlo[:, k, rows]),
                                         (wh[:, k % 4, :], wl[:, k % 4, :]), k == 0, k == KT - 1)
                    if n == 0:
                        mm.then_inc(half_mm, 1)
                mm.then_inc(st.used, 2)

            @block.tensor
            def _(pe):
                pe.sem_inc(st.used, 1)
                norm.tensor(pe)
                pe.wait_ge(s["g_lo"], 1)
                for half in range(2):
                    cols = slice(half * HALF, (half + 1) * HALF)
                    for k in range(KT):
                        mm = product(pe, c.MM[:, cols], (ghi[:, k, :], glo[:, k, :]),
                                     (c.hhi[:, k, cols], c.hlo[:, k, cols]), k == 0, k == KT - 1)
                mm.then_inc(s["glr_mm"], 1)
                pe.wait_ge(s["glr"], 1)

                def body(h):
                    pe.wait_ge(s["g2_in"], 16 * h + 16)
                    wait(pe, s["y_lo"], 2 * h)
                    for half in range(2):
                        cols = slice(half * HALF, (half + 1) * HALF)
                        mm = pe.matmul(c.MM[:, cols], G2, GLR[:, cols], start=True, stop=True)
                    mm.then_inc(s["gate_mm"], 1)
                    wait(pe, s["r"], 2 * h - 1)
                    columns_tile(pe, c, st, h, 0, c.PA).then_inc(st.used, 1)
                    rows_tiles(pe, h, 1, (c.PB, c.PA), ((s["r"], 2 * h), (s["kd"], h + 1)), s["v_mm"])
                    pe.wait_ge(s["v"], 2 * h + 1)
                    columns_tile(pe, c, st, h, 3, c.PB).then_inc(st.used, 1)
                    pe.wait_ge(s["kd"], h + 1)
                    for m in range(MT):
                        mm = pe.transpose(c.MM[:, m * P:(m + 1) * P], T1[:, m * P:(m + 1) * P], c.ident)
                    mm.then_inc(s["kdt_mm"], 1)
                    rows_tiles(pe, h, 4, (c.PA, c.PB), ((s["v"], 2 * h + 2), (s["q"], h + 1)), s["r_mm"])
                    pe.wait_ge(s["kdt"], h + 1)
                    pe.wait_ge(s["v"], 2 * h + 2)
                    pe.wait_ge(s["q"], h + 1)

                    def update(n):
                        if n < 2:
                            pe.wait_ge(s["down_add"], h * DOWN + 1)
                        else:
                            pe.wait_ge(s["s"], h * NCH + n - 1)
                        rows = slice(CHUNK * (n % 2), CHUNK * (n % 2) + CHUNK)
                        pe.matmul(c.DD[:, (n % 2) * HALF:(n % 2) * HALF + DV], KDT[rows, n // 2, :],
                                  V[rows, n // 2, :], start=True, stop=True).then_inc(s["st_mm"], 1)

                    def read(n):
                        pe.wait_ge(s["s"], h * NCH + n + 1)
                        m = n // 2
                        if m >= 2:
                            pe.wait_ge(s["y"], h * MT + m - 1)
                        rows = slice(CHUNK * (n % 2), CHUNK * (n % 2) + CHUNK)
                        pe.matmul(c.MM[rows, (m % 2) * HALF:(m % 2) * HALF + DV],
                                  Q[:, n * CHUNK:(n + 1) * CHUNK], S[:, n % 2, :],
                                  start=True, stop=True).then_inc(s["o_mm"], 1)

                    update(0)
                    for n in range(NCH):
                        if n + 1 < NCH:
                            update(n + 1)
                        read(n)
                    pe.wait_ge(s["y"], h * MT + MT)
                    for k in range(2):
                        if k:
                            pe.wait_ge(s["y_lo"], 2 * h + 1)
                        for m in range(MT):
                            mm = pe.transpose(c.MM[:, m * P:(m + 1) * P], Y[:, m, k * P:(k + 1) * P], c.ident)
                        mm.then_inc(s["yt_mm"], 1)
                    pe.wait_ge(s["y_lo"], 2 * h + 2)
                    down_product(pe, c, st, h, (6, 7), [(yhi[:, k, :], ylo[:, k, :]) for k in range(2)],
                                 s["down_mm"], s["down_add"], h)
                phases(pe, body)

            @block.scalar
            def _(act):
                norm.scalar(act)
                act.wait_ge(s["glr_mm"], 1)
                act.copy(GLR, c.MM).then_inc(s["glr"], 1)

                def body(h):
                    bg = c.par[:, ds(h + C_BG, 1)]
                    act.wait_ge(s["gate_mm"], h + 1)
                    act.activation(T1, c.MM, ACT.Abs, bias=bg).then_inc(s["absd"], 1)
                    act.drain()
                    act.activation(T1, T1, ACT.Exp, scale=-1.0)
                    act.drain()
                    act.activation(T1, T1, ACT.Ln, bias=1.0).then_inc(s["logd"], 1)
                    act.wait_ge(s["rel"], h + 1)
                    act.activation(T2, T2, ACT.Exp, scale=1.0 / TAU)
                    act.activation(DEC, ends, ACT.Exp, scale=1.0 / TAU).then_inc(s["decay"], 1)
                    for n in range(2):
                        act.wait_ge(*((s["v_mm"], h + 1) if n == 0 else (st.used, st.done(h, 2))))
                        act.copy(V[:, 4 * n:4 * n + 4, :], (c.PB, c.PA)[n].rearrange("p (m v) -> p m v", v=DV))\
                           .then_inc(s["v"], 1)
                    act.wait_ge(st.used, st.done(h, 3))
                    act.activation(Q, c.PB, ACT.Copy, scale=DK ** -0.5).then_inc(s["q"], 1)
                    for n in range(2):
                        act.wait_ge(*((s["r_mm"], h + 1) if n == 0 else (st.used, st.done(h, 5))))
                        act.activation(R[:, 4 * n:4 * n + 4, :], (c.PA, c.PB)[n].rearrange("p (m v) -> p m v", v=DV),
                                       ACT.Silu).then_inc(s["r"], 1)
                    for m in range(MT):
                        act.wait_ge(s["o_mm"], h * NCH + 2 * m + 2)
                        o = c.MM[:, (m % 2) * HALF:(m % 2) * HALF + DV]
                        act.activation(T3[:, 0:DV], o, ACT.Square, accum_out=so[:, m:m + 1]).then_inc(s["o_sq"], 1)
                        act.wait_ge(s["o_ms"], h * MT + m + 1)
                        act.activation(qo[:, m:m + 1], vo[:, m:m + 1], ACT.Sqrt).then_inc(s["o_sd"], 1)
                    for k in range(2):
                        act.wait_ge(s["yt_mm"], 2 * h + k + 1)
                        act.activation(yhi[:, k, :], c.MM, ACT.Identity, scale=c.par[:, ds(2 * h + (C_GNW + k), 1)])\
                            .then_inc(s["y_hi"], 1)
                phases(act, body)

            @block.vector
            def _(dve):
                dve.memset(G2, 0.0).then_inc(s["g2_zero"], 1)
                dve.memset(keep, 1.0)
                dve.drain()
                dve.memset(keep.rearrange("p (c t) -> p c t", t=CHUNK)[:, :, 0:1], 0.0)
                norm.vector(dve)
                dve.sem_inc(s["down_add"], 1)

                def body(h):
                    bg = c.par[:, ds(h + C_BG, 1)]
                    dve.wait_ge(s["absd"], h + 1)
                    dve.tensor_scalar(T2, c.MM, bg, 0.0, ALU.add, ALU.min)
                    dve.drain()
                    dve.wait_ge(s["logd"], h + 1)
                    dve.tensor_tensor(T2, T2, T1, ALU.subtract)
                    dve.drain()
                    dve.tensor_tensor_scan(T3, keep, T2, 0.0, ALU.mult, ALU.add)
                    dve.drain()
                    chunks = [x.rearrange("p (c t) -> p c t", t=CHUNK) for x in (T2, T3)]
                    dve.tensor_tensor(chunks[0], ends.unsqueeze(2).broadcast_to([P, NCH, CHUNK]), chunks[1],
                                      ALU.subtract).then_inc(s["rel"], 1)
                    dve.wait_ge(s["decay"], h + 1)
                    dve.wait_ge(st.used, st.done(h, 0))
                    dve.tensor_tensor(T1, c.PA, T2, ALU.mult).then_inc(s["kd"], 1)
                    dve.wait_ge(s["kdt_mm"], h + 1)
                    dve.tensor_copy(KDT.rearrange("p m k -> p (m k)"), c.MM).then_inc(s["kdt"], 1)
                    for n in range(NCH + 3):
                        if n < NCH:
                            dve.wait_ge(s["st_mm"], h * NCH + n + 1)
                            wait(dve, s["o_mm"], h * NCH + n - 1)
                            ps = c.DD[:, (n % 2) * HALF:(n % 2) * HALF + DV]
                            if n == 0:
                                dve.tensor_copy(S[:, 0, :], ps).then_inc(s["s"], 1)
                            else:
                                dve.wait_ge(s["s"], h * NCH + n)
                                dve.scalar_tensor_tensor(out=S[:, n % 2, :], in0=S[:, (n - 1) % 2, :],
                                                         scalar=DEC[:, n:n + 1], in1=ps, op0=ALU.mult,
                                                         op1=ALU.add).then_inc(s["s"], 1)
                        if n % 2 == 1 and n >= 3:
                            m = (n - 3) // 2
                            dve.wait_ge(s["o_sq"], h * MT + m + 1)
                            dve.tensor_scalar(vo[:, m:m + 1], so[:, m:m + 1], 1.0 / DV, EPS, ALU.mult,
                                              ALU.add).then_inc(s["o_ms"], 1)
                        if n % 2 == 0 and n >= 4:
                            m = (n - 4) // 2
                            dve.wait_ge(s["r"], 2 * h + 1 + m // 4)
                            dve.wait_ge(s["o_sd"], h * MT + m + 1)
                            dve.reciprocal(ro[:, m:m + 1], qo[:, m:m + 1])
                            dve.drain()
                            o = c.MM[:, (m % 2) * HALF:(m % 2) * HALF + DV]
                            dve.scalar_tensor_tensor(out=Y[:, m, :], in0=o, scalar=ro[:, m:m + 1],
                                                     in1=R[:, m, :], op0=ALU.mult, op1=ALU.mult)\
                               .then_inc(s["y"], 1)
                    for k in range(2):
                        dve.wait_ge(s["y_hi"], 2 * h + k + 1)
                        dve.scalar_tensor_tensor(out=ylo[:, k, :], in0=c.MM,
                                                 scalar=c.par[:, ds(2 * h + (C_GNW + k), 1)],
                                                 in1=yhi[:, k, :].bitcast(F32), op0=ALU.mult,
                                                 op1=ALU.subtract).then_inc(s["y_lo"], 1)
                    add_down(dve, c, st, s["down_mm"], s["down_add"], h, 7, h)
                phases(dve, body)

    def ffn(self, name, W_up, W_down, row, chunks, gated):
        nc, c = self.nc, self.core
        WU = W_up.rearrange("(k p) n -> p k n", p=P)
        WD = W_down.rearrange("(k p) n -> p k n", p=P)
        n_up = 4 if gated else 2
        slots = 3 if gated else 4
        with ExitStack() as ctx:
            def sb(n, shape, dt=F32):
                return ctx.enter_context(nc.sbuf_tensor(f"{name}_{n}", shape, dt))[:]

            self.split_slots(ctx, name, slots)
            xn = sb("xn", [P, 2, D])
            rowt = sb("row", [P, D])
            UG, UV = sb("u_gate", [P, SEQ]), sb("u_val", [P, SEQ])
            A = sb("a", [P, 2, SEQ])
            ahi, alo = sb("a_hi", [P, 2, SEQ], F32R), sb("a_lo", [P, 2, SEQ], F32R)
            st = Stream(self.sem, name, c, slots, n_up, n_up + 2)
            norm = Norm(self.sem, f"{name}_norm", c, xn, UG, rowt)
            s = {n: self.sem(f"{name}_{n}") for n in (
                "base", "conv", "silu", "prod", "a_hi", "a_lo",
                "down_mm", "down_add")}
            read = s["conv"] if gated else s["base"]
            pair = (c.PA, c.PB)
            block = ctx.enter_context(nc.Block())

            def phases(eng, up, down):
                up(0)
                with eng.Fori(1, chunks) as i:
                    up(i)
                    down(i)
                down(chunks)

            @block.sync
            def _(sp):
                sp.dma_start(rowt, row.partition_broadcast(P)).then_inc(norm.row_in, 16)

                def up(i):
                    for t in range(n_up):
                        off = (t // 2) * P + (t % 2) * FFN_DIM if gated else t * P
                        st.load(sp, i, t, WU[:, :, ds(i * (2 * P) + off, P)], KT)

                def down(i):
                    base = n_up if not (isinstance(i, int) and i == chunks) else 0
                    for k in range(2):
                        st.load(sp, i, base + k, WD[:, ds((i - 1) * 2 + k, 1), :].rearrange("p k n -> p (k n)"), 0)
                phases(sp, up, down)

            @block.gpsimd
            def _(pool):
                def up(i):
                    for t in range(n_up):
                        st.divide(pool, i, t)

                def down(i):
                    base = n_up if not (isinstance(i, int) and i == chunks) else 0
                    for k in range(2):
                        st.divide(pool, i, base + k)
                phases(pool, up, down)

            @block.tensor
            def _(pe):
                pe.sem_inc(st.used, 1)
                norm.tensor(pe)

                def up(i):
                    for t in range(n_up):
                        wait(pe, read, i * n_up + t - 1)
                        columns_tile(pe, c, st, i, t, pair[t % 2]).then_inc(st.used, 1)

                def down(i):
                    base = n_up if not (isinstance(i, int) and i == chunks) else 0
                    pe.wait_ge(s["a_lo"], i * 2)
                    down_product(pe, c, st, i, (base, base + 1),
                                 [(ahi[:, k, :], alo[:, k, :]) for k in range(2)],
                                 s["down_mm"], s["down_add"], i - 1)
                phases(pe, up, down)

            @block.scalar
            def _(act):
                norm.scalar(act)

                def up(i):
                    for t in range(n_up):
                        act.wait_ge(st.used, st.done(i, t))
                        if gated:
                            f = (t // 2) + (t % 2) * FT
                            U = UV if t % 2 else UG
                            wait(act, s["prod"], 2 * i + t // 2)
                            act.activation(U, pair[t % 2], ACT.Identity, bias=c.par[:, ds(2 * i + (C_FCB + f), 1)],
                                           scale=c.par[:, ds(2 * i + (C_FCW + 4 * FT + f), 1)]).then_inc(s["base"], 1)
                            if t % 2 == 0:
                                act.wait_ge(s["conv"], 4 * i + t + 1)
                                act.activation(UG, UG, ACT.Silu).then_inc(s["silu"], 1)
                        else:
                            wait(act, s["prod"], 2 * i + t - 1)
                            act.activation((UG, UV)[t], pair[t], ACT.Relu).then_inc(s["base"], 1)
                    for k in range(2):
                        act.wait_ge(s["prod"], 2 * i + k + 1)
                        if not (isinstance(i, int) and i == 0):
                            act.wait_ge(st.used, st.done(i, n_up + 1))
                        act.copy(ahi[:, k, :], A[:, k, :]).then_inc(s["a_hi"], 1)
                phases(act, up, lambda i: None)

            @block.vector
            def _(dve):
                norm.vector(dve)
                dve.sem_inc(s["down_add"], 1)

                def low(i):
                    for k in range(2):
                        dve.wait_ge(s["a_hi"], 2 * i + k + 1)
                        dve.tensor_tensor(alo[:, k, :], A[:, k, :], ahi[:, k, :].bitcast(F32),
                                          ALU.subtract).then_inc(s["a_lo"], 1)

                def up(i):
                    for t in range(n_up):
                        dve.wait_ge(s["base"], i * n_up + t + 1)
                        if gated:
                            f = (t // 2) + (t % 2) * FT
                            U = UV if t % 2 else UG
                            for tap in (1, 0):
                                lag = 2 - tap
                                dve.scalar_tensor_tensor(
                                    out=U[:, lag:SEQ], in0=pair[t % 2][:, 0:SEQ - lag],
                                    scalar=c.par[:, ds(2 * i + (C_FCW + tap * 2 * FT + f), 1)],
                                    in1=U[:, lag:SEQ], op0=ALU.mult, op1=ALU.add)
                                if tap:
                                    dve.drain()
                            dve.drain().then_inc(s["conv"], 1)
                            if t % 2:
                                dve.wait_ge(s["silu"], 2 * i + t // 2 + 1)
                                if not isinstance(i, int):
                                    dve.wait_ge(s["a_lo"], 2 * i)
                                dve.tensor_tensor(A[:, t // 2, :], UG, UV, ALU.mult).then_inc(s["prod"], 1)
                        else:
                            U = (UG, UV)[t]
                            if not isinstance(i, int):
                                dve.wait_ge(s["a_lo"], 2 * i)
                            dve.tensor_tensor(A[:, t, :], U, U, ALU.mult).then_inc(s["prod"], 1)

                def down(i):
                    base = n_up if not (isinstance(i, int) and i == chunks) else 0
                    add_down(dve, c, st, s["down_mm"], s["down_add"], i, base + 1, i - 1)

                up(0)
                low(0)
                with dve.Fori(1, chunks) as i:
                    up(i)
                    down(i)
                    low(i)
                down(chunks)

    def hybrid(self):
        nc, c, a = self.nc, self.core, self.a
        W = a["w_in_2"][0].rearrange("(k p) n -> p k n", p=P)
        WO = a["w_out_2"][0].rearrange("(k p) n -> p k n", p=P)
        WR = a["w_r_2"][0].rearrange("n (j p) k -> p n j k", p=P)
        WI = a["w_i_2"][0].rearrange("n (j p) k -> p n j k", p=P)
        XA_, GA_, Q_, F_, V_, G_, MA_, MB_ = (n * D for n in range(8))
        POS = {n: k for k, n in enumerate((
            "xa0", "xa1", "q0", "f0", "v0", "v1", "ga0", "ma0", "g0", "mb0", "dn0",
            "q1", "f1", "ga1", "ma1", "g1", "mb1", "dn1"))}
        PAIRS = HG_HEADS // 2
        with ExitStack() as ctx:
            def sb(name, shape, dt=F32):
                return ctx.enter_context(nc.sbuf_tensor(f"hy_{name}", shape, dt))[:]

            self.split_slots(ctx, "hy", 3)
            XA = sb("xa", [P, 2, SEQ])
            GM, Q, F, K, GB, TM = (sb(n, [P, SEQ]) for n in ("gm", "q", "f", "k", "gb", "tm"))
            V = sb("v", [P, MT, 2 * HG_DV])
            T1, T2, T3, T4 = (sb(n, [P, SEQ]) for n in ("t1", "t2", "t3", "t4"))
            TOT, SC, KTT, ON = T1, T2, T3, T4
            yhi, ylo = sb("y_hi", [P, SEQ], F32R), sb("y_lo", [P, SEQ], F32R)
            WRI = sb("w_ri", [P, 2, 2, 2 * P])
            S = sb("state", [P, 2, HG_DV])
            oss, oms, osd, ors = (sb(n, [P, MT]) for n in ("o_ss", "o_ms", "o_sd", "o_rs"))
            st = Stream(self.sem, "hy", c, 3, 18, 18)
            fin = RowNorm(self.sem, "hy_fin", c, K, GM)
            xn = V.rearrange("p (b m) v -> p b (m v)", b=2)
            norm = Norm(self.sem, "hy_norm", c, xn, F, Q, lambda m: (fin.scaled, m + 1))
            s = {n: self.sem(f"hy_{n}") for n in (
                "wri_in", "xa_base", "conv", "q", "f", "kf", "v_mm", "v", "gates_mm", "r", "i",
                "lru_a", "lru_m", "lru_sd", "h", "ga", "ma", "gh", "g", "mb", "gb", "diag_mm", "sc0",
                "qp", "lev_mm", "lev", "pc", "kt_mm", "kt", "kv_mm", "s", "o_mm", "o_sq", "o_ms",
                "o_sd", "on", "ot_mm", "y", "y_hi", "y_lo", "down_mm", "down_add")}
            TOT_AT = [None, 0, 512, 768, 896, 960, 992, 1008]
            block = ctx.enter_context(nc.Block())

            def phases(eng, body):
                body(0)
                with eng.Fori(1, PAIRS) as i:
                    body(i)

            def tiles(x):
                return x.rearrange("p (m n) -> p m n", n=P)

            def halves(x, n, tiled=False):
                if tiled:
                    return x.rearrange("p (m b h n) -> p m b h n", m=MT, h=2, n=n)
                return x.rearrange("p (b h n) -> p b h n", h=2, n=n)

            @block.sync
            def _(sp):
                sp.dma_start(fin.row, a["final_norm_w"].partition_broadcast(P)).then_inc(fin.row_in, 16)
                sp.dma_start(norm.row, a["norm_mix_2"][0].partition_broadcast(P)).then_inc(norm.row_in, 16)

                def body(i):
                    def cols(name, off, j=0):
                        st.load(sp, i, POS[name], W[:, :, ds(i * (2 * P) + (off + j * P), P)], KT)

                    cols("xa0", XA_)
                    cols("xa1", XA_, 1)
                    wait(sp, s["gates_mm"], 4 * i)
                    sp.dma_start(WRI[:, 0, :, :], WR[:, ds(i, 1), :, :].rearrange("p n j k -> p (n j) k"))\
                        .then_inc(s["wri_in"], 16)
                    sp.dma_start(WRI[:, 1, :, :], WI[:, ds(i, 1), :, :].rearrange("p n j k -> p (n j) k"))\
                        .then_inc(s["wri_in"], 16)
                    for j in range(2):
                        cols(f"q{j}", Q_, j)
                        cols(f"f{j}", F_, j)
                        if j == 0:
                            for u in range(2):
                                st.load(sp, i, POS[f"v{u}"], W[:, 4 * u:4 * u + 4, ds(i * (2 * P) + V_, 2 * P)], 4)
                        cols(f"ga{j}", GA_, j)
                        cols(f"ma{j}", MA_, j)
                        cols(f"g{j}", G_, j)
                        cols(f"mb{j}", MB_, j)
                        st.load(sp, i, POS[f"dn{j}"], WO[:, ds(2 * i + j, 1), :].rearrange("p k n -> p (k n)"), 0)
                phases(sp, body)

            @block.gpsimd
            def _(pool):
                def body(i):
                    for pos in range(18):
                        st.divide(pool, i, pos)
                phases(pool, body)

            @block.tensor
            def _(pe):
                pe.sem_inc(st.used, 1)
                norm.tensor(pe)

                def body(i):
                    def tile(name, pair, sem, count):
                        wait(pe, sem, count)
                        columns_tile(pe, c, st, i, POS[name], pair).then_inc(st.used, 1)

                    def value_tiles():
                        pos = POS["v0"]
                        pe.wait_ge(st.split, st.ready(i, pos + 1))
                        parts = [[x.rearrange("p (k n) -> p k n", k=4) for x in st.slot(i, pos + u)]
                                 for u in range(2)]
                        for n, pair in enumerate((c.PA, c.PB)):
                            pe.wait_ge(*((s["q"], 2 * i + 1), (s["f"], 2 * i + 1))[n])
                            for q in range(4):
                                m = 4 * n + q
                                rows = slice(m * P, (m + 1) * P)
                                for k in range(KT):
                                    wh, wl = parts[k // 4]
                                    mm = product(pe, pair[:, q * 2 * P:(q + 1) * 2 * P],
                                                 (c.hhi[:, k, rows], c.hlo[:, k, rows]),
                                                 (wh[:, k % 4, :], wl[:, k % 4, :]), k == 0, k == KT - 1)
                            if n == 0:
                                mm.then_inc(s["v_mm"], 1)
                        mm.then_inc(st.used, 2)

                    def gate(which, j, pair, sem, count):
                        wait(pe, sem, count)
                        for half in range(2):
                            cols = slice(half * HALF, (half + 1) * HALF)
                            for jj in range(2):
                                mm = pe.matmul(pair[:, cols], WRI[:, which, jj, j * P:(j + 1) * P],
                                               XA[:, jj, cols], start=(jj == 0), stop=(jj == 1))
                        mm.then_inc(s["gates_mm"], 1)

                    def hgrn(j):
                        hd = 2 * i + j
                        KT_, QT, VT = tiles(K), tiles(Q), V[:, :, j * HG_DV:(j + 1) * HG_DV]
                        MT_ = tiles(c.MM)
                        pe.wait_ge(s["kf"], hd + 1)
                        pe.wait_ge(s["q"], hd + 1)
                        wait(pe, s["y"], hd)
                        for m in range(MT):
                            mm = pe.matmul(MT_[:, m, :], KT_[:, m, :], QT[:, m, :], start=True, stop=True)
                        mm.then_inc(s["diag_mm"], 1)
                        for l in range(LEVELS):
                            if l == 0:
                                pe.wait_ge(s["qp"], hd + 1)
                            else:
                                pe.wait_ge(s["lev"], hd * LEVELS + l)
                                wait(pe, s["pc"], hd * LEVELS + l - 1)
                            bank = c.MM[:, (l % 2) * HALF:(l % 2 + 1) * HALF]
                            right = halves(Q, 1 << l, True)
                            for m in range(MT):
                                mm = pe.matmul(bank[:, m * (P // 2):(m + 1) * (P // 2)].rearrange(
                                    "p (b n) -> p b n", n=1 << l), KT_[:, m, :], right[:, m, :, 1, :],
                                    start=True, stop=True)
                            mm.then_inc(s["lev_mm"], 1)
                        pe.wait_ge(s["lev"], (hd + 1) * LEVELS)
                        pe.wait_ge(s["pc"], (hd + 1) * LEVELS)
                        for m in range(MT):
                            mm = pe.transpose(MT_[:, m, :], KT_[:, m, :], c.ident)
                        mm.then_inc(s["kt_mm"], 1)

                        def update(m):
                            if m < 2:
                                pe.wait_ge(s["down_add"], hd * DOWN + 1)
                            else:
                                pe.wait_ge(s["s"], hd * (MT - 1) + m - 1)
                            pe.matmul(c.DD[:, (m % 2) * HALF:(m % 2) * HALF + HG_DV],
                                      tiles(KTT)[:, m, :], VT[:, m, :], start=True, stop=True)\
                                .then_inc(s["kv_mm"], 1)

                        pe.wait_ge(s["kt"], hd + 1)
                        pe.wait_ge(s["v"], 2 * i + 2)
                        update(0)
                        for m in range(MT):
                            if m + 1 < MT - 1:
                                update(m + 1)
                            if m:
                                pe.wait_ge(s["s"], hd * (MT - 1) + m)
                            mm = pe.matmul(MT_[:, m, :], tiles(SC)[:, m, :], VT[:, m, :], start=True, stop=(m == 0))
                            if m:
                                mm = pe.matmul(MT_[:, m, :], QT[:, m, :], S[:, (m - 1) % 2, :],
                                               start=False, stop=True)
                            mm.then_inc(s["o_mm"], 1)
                        pe.wait_ge(s["on"], hd + 1)
                        for m in range(MT):
                            mm = pe.transpose(MT_[:, m, :], tiles(ON)[:, m, :], c.ident)
                        mm.then_inc(s["ot_mm"], 1)

                    def down(j):
                        pe.wait_ge(s["y_lo"], 2 * i + j + 1)
                        down_product(pe, c, st, i, (POS[f"dn{j}"],), [(yhi, ylo)],
                                     s["down_mm"], s["down_add"], 2 * i + j)

                    tile("xa0", c.PA, s["g"], 2 * i)
                    tile("xa1", c.PB, s["mb"], 2 * i)
                    tile("q0", c.PA, s["conv"], 2 * i + 1)
                    tile("f0", c.PB, s["conv"], 2 * i + 2)
                    value_tiles()
                    pe.wait_ge(s["wri_in"], i * 32 + 32)
                    gate(0, 0, c.PA, s["v"], 2 * i + 1)
                    gate(1, 0, c.PB, s["v"], 2 * i + 2)
                    gate(0, 1, c.PA, s["r"], 2 * i + 1)
                    gate(1, 1, c.PB, s["i"], 2 * i + 1)
                    tile("ga0", c.PA, s["r"], 2 * i + 2)
                    tile("ma0", c.PB, s["i"], 2 * i + 2)
                    tile("g0", c.PA, s["ga"], 2 * i + 1)
                    tile("mb0", c.PB, s["ma"], 2 * i + 1)
                    hgrn(0)
                    down(0)
                    tile("q1", c.PA, s["g"], 2 * i + 1)
                    tile("f1", c.PB, s["mb"], 2 * i + 1)
                    tile("ga1", c.PA, s["q"], 2 * i + 2)
                    tile("ma1", c.PB, s["f"], 2 * i + 2)
                    tile("g1", c.PA, s["ga"], 2 * i + 2)
                    tile("mb1", c.PB, s["ma"], 2 * i + 2)
                    hgrn(1)
                    down(1)
                phases(pe, body)

            @block.scalar
            def _(act):
                fin.scalar(act)
                norm.scalar(act)

                def body(i):
                    def par(col, j):
                        return c.par[:, ds(2 * i + (col + j), 1)]

                    for j, pair in ((0, c.PA), (1, c.PB)):
                        act.wait_ge(st.used, st.done(i, POS[f"xa{j}"]))
                        wait(act, s["gh"], 2 * i)
                        act.activation(XA[:, j, :], pair, ACT.Identity, bias=par(C_CB, j),
                                       scale=par(C_CW + 24, j)).then_inc(s["xa_base"], 1)

                    def query(j):
                        hd = 2 * i + j
                        act.wait_ge(st.used, st.done(i, POS[f"q{j}"]))
                        wait(act, s["o_mm"], hd * MT)
                        act.activation(Q, c.PA, ACT.Silu).then_inc(s["q"], 1)
                        act.wait_ge(st.used, st.done(i, POS[f"f{j}"]))
                        act.activation(F, c.PB, ACT.Sigmoid)
                        act.activation(K, c.PB, ACT.Sigmoid, scale=-1.0).then_inc(s["f"], 1)

                    def lru(j):
                        act.wait_ge(s["gates_mm"], 4 * i + 2 * j + 1)
                        wait(act, s["y_lo"], 2 * i)
                        if j:
                            act.wait_ge(s["h"], 2 * i + 1)
                        act.activation(T1, c.PA, ACT.Sigmoid, bias=par(C_BR, j)).then_inc(s["r"], 1)
                        act.wait_ge(s["gates_mm"], 4 * i + 2 * j + 2)
                        act.activation(T2, c.PB, ACT.Sigmoid, bias=par(C_BI, j)).then_inc(s["i"], 1)
                        act.drain()
                        act.activation(T3, T1, ACT.Tanh, scale=c.decay[:, 1, ds(2 * i + j, 1)])
                        act.drain()
                        act.activation(T1, T1, ACT.Exp, scale=c.decay[:, 0, ds(2 * i + j, 1)])\
                            .then_inc(s["lru_a"], 1)
                        act.wait_ge(s["lru_m"], 2 * i + j + 1)
                        act.activation(T3, T3, ACT.Sqrt).then_inc(s["lru_sd"], 1)

                    def gates(j):
                        hd = 2 * i + j
                        act.wait_ge(st.used, st.done(i, POS[f"ga{j}"]))
                        wait(act, s["y"], hd)
                        act.activation(GM, c.PA, ACT.Gelu_apprx_tanh).then_inc(s["ga"], 1)
                        act.wait_ge(st.used, st.done(i, POS[f"ma{j}"]))
                        wait(act, s["gb"], hd)
                        act.activation(TM, c.PB, ACT.Sigmoid).then_inc(s["ma"], 1)
                        act.wait_ge(st.used, st.done(i, POS[f"g{j}"]))
                        act.activation(GB, c.PA, ACT.Silu).then_inc(s["g"], 1)
                        act.wait_ge(st.used, st.done(i, POS[f"mb{j}"]))
                        act.wait_ge(s["gh"], hd + 1)
                        act.activation(TM, c.PB, ACT.Sigmoid).then_inc(s["mb"], 1)

                    def hgrn(j):
                        hd = 2 * i + j
                        act.wait_ge(s["o_mm"], (hd + 1) * MT)
                        act.activation(TOT, c.MM, ACT.Square).then_inc(s["o_sq"], 1)
                        act.wait_ge(s["o_ms"], hd + 1)
                        act.activation(osd, oms, ACT.Sqrt).then_inc(s["o_sd"], 1)
                        act.wait_ge(s["y"], hd + 1)
                        act.copy(yhi, SC).then_inc(s["y_hi"], 1)

                    query(0)
                    for n, pair in ((0, c.PA), (1, c.PB)):
                        act.wait_ge(*((s["v_mm"], i + 1) if n == 0 else (st.used, st.done(i, POS["v1"]))))
                        act.copy(V[:, 4 * n:4 * n + 4, :], pair.rearrange("p (m v) -> p m v", v=2 * HG_DV))\
                           .then_inc(s["v"], 1)
                    lru(0)
                    lru(1)
                    gates(0)
                    hgrn(0)
                    query(1)
                    gates(1)
                    hgrn(1)
                phases(act, body)

            @block.vector
            def _(dve):
                fin.vector(dve)
                norm.vector(dve)
                dve.sem_inc(s["down_add"], 1)

                def body(i):
                    def par(col, j):
                        return c.par[:, ds(2 * i + (col + j), 1)]

                    for j, pair in ((0, c.PA), (1, c.PB)):
                        dve.wait_ge(s["xa_base"], 2 * i + j + 1)
                        for tap in (2, 1, 0):
                            lag = 3 - tap
                            mm = dve.scalar_tensor_tensor(
                                out=XA[:, j, lag:SEQ], in0=pair[:, 0:SEQ - lag], scalar=par(C_CW + 8 * tap, j),
                                in1=XA[:, j, lag:SEQ], op0=ALU.mult, op1=ALU.add)
                            if tap:
                                dve.drain()
                        mm.then_inc(s["conv"], 1)

                    def forget(j):
                        hd = 2 * i + j
                        lb, rest = (c.lb[:, n, ds(2 * i + j, 1)] for n in range(2))
                        dve.wait_ge(s["f"], hd + 1)
                        dve.tensor_scalar(F, F, rest, lb, ALU.mult, ALU.add)
                        dve.tensor_scalar(K, K, rest, None, ALU.mult)
                        dve.drain()
                        dve.tensor_scalar(F, F, F_MIN, None, ALU.max).then_inc(s["kf"], 1)

                    def lru(j):
                        hd = 2 * i + j
                        dve.wait_ge(s["lru_a"], hd + 1)
                        dve.tensor_tensor(T4, T1, T1, ALU.mult)
                        dve.drain()
                        dve.scalar_tensor_tensor(out=T3, in0=T4, scalar=1.0, in1=T3, op0=ALU.add, op1=ALU.mult)
                        dve.drain()
                        dve.tensor_scalar(T3, T3, 0.0, None, ALU.max).then_inc(s["lru_m"], 1)
                        dve.tensor_tensor(T2, T2, XA[:, j, :], ALU.mult)
                        dve.drain()
                        dve.wait_ge(s["lru_sd"], hd + 1)
                        dve.tensor_tensor(T2, T2, T3, ALU.mult)
                        dve.drain()
                        dve.wait_ge(s["gates_mm"], 4 * i + 4)
                        dve.tensor_tensor_scan(XA[:, j, :], T1, T2, 0.0, ALU.mult, ALU.add).then_inc(s["h"], 1)

                    def gates(j):
                        hd = 2 * i + j
                        dve.wait_ge(s["ma"], hd + 1)
                        dve.tensor_tensor(GM, GM, TM, ALU.mult)
                        dve.drain()
                        dve.wait_ge(s["h"], 2 * i + 2)
                        dve.tensor_tensor(GM, GM, XA[:, j, :], ALU.mult).then_inc(s["gh"], 1)
                        dve.wait_ge(s["mb"], hd + 1)
                        dve.scalar_tensor_tensor(out=GB, in0=GB, scalar=c.par[:, C_HGN:C_HGN + 1], in1=TM,
                                                 op0=ALU.mult, op1=ALU.mult).then_inc(s["gb"], 1)

                    def hgrn(j):
                        hd = 2 * i + j
                        dve.wait_ge(s["diag_mm"], hd + 1)
                        dve.tensor_tensor(tiles(SC), tiles(c.MM), c.ident.unsqueeze(1).broadcast_to([P, MT, P]),
                                          ALU.mult).then_inc(s["sc0"], 1)
                        dve.tensor_tensor(Q, Q, F, ALU.mult).then_inc(s["qp"], 1)
                        for l in range(LEVELS):
                            n = 1 << l
                            nb = SEQ // (2 * n)
                            tot = F if l == 0 else TOT[:, TOT_AT[l]:TOT_AT[l] + 2 * nb]
                            left, right = (tot.rearrange("p (b h) -> p b h", h=2)[:, :, x] for x in range(2))
                            dve.drain()
                            dve.wait_ge(s["lev_mm"], hd * LEVELS + l + 1)
                            dve.tensor_tensor(halves(Q, n)[:, :, 1, :], halves(Q, n)[:, :, 1, :],
                                              left.unsqueeze(2).broadcast_to([P, nb, n]), ALU.mult)
                            dve.tensor_tensor(halves(K, n)[:, :, 0, :], halves(K, n)[:, :, 0, :],
                                              right.unsqueeze(2).broadcast_to([P, nb, n]), ALU.mult)
                            dve.tensor_tensor(TOT[:, TOT_AT[l + 1]:TOT_AT[l + 1] + nb], left, right, ALU.mult)\
                               .then_inc(s["lev"], 1)
                            bank = c.MM[:, (l % 2) * HALF:(l % 2 + 1) * HALF]
                            dve.copy_predicated(
                                halves(SC, n, True)[:, :, :, 1, :],
                                c.masks[:, l, :].rearrange("p (b n) -> p b n", n=n).unsqueeze(1).broadcast_to(
                                    [P, MT, P // (2 * n), n]),
                                bank.rearrange("p (m b n) -> p m b n", m=MT, n=n)).then_inc(s["pc"], 1)
                        dve.wait_ge(s["kt_mm"], hd + 1)
                        dve.tensor_copy(KTT, c.MM).then_inc(s["kt"], 1)
                        for m in range(MT - 1):
                            dve.wait_ge(s["kv_mm"], hd * (MT - 1) + m + 1)
                            wait(dve, s["o_mm"], hd * MT + m)
                            ps = c.DD[:, (m % 2) * HALF:(m % 2) * HALF + HG_DV]
                            if m == 0:
                                dve.tensor_copy(S[:, 0, :], ps).then_inc(s["s"], 1)
                            else:
                                dve.wait_ge(s["s"], hd * (MT - 1) + m)
                                dve.scalar_tensor_tensor(
                                    out=S[:, m % 2, :], in0=S[:, (m - 1) % 2, :],
                                    scalar=TOT[:, TOT_AT[7] + m:TOT_AT[7] + m + 1], in1=ps, op0=ALU.mult,
                                    op1=ALU.add).then_inc(s["s"], 1)
                        dve.wait_ge(s["o_sq"], hd + 1)
                        dve.tensor_reduce(oss, tiles(TOT), AX, ALU.add)
                        dve.drain()
                        dve.tensor_scalar(oms, oss, 1.0 / HG_DV, EPS, ALU.mult, ALU.add).then_inc(s["o_ms"], 1)
                        dve.wait_ge(s["o_sd"], hd + 1)
                        dve.reciprocal(ors, osd)
                        dve.drain()
                        dve.tensor_tensor(tiles(ON), tiles(c.MM), ors.unsqueeze(2).broadcast_to([P, MT, HG_DV]),
                                          ALU.mult).then_inc(s["on"], 1)
                        dve.wait_ge(s["ot_mm"], hd + 1)
                        dve.tensor_tensor(SC, c.MM, GB, ALU.mult)
                        dve.drain()
                        dve.tensor_tensor(SC, SC, GM, ALU.add).then_inc(s["y"], 1)
                        dve.wait_ge(s["y_hi"], hd + 1)
                        dve.tensor_tensor(ylo, SC, yhi.bitcast(F32), ALU.subtract).then_inc(s["y_lo"], 1)

                    def down(j):
                        add_down(dve, c, st, s["down_mm"], s["down_add"], i, POS[f"dn{j}"], 2 * i + j)

                    forget(0)
                    lru(0)
                    lru(1)
                    gates(0)
                    hgrn(0)
                    down(0)
                    forget(1)
                    gates(1)
                    hgrn(1)
                    down(1)
                phases(dve, body)

    def finish(self):
        nc, c, a = self.nc, self.core, self.a
        with ExitStack() as ctx:
            junk = ctx.enter_context(nc.sbuf_tensor("out_junk", [P, D], F32))[:]
            row = ctx.enter_context(nc.sbuf_tensor("out_row", [P, D], F32))[:]
            norm = RowNorm(self.sem, "out", c, junk, row)
            stored = self.sem("stored")
            block = ctx.enter_context(nc.Block())

            @block.sync
            def _(sp):
                sp.dma_start(row, a["norm_final_2"].partition_broadcast(P)).then_inc(norm.row_in, 16)
                for m in range(MT):
                    sp.wait_ge(norm.scaled, m + 1)
                    sp.dma_start(a["out"][0, m * P:(m + 1) * P, :], c.X[:, m, :]).then_inc(stored, 16)
                sp.wait_ge(stored, 16 * MT)

            @block.scalar
            def _(act):
                norm.scalar(act)

            @block.vector
            def _(dve):
                norm.vector(dve)


def build(nc, a):
    with ExitStack() as ctx:
        p = Program(nc, ctx, a)
        p.parameters()
        p.end_stage()
        p.gla()
        p.end_stage()
        p.ffn("f1", a["ffn_w_up"][0], a["ffn_w_down"][0], a["ffn_norm_w"][0], FT // 2, True)
        p.end_stage()
        p.hybrid()
        p.end_stage()
        p.ffn("f2", a["w_up_2"][0], a["w_down_2"][0], a["norm_mlp_2"][0], D_FF // (2 * P), False)
        p.end_stage()
        p.finish()


_INS = ["x", "mix_norm_w", "ffn_norm_w", "final_norm_w", "gla_w_in", "gla_w_gate2", "gla_b_gate",
        "gla_norm_w", "gla_w_out", "ffn_w_up", "ffn_conv_w", "ffn_conv_b", "ffn_w_down",
        "lb_logits_2", "norm_mix_2", "w_in_2", "conv_w_2", "conv_b_2", "w_r_2", "b_r_2", "w_i_2",
        "b_i_2", "lam_2", "hg_norm_2", "w_out_2", "norm_mlp_2", "w_up_2", "w_down_2", "norm_final_2"]


def kernel(**inputs):
    import numpy as _np
    import concourse.bacc as _bacc
    from concourse import mybir as _mybir
    from concourse.bass_utils import run_bass_kernel_spmd as _run

    nc = _bacc.Bacc("TRN2", target_bir_lowering=False, num_devices=1)
    arrays, aps = {}, {}
    for name in _INS:
        arrays[f"in_{name}"] = _np.ascontiguousarray(inputs[name])
    arrays["in_ident"] = _np.eye(P, dtype=_np.float32)
    masks = _np.zeros((P, LEVELS, P // 2), _np.float32)
    for l in range(LEVELS):
        n = 1 << l
        for t in range(P // 2):
            at = (t // n) * 2 * n
            masks[at:at + n, l, t] = 1
    arrays["in_masks"] = masks
    for name, x in arrays.items():
        aps[name[3:]] = nc.dram_tensor(name, x.shape, _mybir.dt.from_np(x.dtype), kind="ExternalInput").ap()
    aps["out"] = nc.dram_tensor("out", (1, SEQ, D), _mybir.dt.float32, kind="ExternalOutput").ap()
    build(nc, aps)
    r = _run(nc, [arrays], core_ids=[0])
    return r.results[0]["out"]
```

```python
from contextlib import ExitStack

import concourse.bass as bass
from concourse import mybir

ALU = mybir.AluOpType
ACT = mybir.ActivationFunctionType
AX = mybir.AxisListType.X
F32 = mybir.dt.float32
F32R = mybir.dt.float32r
BF16 = mybir.dt.bfloat16
U8 = mybir.dt.uint8
ds = bass.ds

P = 128
SEQ = 1024
D = 1024
MT = SEQ // P
DOWN = 2 * MT
KT = D // P
HALF = 512
UNIT = 1024
EPS = 1e-6

GLA_HEADS, DK, DV, RANK, TAU, CHUNK = 4, 128, 256, 16, 16.0, 64
NCH = SEQ // CHUNK
GLA_IN = 2 * GLA_HEADS * DK + 2 * GLA_HEADS * DV + RANK
FFN_DIM = 2816
FT = FFN_DIM // P
HG_HEADS, HG_DV, LEVELS = 8, 128, 7
RG_C = 8.0
F_MIN = 1e-30
D_FF = 4096

C_FCW, C_FCB = 0, 3 * 2 * FT
C_BG = C_FCB + 2 * FT
C_GNW = C_BG + 4
C_CW = C_GNW + 8
C_CB = C_CW + 32
C_BR = C_CB + 8
C_BI = C_BR + 8
C_LAM = C_BI + 8
C_HGN = C_LAM + 8
C_LB = C_HGN + 1
C_END = C_LB + 8
ROWS = 4 * FT


def wait(eng, sem, value):
    if isinstance(value, int) and value <= 0:
        return
    eng.wait_ge(sem, value)


class Core:
    pass


class Stream:

    def __init__(self, sem, name, core, slots, first, per):
        self.slots, self.first, self.per, self.core = slots, first, per, core
        self.raw_in = [sem(f"{name}_raw_in{n}") for n in range(2)]
        self.hi_done = sem(f"{name}_hi_done")
        self.split = sem(f"{name}_split")
        self.used = sem(f"{name}_used")

    def number(self, it, pos):
        if isinstance(it, int) and it == 0:
            return pos, pos
        return self.first + pos, (it - 1) * self.per + self.first + pos

    def done(self, it, pos):
        return self.number(it, pos)[1] + 2

    def ready(self, it, pos):
        return self.number(it, pos)[1] + 1

    def slot(self, it, pos):
        n = self.number(it, pos)[0] % self.slots
        return self.core.whi[:, n, :], self.core.wlo[:, n, :]

    def load(self, sp, it, pos, source, dims):
        s, g = self.number(it, pos)
        wait(sp, self.split, g - 1)
        dst = self.core.raw[:, s % 2, :]
        if dims:
            dst = dst.rearrange("p (k n) -> p k n", k=dims)
        sp.dma_start(dst, source).then_inc(self.raw_in[s % 2], 16)

    def divide(self, pool, it, pos):
        s, g = self.number(it, pos)
        hi, lo = self.slot(it, pos)
        raw = self.core.raw[:, s % 2, :]
        if isinstance(g, int):
            arrived = 16 * (g // 2 + 1)
        else:
            arrived = (it - 1) * (8 * self.per) + 16 * (s // 2 + 1)
        pool.wait_ge(self.raw_in[s % 2], arrived)
        wait(pool, self.used, g - self.slots + 2)
        pool.tensor_tensor(hi, raw, self.core.zero[:, 0:1].broadcast_to([P, UNIT]), ALU.add)\
            .then_inc(self.hi_done, 1)
        pool.wait_ge(self.hi_done, g + 1)
        pool.tensor_tensor(lo, raw, hi.bitcast(F32), ALU.subtract).then_inc(self.split, 1)


def product(pe, out, a, b, first, last):
    (ah, al), (bh, bl) = a, b
    pe.matmul(out, ah, bh, start=first, stop=False)
    pe.matmul(out, ah, bl, start=False, stop=False)
    return pe.matmul(out, al, bh, start=False, stop=last)


def columns_half(pe, core, st, it, pos, pair, half):
    if half == 0:
        pe.wait_ge(st.split, st.ready(it, pos))
    hi, lo = (x.rearrange("p (k n) -> p k n", k=KT) for x in st.slot(it, pos))
    cols = slice(half * HALF, (half + 1) * HALF)
    for k in range(KT):
        mm = product(pe, pair[:, cols], (hi[:, k, :], lo[:, k, :]),
                     (core.hhi[:, k, cols], core.hlo[:, k, cols]), k == 0, k == KT - 1)
    if half:
        mm.then_inc(st.used, 1)


def columns_tile(pe, core, st, it, pos, pair):
    columns_half(pe, core, st, it, pos, pair, 0)
    columns_half(pe, core, st, it, pos, pair, 1)


def rows_group(pe, core, parts, pair, m, first):
    rows = slice(m * P, (m + 1) * P)
    for k in range(KT):
        wh, wl = parts[k // 4]
        mm = product(pe, pair[:, (m - first) * 2 * P:(m - first + 1) * 2 * P],
                     (core.hhi[:, k, rows], core.hlo[:, k, rows]),
                     (wh[:, k % 4, :], wl[:, k % 4, :]), k == 0, k == KT - 1)
    return mm


def row_parts(st, it, pos):
    return [[x.rearrange("p (k n) -> p k n", k=4) for x in st.slot(it, pos + u)] for u in range(2)]


def down_tile(pe, core, m, half, parts, weights, bank):
    n = len(parts)
    rows, cols = slice(m * P, (m + 1) * P), slice(half * HALF, (half + 1) * HALF)
    for k, ((ah, al), (wh, wl)) in enumerate(zip(parts, weights)):
        mm = product(pe, bank, (ah[:, rows], al[:, rows]), (wh[:, cols], wl[:, cols]),
                     k == 0, k == n - 1)
    return mm


class Norm:
    def __init__(self, sem, name, core, xn, junk, row, ready=None):
        self.core, self.xn, self.junk, self.row, self.ready = core, xn, junk, row, ready
        self.row_in, self.squared, self.var, self.root, self.scaled, self.turned, self.hi, self.lo = (
            sem(f"{name}_{s}") for s in ("row_in", "squared", "var", "root", "scaled", "turned", "hi", "lo"))

    def pair(self, m):
        return self.core.DD if m % 2 == 0 else self.core.MM

    def scalar(self, act):
        c = self.core

        def square(m):
            if self.ready:
                act.wait_ge(*self.ready(m))
            act.activation(self.junk, c.X[:, m, :], ACT.Square, accum_out=c.ss[:, m:m + 1])\
                .then_inc(self.squared, 1)

        def root(m):
            act.wait_ge(self.var, m + 1)
            act.activation(c.sd[:, m:m + 1], c.ms[:, m:m + 1], ACT.Sqrt).then_inc(self.root, 1)

        def high(m):
            act.wait_ge(self.turned, m + 1)
            act.copy(c.hhi[:, :, m * P:(m + 1) * P],
                     self.pair(m).rearrange("p (k n) -> p k n", k=KT)).then_inc(self.hi, 1)

        for n in range(MT + 3):
            if n < MT:
                if n:
                    act.wait_ge(self.squared, n)
                square(n)
            if 1 <= n <= MT:
                root(n - 1)
            if n >= 3:
                high(n - 3)

    def vector(self, dve):
        c = self.core
        dve.wait_ge(self.row_in, 16)
        for n in range(MT + 3):
            if n < MT:
                dve.wait_ge(self.squared, n + 1)
                dve.tensor_scalar(c.ms[:, n:n + 1], c.ss[:, n:n + 1], 1.0 / D, EPS, ALU.mult,
                                  ALU.add).then_inc(self.var, 1)
            if 1 <= n <= MT:
                m = n - 1
                dve.wait_ge(self.root, m + 1)
                dve.reciprocal(c.rs[:, m:m + 1], c.sd[:, m:m + 1])
                dve.drain()
                wait(dve, self.turned, m - 1)
                dve.scalar_tensor_tensor(out=self.xn[:, m % 2, :], in0=c.X[:, m, :],
                                         scalar=c.rs[:, m:m + 1], in1=self.row, op0=ALU.mult,
                                         op1=ALU.mult).then_inc(self.scaled, 1)
            if n >= 3:
                m = n - 3
                dve.wait_ge(self.hi, m + 1)
                rows = slice(m * P, (m + 1) * P)
                dve.tensor_tensor(c.hlo[:, :, rows], self.pair(m).rearrange("p (k n) -> p k n", k=KT),
                                  c.hhi[:, :, rows].bitcast(F32), ALU.subtract).then_inc(self.lo, 1)

    def tensor(self, pe):
        for m in range(MT):
            pe.wait_ge(self.scaled, m + 1)
            wait(pe, self.lo, m - 1)
            for k in range(KT):
                mm = pe.transpose(self.pair(m)[:, k * P:(k + 1) * P],
                                  self.xn[:, m % 2, k * P:(k + 1) * P], self.core.ident[:, :])
            mm.then_inc(self.turned, 1)
        pe.wait_ge(self.lo, MT)


def down_product(pe, c, st, it, positions, parts, down_mm, down_add, before, banks=2, hook=None):
    pe.wait_ge(st.split, st.ready(it, positions[-1]))
    weights = [st.slot(it, pos) for pos in positions]
    for m in range(MT):
        if hook and m:
            hook(m)
        for half in range(2):
            n = 2 * m + half
            pe.wait_ge(down_add, before * DOWN + max(n - banks + 2, 1))
            mm = down_tile(pe, c, m, half, parts, weights, down_bank(c, n, banks))
            if n < DOWN - 1:
                mm.then_inc(down_mm, 1)
    mm.then_inc(st.used, len(positions))


def down_bank(c, n, banks):
    return (c.DD, c.MM)[n % banks // 2][:, (n % 2) * HALF:(n % 2 + 1) * HALF]


class RowNorm:

    def __init__(self, sem, name, core, junk, row):
        self.core, self.junk, self.row = core, junk, row
        self.row_in, self.squared, self.var, self.root, self.scaled = (
            sem(f"{name}_{s}") for s in ("row_in", "squared", "var", "root", "scaled"))

    def scalar(self, act):
        c = self.core
        for n in range(MT + 1):
            if n < MT:
                wait(act, self.squared, n)
                act.activation(self.junk, c.X[:, n, :], ACT.Square, accum_out=c.ss[:, n:n + 1])\
                    .then_inc(self.squared, 1)
            if n:
                act.wait_ge(self.var, n)
                act.activation(c.sd[:, n - 1:n], c.ms[:, n - 1:n], ACT.Sqrt).then_inc(self.root, 1)

    def vector(self, dve):
        c = self.core
        dve.wait_ge(self.row_in, 16)
        for n in range(MT + 1):
            if n < MT:
                dve.wait_ge(self.squared, n + 1)
                dve.tensor_scalar(c.ms[:, n:n + 1], c.ss[:, n:n + 1], 1.0 / D, EPS, ALU.mult,
                                  ALU.add).then_inc(self.var, 1)
            if n:
                m = n - 1
                dve.wait_ge(self.root, m + 1)
                dve.reciprocal(c.rs[:, m:m + 1], c.sd[:, m:m + 1])
                dve.drain()
                dve.scalar_tensor_tensor(out=c.X[:, m, :], in0=c.X[:, m, :], scalar=c.rs[:, m:m + 1],
                                         in1=self.row, op0=ALU.mult, op1=ALU.mult).then_inc(self.scaled, 1)


def add_down(dve, c, st, down_mm, down_add, it, pos, before, banks=2):
    for m in range(MT):
        for half in range(2):
            n = 2 * m + half
            if n < DOWN - 1:
                dve.wait_ge(down_mm, before * (DOWN - 1) + n + 1)
            else:
                dve.wait_ge(st.used, st.done(it, pos))
            cols = slice(half * HALF, (half + 1) * HALF)
            dve.tensor_tensor(c.X[:, m, cols], c.X[:, m, cols], down_bank(c, n, banks), ALU.add)\
               .then_inc(down_add, 1)


class Program:
    def __init__(self, nc, ctx, a):
        self.nc, self.ctx, self.a = nc, ctx, a
        self.stage_sems = []
        c = self.core = Core()
        c.X = self.sb("X", [P, MT, D])
        c.hhi = self.sb("h_hi", [P, KT, SEQ], F32R)
        c.hlo = self.sb("h_lo", [P, KT, SEQ], F32R)
        c.raw = self.sb("w_raw", [P, 2, UNIT])
        c.zero = self.sb("zero", [P, 1])
        c.ident = self.sb("ident", [P, P])
        c.masks = self.sb("masks", [P, LEVELS, P // 2], U8)
        c.par = self.sb("params", [P, C_END])
        c.decay = self.sb("lru_decay", [P, 2, 8])
        c.lb = self.sb("lower_bound", [P, 2, 8])
        c.ss, c.ms, c.sd, c.rs = (self.sb(n, [P, MT]) for n in ("ss", "ms", "sd", "rs"))
        c.PA = self.ps("PA", [P, SEQ])
        c.PB = self.ps("PB", [P, SEQ])
        c.DD = self.ps("DD", [P, SEQ])
        c.MM = self.ps("MM", [P, SEQ])
        self.x_in = [ctx.enter_context(nc.semaphore(f"x_in{m}")) for m in range(MT)]

    def sb(self, name, shape, dt=F32):
        return self.ctx.enter_context(self.nc.sbuf_tensor(name, shape, dt))[:]

    def ps(self, name, shape):
        return self.ctx.enter_context(self.nc.psum_tensor(name, shape, F32))[:]

    def sem(self, name):
        handle = self.nc.alloc_semaphore(name)
        self.stage_sems.append(handle)
        return handle

    def end_stage(self):
        self.nc.clear_and_free_semaphores(self.stage_sems)
        self.nc.all_engine_barrier()
        self.stage_sems = []

    def split_slots(self, ctx, name, slots):
        c = self.core
        c.whi = ctx.enter_context(self.nc.sbuf_tensor(f"{name}_w_hi", [P, slots, UNIT], F32R))[:]
        c.wlo = ctx.enter_context(self.nc.sbuf_tensor(f"{name}_w_lo", [P, slots, UNIT], F32R))[:]

    def parameters(self):
        nc, c, a = self.nc, self.core, self.a
        with ExitStack() as ctx:
            rows = ctx.enter_context(nc.sbuf_tensor("param_rows", [P, 3, P], F32))[:]
            t = ctx.enter_context(nc.sbuf_tensor("param_temps", [P, 6, 8], F32))[:]
            maskf = ctx.enter_context(nc.sbuf_tensor("masks_in", [P, LEVELS, P // 2], F32))[:]
            s_rows, s_id, s_par, s_turn, s_zero = (self.sem(n) for n in (
                "rows_in", "ident_in", "params_ready", "params_turned", "rows_zeroed"))
            s_abs, s_exp, s_lb = self.sem("lam_abs"), self.sem("lam_exp"), self.sem("lb_exp")
            s_e = self.sem("lb_shifted")
            last = C_END - 2 * ROWS
            block = ctx.enter_context(nc.Block())

            @block.sync
            def _(sp):
                sp.dma_start(c.ident, a["ident"]).then_inc(s_id, 16)
                sp.dma_start(maskf, a["masks"]).then_inc(s_id, 16)
                taps = a["ffn_conv_w"][0].rearrange("t (f p) -> (t f) p", p=P)
                sp.dma_start(rows[0:ROWS, 0, :], taps[0:ROWS, :]).then_inc(s_rows, 16)
                sp.dma_start(rows[0:2 * FT, 1, :], taps[ROWS:3 * 2 * FT, :]).then_inc(s_rows, 16)
                sp.dma_start(rows[2 * FT:ROWS, 1, :],
                             a["ffn_conv_b"][0].rearrange("(f p) -> f p", p=P)).then_inc(s_rows, 16)
                n = 0
                for src in (
                    a["gla_b_gate"][0].rearrange("(f p) -> f p", p=P),
                    a["gla_norm_w"][0].rearrange("(f p) -> f p", p=P),
                    a["conv_w_2"][0].rearrange("t (f p) -> (t f) p", p=P),
                    a["conv_b_2"][0].rearrange("(f p) -> f p", p=P),
                    a["b_r_2"][0].rearrange("(f p) -> f p", p=P),
                    a["b_i_2"][0].rearrange("(f p) -> f p", p=P),
                    a["lam_2"][0].rearrange("(f p) -> f p", p=P),
                    a["hg_norm_2"],
                    a["lb_logits_2"][0].rearrange("(f p) -> f p", p=P),
                ):
                    k = src.shape[0]
                    sp.dma_start(rows[n:n + k, 2, :], src).then_inc(s_rows, 16)
                    n += k
                for m in range(MT):
                    sp.dma_start(c.X[:, m, :], a["x"][0, m * P:(m + 1) * P, :]).then_inc(self.x_in[m], 16)

            @block.tensor
            def _(pe):
                pe.wait_ge(s_id, 32)
                pe.wait_ge(s_rows, 16 * 12)
                for g in range(3):
                    k = ROWS if g < 2 else last
                    mm = pe.transpose(c.MM[:, g * ROWS:g * ROWS + k], rows[0:k, g, :], c.ident[0:k, 0:k])
                mm.then_inc(s_turn, 1)

            @block.scalar
            def _(act):
                act.wait_ge(s_abs, 1)
                act.activation(t[:, 1, :], t[:, 0, :], ACT.Exp, scale=-1.0).then_inc(s_exp, 1)
                act.wait_ge(s_e, 1)
                act.activation(t[:, 5, :], t[:, 4, :], ACT.Exp).then_inc(s_lb, 1)

            @block.vector
            def _(dve):
                def then(ins):
                    dve.drain()
                    return ins

                dve.memset(c.zero, 0.0)
                dve.wait_ge(s_id, 32)
                dve.tensor_copy(c.masks, maskf)
                dve.wait_ge(s_turn, 1)
                then(dve.tensor_copy(c.par, c.MM[:, 0:C_END]))
                lam, lbl = c.par[:, C_LAM:C_LAM + 8], c.par[:, C_LB:C_LB + 8]
                dve.tensor_scalar(t[:, 2, :], lam, -1.0, 0.0, ALU.mult, ALU.max)
                then(dve.tensor_scalar(t[:, 3, :], lam, 0.0, None, ALU.max))
                dve.tensor_tensor(t[:, 0, :], t[:, 2, :], t[:, 3, :], ALU.add).then_inc(s_abs, 1)
                dve.tensor_tensor(t[:, 4, :], lbl, lbl, ALU.subtract).then_inc(s_e, 1)
                dve.wait_ge(s_exp, 1)
                then(dve.tensor_scalar(t[:, 3, :], t[:, 1, :], 2.0, None, ALU.add))
                then(dve.reciprocal(t[:, 3, :], t[:, 3, :]))
                then(dve.tensor_tensor(t[:, 1, :], t[:, 1, :], t[:, 3, :], ALU.mult))
                then(dve.tensor_tensor(t[:, 3, :], t[:, 1, :], t[:, 1, :], ALU.mult))
                then(dve.tensor_scalar(t[:, 0, :], t[:, 3, :], 1.0 / 17, 1.0 / 15, ALU.mult, ALU.add))
                for d in (13, 11, 9, 7, 5, 3, 1):
                    then(dve.tensor_tensor(t[:, 0, :], t[:, 0, :], t[:, 3, :], ALU.mult))
                    then(dve.tensor_scalar(t[:, 0, :], t[:, 0, :], 1.0 / d, None, ALU.add))
                then(dve.tensor_tensor(t[:, 0, :], t[:, 0, :], t[:, 1, :], ALU.mult))
                then(dve.scalar_tensor_tensor(out=t[:, 0, :], in0=t[:, 0, :], scalar=2.0,
                                              in1=t[:, 2, :], op0=ALU.mult, op1=ALU.add))
                dve.tensor_scalar(c.decay[:, 0, :], t[:, 0, :], -RG_C, None, ALU.mult)
                dve.tensor_scalar(c.decay[:, 1, :], t[:, 0, :], RG_C, None, ALU.mult)
                dve.wait_ge(s_lb, 1)
                then(dve.reciprocal(t[:, 4, :], t[:, 5, :]))
                then(dve.tensor_tensor(t[:, 4, :], t[:, 4, :], t[:, 5, :], ALU.mult))
                then(dve.tensor_tensor(t[:, 5, :], t[:, 4, :], t[:, 4, :], ALU.subtract))
                then(dve.tensor_scalar(c.lb[:, 0, :], t[:, 5, :], 0.0, 1.0, ALU.max, ALU.min))
                dve.tensor_scalar(c.lb[:, 1, :], c.lb[:, 0, :], -1.0, 1.0, ALU.mult, ALU.add)\
                    .then_inc(s_par, 1)
                dve.wait_ge(s_par, 1)

    def gla(self):
        nc, c, a = self.nc, self.core, self.a
        W = a["gla_w_in"][0].rearrange("(k p) n -> p k n", p=P)
        WO = a["gla_w_out"][0].rearrange("(k p) n -> p k n", p=P)
        H = GLA_HEADS
        QC, KC, VC, RC = 0, H * DK, 2 * H * DK, 2 * H * DK + H * DV
        with ExitStack() as ctx:
            def sb(name, shape, dt=F32):
                return ctx.enter_context(nc.sbuf_tensor(name, shape, dt))[:]

            self.split_slots(ctx, "gla", 4)
            T1, T2, T3, Q = (sb(f"gla_{n}", [P, SEQ]) for n in ("t1", "t2", "t3", "q"))
            GLR = sb("gla_glr", [P, SEQ])
            V, R, Y = (sb(f"gla_{n}", [P, MT, DV]) for n in ("v", "r", "y"))
            KDT = sb("gla_kdT", [P, MT, DK])
            yhi, ylo = (sb(f"gla_y_{n}", [P, 2, SEQ], F32R) for n in ("hi", "lo"))
            keep = sb("gla_keep", [P, SEQ], BF16)
            G2 = sb("gla_gate2", [P, DK])
            S = sb("gla_state", [P, 2, DV])
            DEC = sb("gla_dec", [P, NCH])
            so, vo, qo, ro = (sb(f"gla_o_{n}", [P, MT]) for n in ("ss", "ms", "sd", "rs"))
            graw = Y.rearrange("p m v -> p (m v)")[:, 0:UNIT].rearrange("p (k n) -> p k n", k=KT)
            ghi, glo = (y[:, 0, :].rearrange("p (k n) -> p k n", k=KT) for y in (yhi, ylo))

            st = Stream(self.sem, "gla", c, 4, 8, 8)
            norm = Norm(self.sem, "gla_norm", c, V.rearrange("p (b m) v -> p b (m v)", b=2),
                        R[:, 0:4, :].rearrange("p m v -> p (m v)"), Q,
                        lambda m: (self.x_in[m], 16))
            s = {n: self.sem(f"gla_{n}") for n in (
                "graw_in", "g_hi", "g_lo", "glr_mm", "glr", "g2_zero", "g2_in",
                "gate_mm", "absd", "logd", "rel", "decay", "kd", "v_mm", "r_mm", "v", "q", "r", "kdt_mm", "kdt", "st_mm", "s", "o_mm",
                "o_sq", "o_ms", "o_sd", "y", "yt_mm", "y_hi", "y_lo", "down_mm", "down_add")}
            block = ctx.enter_context(nc.Block())
            ends = T3.rearrange("p (c t) -> p c t", t=CHUNK)[:, :, CHUNK - 1]

            def phases(eng, body):
                body(0)
                with eng.Fori(1, H) as h:
                    body(h)

            @block.sync
            def _(sp):
                sp.dma_start(norm.row, a["mix_norm_w"][0].partition_broadcast(P)).then_inc(norm.row_in, 16)
                sp.dma_start(graw, W[:, :, GLA_IN - P:GLA_IN]).then_inc(s["graw_in"], 16)

                def body(h):
                    if isinstance(h, int):
                        sp.wait_ge(s["g2_zero"], 1)
                    wait(sp, s["gate_mm"], h)
                    sp.dma_start(G2[P - RANK:P, :], a["gla_w_gate2"][0][:, ds(h * DK, DK)])\
                        .then_inc(s["g2_in"], 16)
                    st.load(sp, h, 0, W[:, :, ds(h * DK + KC, DK)], KT)
                    for k in range(2):
                        st.load(sp, h, 1 + k, W[:, 4 * k:4 * k + 4, ds(h * DV + VC, DV)], 4)
                    st.load(sp, h, 3, W[:, :, ds(h * DK + QC, DK)], KT)
                    for k in range(2):
                        st.load(sp, h, 4 + k, W[:, 4 * k:4 * k + 4, ds(h * DV + RC, DV)], 4)
                    for k in range(2):
                        st.load(sp, h, 6 + k, WO[:, ds(h * 2 + k, 1), :].rearrange("p k n -> p (k n)"), 0)
                phases(sp, body)

            @block.gpsimd
            def _(pool):
                pool.wait_ge(s["graw_in"], 16)
                pool.tensor_tensor(ghi, graw, c.zero[:, 0:1].unsqueeze(2).broadcast_to([P, KT, P]),
                                   ALU.add).then_inc(s["g_hi"], 1)
                pool.wait_ge(s["g_hi"], 1)
                pool.tensor_tensor(glo, graw, ghi.bitcast(F32), ALU.subtract).then_inc(s["g_lo"], 1)

                def body(h):
                    for pos in range(8):
                        st.divide(pool, h, pos)
                phases(pool, body)

            def rows_tiles(pe, h, pos, pairs, frees, half_mm):
                _, g = st.number(h, pos + 1)
                wait(pe, st.split, g + 1)
                parts = [[x.rearrange("p (k n) -> p k n", k=4) for x in st.slot(h, pos + u)] for u in range(2)]
                for n, (pair, (free, count)) in enumerate(zip(pairs, frees)):
                    wait(pe, free, count)
                    for q in range(4):
                        m = 4 * n + q
                        for k in range(KT):
                            wh, wl = parts[k // 4]
                            rows = slice(m * P, (m + 1) * P)
                            mm = product(pe, pair[:, q * DV:(q + 1) * DV],
                                         (c.hhi[:, k, rows], c.hlo[:, k, rows]),
                                         (wh[:, k % 4, :], wl[:, k % 4, :]), k == 0, k == KT - 1)
                    if n == 0:
                        mm.then_inc(half_mm, 1)
                mm.then_inc(st.used, 2)

            @block.tensor
            def _(pe):
                pe.sem_inc(st.used, 1)
                norm.tensor(pe)
                pe.wait_ge(s["g_lo"], 1)
                for half in range(2):
                    cols = slice(half * HALF, (half + 1) * HALF)
                    for k in range(KT):
                        mm = product(pe, c.MM[:, cols], (ghi[:, k, :], glo[:, k, :]),
                                     (c.hhi[:, k, cols], c.hlo[:, k, cols]), k == 0, k == KT - 1)
                mm.then_inc(s["glr_mm"], 1)
                pe.wait_ge(s["glr"], 1)

                def body(h):
                    pe.wait_ge(s["g2_in"], 16 * h + 16)
                    wait(pe, s["y_lo"], 2 * h)
                    for half in range(2):
                        cols = slice(half * HALF, (half + 1) * HALF)
                        mm = pe.matmul(c.MM[:, cols], G2, GLR[:, cols], start=True, stop=True)
                    mm.then_inc(s["gate_mm"], 1)
                    wait(pe, s["r"], 2 * h - 1)
                    columns_tile(pe, c, st, h, 0, c.PA)
                    rows_tiles(pe, h, 1, (c.PB, c.PA), ((s["r"], 2 * h), (s["kd"], h + 1)), s["v_mm"])
                    pe.wait_ge(s["v"], 2 * h + 1)
                    columns_tile(pe, c, st, h, 3, c.PB)
                    pe.wait_ge(s["kd"], h + 1)
                    for m in range(MT):
                        mm = pe.transpose(c.MM[:, m * P:(m + 1) * P], T1[:, m * P:(m + 1) * P], c.ident)
                    mm.then_inc(s["kdt_mm"], 1)
                    rows_tiles(pe, h, 4, (c.PA, c.PB), ((s["v"], 2 * h + 2), (s["q"], h + 1)), s["r_mm"])
                    pe.wait_ge(s["kdt"], h + 1)
                    pe.wait_ge(s["v"], 2 * h + 2)
                    pe.wait_ge(s["q"], h + 1)

                    def update(n):
                        if n < 2:
                            pe.wait_ge(s["down_add"], h * DOWN + 1)
                        else:
                            pe.wait_ge(s["s"], h * NCH + n - 1)
                        rows = slice(CHUNK * (n % 2), CHUNK * (n % 2) + CHUNK)
                        pe.matmul(c.DD[:, (n % 2) * HALF:(n % 2) * HALF + DV], KDT[rows, n // 2, :],
                                  V[rows, n // 2, :], start=True, stop=True).then_inc(s["st_mm"], 1)

                    def read(n):
                        pe.wait_ge(s["s"], h * NCH + n + 1)
                        m = n // 2
                        if m >= 2:
                            pe.wait_ge(s["y"], h * MT + m - 1)
                        rows = slice(CHUNK * (n % 2), CHUNK * (n % 2) + CHUNK)
                        pe.matmul(c.MM[rows, (m % 2) * HALF:(m % 2) * HALF + DV],
                                  Q[:, n * CHUNK:(n + 1) * CHUNK], S[:, n % 2, :],
                                  start=True, stop=True).then_inc(s["o_mm"], 1)

                    update(0)
                    for n in range(NCH):
                        if n + 1 < NCH:
                            update(n + 1)
                        read(n)
                    pe.wait_ge(s["y"], h * MT + MT)
                    for k in range(2):
                        if k:
                            pe.wait_ge(s["y_lo"], 2 * h + 1)
                        for m in range(MT):
                            mm = pe.transpose(c.MM[:, m * P:(m + 1) * P], Y[:, m, k * P:(k + 1) * P], c.ident)
                        mm.then_inc(s["yt_mm"], 1)
                    pe.wait_ge(s["y_lo"], 2 * h + 2)
                    down_product(pe, c, st, h, (6, 7), [(yhi[:, k, :], ylo[:, k, :]) for k in range(2)],
                                 s["down_mm"], s["down_add"], h)
                phases(pe, body)

            @block.scalar
            def _(act):
                norm.scalar(act)
                act.wait_ge(s["glr_mm"], 1)
                act.copy(GLR, c.MM).then_inc(s["glr"], 1)

                def body(h):
                    bg = c.par[:, ds(h + C_BG, 1)]
                    act.wait_ge(s["gate_mm"], h + 1)
                    act.activation(T1, c.MM, ACT.Abs, bias=bg).then_inc(s["absd"], 1)
                    act.drain()
                    act.activation(T1, T1, ACT.Exp, scale=-1.0)
                    act.drain()
                    act.activation(T1, T1, ACT.Ln, bias=1.0).then_inc(s["logd"], 1)
                    act.wait_ge(s["rel"], h + 1)
                    act.activation(T2, T2, ACT.Exp, scale=1.0 / TAU)
                    act.activation(DEC, ends, ACT.Exp, scale=1.0 / TAU).then_inc(s["decay"], 1)
                    for n in range(2):
                        act.wait_ge(*((s["v_mm"], h + 1) if n == 0 else (st.used, st.done(h, 2))))
                        act.copy(V[:, 4 * n:4 * n + 4, :], (c.PB, c.PA)[n].rearrange("p (m v) -> p m v", v=DV))\
                           .then_inc(s["v"], 1)
                    act.wait_ge(st.used, st.done(h, 3))
                    act.activation(Q, c.PB, ACT.Copy, scale=DK ** -0.5).then_inc(s["q"], 1)
                    for n in range(2):
                        act.wait_ge(*((s["r_mm"], h + 1) if n == 0 else (st.used, st.done(h, 5))))
                        act.activation(R[:, 4 * n:4 * n + 4, :], (c.PA, c.PB)[n].rearrange("p (m v) -> p m v", v=DV),
                                       ACT.Silu).then_inc(s["r"], 1)
                    for m in range(MT):
                        act.wait_ge(s["o_mm"], h * NCH + 2 * m + 2)
                        o = c.MM[:, (m % 2) * HALF:(m % 2) * HALF + DV]
                        act.activation(T3[:, 0:DV], o, ACT.Square, accum_out=so[:, m:m + 1]).then_inc(s["o_sq"], 1)
                        act.wait_ge(s["o_ms"], h * MT + m + 1)
                        act.activation(qo[:, m:m + 1], vo[:, m:m + 1], ACT.Sqrt).then_inc(s["o_sd"], 1)
                    for k in range(2):
                        act.wait_ge(s["yt_mm"], 2 * h + k + 1)
                        act.activation(yhi[:, k, :], c.MM, ACT.Identity, scale=c.par[:, ds(2 * h + (C_GNW + k), 1)])\
                            .then_inc(s["y_hi"], 1)
                phases(act, body)

            @block.vector
            def _(dve):
                dve.memset(G2, 0.0).then_inc(s["g2_zero"], 1)
                dve.memset(keep, 1.0)
                dve.drain()
                dve.memset(keep.rearrange("p (c t) -> p c t", t=CHUNK)[:, :, 0:1], 0.0)
                norm.vector(dve)
                dve.sem_inc(s["down_add"], 1)

                def body(h):
                    bg = c.par[:, ds(h + C_BG, 1)]
                    dve.wait_ge(s["absd"], h + 1)
                    dve.tensor_scalar(T2, c.MM, bg, 0.0, ALU.add, ALU.min)
                    dve.drain()
                    dve.wait_ge(s["logd"], h + 1)
                    dve.tensor_tensor(T2, T2, T1, ALU.subtract)
                    dve.drain()
                    dve.tensor_tensor_scan(T3, keep, T2, 0.0, ALU.mult, ALU.add)
                    dve.drain()
                    chunks = [x.rearrange("p (c t) -> p c t", t=CHUNK) for x in (T2, T3)]
                    dve.tensor_tensor(chunks[0], ends.unsqueeze(2).broadcast_to([P, NCH, CHUNK]), chunks[1],
                                      ALU.subtract).then_inc(s["rel"], 1)
                    dve.wait_ge(s["decay"], h + 1)
                    dve.wait_ge(st.used, st.done(h, 0))
                    dve.tensor_tensor(T1, c.PA, T2, ALU.mult).then_inc(s["kd"], 1)
                    dve.wait_ge(s["kdt_mm"], h + 1)
                    dve.tensor_copy(KDT.rearrange("p m k -> p (m k)"), c.MM).then_inc(s["kdt"], 1)
                    for n in range(NCH + 3):
                        if n < NCH:
                            dve.wait_ge(s["st_mm"], h * NCH + n + 1)
                            wait(dve, s["o_mm"], h * NCH + n - 1)
                            ps = c.DD[:, (n % 2) * HALF:(n % 2) * HALF + DV]
                            if n == 0:
                                dve.tensor_copy(S[:, 0, :], ps).then_inc(s["s"], 1)
                            else:
                                dve.wait_ge(s["s"], h * NCH + n)
                                dve.scalar_tensor_tensor(out=S[:, n % 2, :], in0=S[:, (n - 1) % 2, :],
                                                         scalar=DEC[:, n:n + 1], in1=ps, op0=ALU.mult,
                                                         op1=ALU.add).then_inc(s["s"], 1)
                        if n % 2 == 1 and n >= 3:
                            m = (n - 3) // 2
                            dve.wait_ge(s["o_sq"], h * MT + m + 1)
                            dve.tensor_scalar(vo[:, m:m + 1], so[:, m:m + 1], 1.0 / DV, EPS, ALU.mult,
                                              ALU.add).then_inc(s["o_ms"], 1)
                        if n % 2 == 0 and n >= 4:
                            m = (n - 4) // 2
                            dve.wait_ge(s["r"], 2 * h + 1 + m // 4)
                            dve.wait_ge(s["o_sd"], h * MT + m + 1)
                            dve.reciprocal(ro[:, m:m + 1], qo[:, m:m + 1])
                            dve.drain()
                            o = c.MM[:, (m % 2) * HALF:(m % 2) * HALF + DV]
                            dve.scalar_tensor_tensor(out=Y[:, m, :], in0=o, scalar=ro[:, m:m + 1],
                                                     in1=R[:, m, :], op0=ALU.mult, op1=ALU.mult)\
                               .then_inc(s["y"], 1)
                    for k in range(2):
                        dve.wait_ge(s["y_hi"], 2 * h + k + 1)
                        dve.scalar_tensor_tensor(out=ylo[:, k, :], in0=c.MM,
                                                 scalar=c.par[:, ds(2 * h + (C_GNW + k), 1)],
                                                 in1=yhi[:, k, :].bitcast(F32), op0=ALU.mult,
                                                 op1=ALU.subtract).then_inc(s["y_lo"], 1)
                    add_down(dve, c, st, s["down_mm"], s["down_add"], h, 7, h)
                phases(dve, body)

    def ffn(self, name, W_up, W_down, row, chunks, gated):
        nc, c = self.nc, self.core
        WU = W_up.rearrange("(k p) n -> p k n", p=P)
        WD = W_down.rearrange("(k p) n -> p k n", p=P)
        n_up = 4 if gated else 2
        slots = 3 if gated else 4
        with ExitStack() as ctx:
            def sb(n, shape, dt=F32):
                return ctx.enter_context(nc.sbuf_tensor(f"{name}_{n}", shape, dt))[:]

            self.split_slots(ctx, name, slots)
            xn = sb("xn", [P, 2, D])
            rowt = sb("row", [P, D])
            UG, UV = sb("u_gate", [P, SEQ]), sb("u_val", [P, SEQ])
            A = sb("a", [P, 2, SEQ])
            ahi, alo = sb("a_hi", [P, 2, SEQ], F32R), sb("a_lo", [P, 2, SEQ], F32R)
            st = Stream(self.sem, name, c, slots, n_up, n_up + 2)
            norm = Norm(self.sem, f"{name}_norm", c, xn, UG, rowt)
            s = {n: self.sem(f"{name}_{n}") for n in (
                "base", "conv", "silu", "prod", "a_hi", "a_lo",
                "down_mm", "down_add")}
            read = s["conv"] if gated else s["base"]
            pair = (c.PA, c.PB)
            block = ctx.enter_context(nc.Block())

            def phases(eng, up, down):
                up(0)
                with eng.Fori(1, chunks) as i:
                    up(i)
                    down(i)
                down(chunks)

            @block.sync
            def _(sp):
                sp.dma_start(rowt, row.partition_broadcast(P)).then_inc(norm.row_in, 16)

                def up(i):
                    for t in range(n_up):
                        off = (t // 2) * P + (t % 2) * FFN_DIM if gated else t * P
                        st.load(sp, i, t, WU[:, :, ds(i * (2 * P) + off, P)], KT)

                def down(i):
                    base = n_up if not (isinstance(i, int) and i == chunks) else 0
                    for k in range(2):
                        st.load(sp, i, base + k, WD[:, ds((i - 1) * 2 + k, 1), :].rearrange("p k n -> p (k n)"), 0)
                phases(sp, up, down)

            @block.gpsimd
            def _(pool):
                def up(i):
                    for t in range(n_up):
                        st.divide(pool, i, t)

                def down(i):
                    base = n_up if not (isinstance(i, int) and i == chunks) else 0
                    for k in range(2):
                        st.divide(pool, i, base + k)
                phases(pool, up, down)

            @block.tensor
            def _(pe):
                pe.sem_inc(st.used, 1)
                norm.tensor(pe)

                def up(i):
                    for t in range(n_up):
                        wait(pe, read, i * n_up + t - 1)
                        columns_tile(pe, c, st, i, t, pair[t % 2])

                def down(i):
                    base = n_up if not (isinstance(i, int) and i == chunks) else 0
                    pe.wait_ge(s["a_lo"], i * 2)
                    down_product(pe, c, st, i, (base, base + 1),
                                 [(ahi[:, k, :], alo[:, k, :]) for k in range(2)],
                                 s["down_mm"], s["down_add"], i - 1, 4)
                phases(pe, up, down)

            @block.scalar
            def _(act):
                norm.scalar(act)

                def up(i):
                    for t in range(n_up):
                        act.wait_ge(st.used, st.done(i, t))
                        if gated:
                            f = (t // 2) + (t % 2) * FT
                            U = UV if t % 2 else UG
                            wait(act, s["prod"], 2 * i + t // 2)
                            act.activation(U, pair[t % 2], ACT.Identity, bias=c.par[:, ds(2 * i + (C_FCB + f), 1)],
                                           scale=c.par[:, ds(2 * i + (C_FCW + 4 * FT + f), 1)]).then_inc(s["base"], 1)
                            if t % 2 == 0:
                                act.wait_ge(s["conv"], 4 * i + t + 1)
                                act.activation(UG, UG, ACT.Silu).then_inc(s["silu"], 1)
                        else:
                            wait(act, s["prod"], 2 * i + t - 1)
                            act.activation((UG, UV)[t], pair[t], ACT.Relu).then_inc(s["base"], 1)
                    for k in range(2):
                        act.wait_ge(s["prod"], 2 * i + k + 1)
                        if not (isinstance(i, int) and i == 0):
                            act.wait_ge(st.used, st.done(i, n_up + 1))
                        act.copy(ahi[:, k, :], A[:, k, :]).then_inc(s["a_hi"], 1)
                phases(act, up, lambda i: None)

            @block.vector
            def _(dve):
                norm.vector(dve)
                dve.sem_inc(s["down_add"], 1)

                def low(i):
                    for k in range(2):
                        dve.wait_ge(s["a_hi"], 2 * i + k + 1)
                        dve.tensor_tensor(alo[:, k, :], A[:, k, :], ahi[:, k, :].bitcast(F32),
                                          ALU.subtract).then_inc(s["a_lo"], 1)

                def up(i):
                    for t in range(n_up):
                        dve.wait_ge(s["base"], i * n_up + t + 1)
                        if gated:
                            f = (t // 2) + (t % 2) * FT
                            U = UV if t % 2 else UG
                            for tap in (1, 0):
                                lag = 2 - tap
                                dve.scalar_tensor_tensor(
                                    out=U[:, lag:SEQ], in0=pair[t % 2][:, 0:SEQ - lag],
                                    scalar=c.par[:, ds(2 * i + (C_FCW + tap * 2 * FT + f), 1)],
                                    in1=U[:, lag:SEQ], op0=ALU.mult, op1=ALU.add)
                                if tap:
                                    dve.drain()
                            dve.drain().then_inc(s["conv"], 1)
                            if t % 2:
                                dve.wait_ge(s["silu"], 2 * i + t // 2 + 1)
                                if not isinstance(i, int):
                                    dve.wait_ge(s["a_lo"], 2 * i)
                                dve.tensor_tensor(A[:, t // 2, :], UG, UV, ALU.mult).then_inc(s["prod"], 1)
                        else:
                            U = (UG, UV)[t]
                            if not isinstance(i, int):
                                dve.wait_ge(s["a_lo"], 2 * i)
                            dve.tensor_tensor(A[:, t, :], U, U, ALU.mult).then_inc(s["prod"], 1)

                def down(i):
                    base = n_up if not (isinstance(i, int) and i == chunks) else 0
                    add_down(dve, c, st, s["down_mm"], s["down_add"], i, base + 1, i - 1, 4)

                up(0)
                low(0)
                with dve.Fori(1, chunks) as i:
                    up(i)
                    down(i)
                    low(i)
                down(chunks)

    def hybrid(self):
        nc, c, a = self.nc, self.core, self.a
        W = a["w_in_2"][0].rearrange("(k p) n -> p k n", p=P)
        WO = a["w_out_2"][0].rearrange("(k p) n -> p k n", p=P)
        WR = a["w_r_2"][0].rearrange("n (j p) k -> p n j k", p=P)
        WI = a["w_i_2"][0].rearrange("n (j p) k -> p n j k", p=P)
        XA_, GA_, Q_, F_, V_, G_, MA_, MB_ = (n * D for n in range(8))
        POS = {n: k for k, n in enumerate((
            "xa0", "xa1", "q0", "f0", "dn1", "v0", "v1", "ga0", "ma0", "g0", "mb0",
            "q1", "f1", "dn0", "ga1", "ma1", "g1", "mb1"))}
        PAIRS = HG_HEADS // 2

        def at(i, name):
            if isinstance(i, int):
                if i == 0 and POS[name] > POS["dn1"]:
                    return POS[name] - 1
                if i == PAIRS:
                    return 0
            return POS[name]

        TAIL = ("xa0.0 O1/1 xa0.1 xa0 O2/1 xa1.0 O3/1 xa1.1 xa1 SQ/1 q0.0 OT/1 q0.1 q0 Y/1 f0.0 f0.1 f0 "
                "dn1.0 D/0 dn1.1 dn1")
        ORDER = (TAIL + " v.0 L0/0 v.1 v0 L1/0 v.2 L2/0 v.3 v1 L3/0 r0 L4/0 i0 L5/0 lruA0 ga0.0 L6/0 ga0.1 ga0 KT/0 "
                 "lruB0 ma0.0 O0/0 ma0.1 ma0 O1/0 lruC0 gh0 r1 O2/0 i1 O3/0 lruA1 g0.0 SQ/0 g0.1 g0 lruB1 OT/0 mb0.0 mb0.1 "
                 "mb0 gb0 Y/0 q1.0 lruC1 q1.1 q1 f1.0 f1.1 f1 dn0.0 D/1 dn0.1 dn0 ga1.0 L0/1 ga1.1 ga1 L1/1 "
                 "ma1.0 L2/1 ma1.1 ma1 gh1 L3/1 g1.0 L4/1 g1.1 g1 L5/1 mb1.0 L6/1 mb1.1 mb1 gb1 KT/1 O0/1").split()
        OF_LAST = {x for x in TAIL.split() if x.endswith("/1") or x.startswith("dn1")}
        OF_LAST.discard("D/0")

        def steps(i, run):
            for x in ORDER:
                if x in OF_LAST and ORDER.index(x) < len(TAIL.split()):
                    if not (isinstance(i, int) and i == 0):
                        run(x, i - 1)
                elif not (isinstance(i, int) and i == PAIRS):
                    run(x, i)

        with ExitStack() as ctx:
            def sb(name, shape, dt=F32):
                return ctx.enter_context(nc.sbuf_tensor(f"hy_{name}", shape, dt))[:]

            self.split_slots(ctx, "hy", 3)
            XA = sb("xa", [P, 2, SEQ])
            GM, Q, F, K, GB, TM = (sb(n, [P, SEQ]) for n in ("gm", "q", "f", "k", "gb", "tm"))
            V = sb("v", [P, MT, 2 * HG_DV])
            T1, T2, T3, T4 = (sb(n, [P, SEQ]) for n in ("t1", "t2", "t3", "t4"))
            TOT, SC = sb("totals", [P, SEQ]), sb("scores", [P, SEQ])
            KTT, ON = K, F
            yhi, ylo = sb("y_hi", [P, SEQ], F32R), sb("y_lo", [P, SEQ], F32R)
            WRI = sb("w_ri", [P, 2, 2, 2 * P])
            S = sb("state", [P, 2, HG_DV])
            oss, oms, osd, ors = (sb(n, [P, MT]) for n in ("o_ss", "o_ms", "o_sd", "o_rs"))
            st = Stream(self.sem, "hy", c, 3, 17, 18)
            fin = RowNorm(self.sem, "hy_fin", c, K, GM)
            xn = V.rearrange("p (b m) v -> p b (m v)", b=2)
            norm = Norm(self.sem, "hy_norm", c, xn, F, Q, lambda m: (fin.scaled, m + 1))
            s = {n: self.sem(f"hy_{n}") for n in (
                "wri_in", "xa_base", "conv", "q", "f", "kf", "v_mm", "v", "gates_mm", "r", "i",
                "lru_a", "lru_m", "lru_sd", "lru_u", "h", "ga", "ma", "gh", "g", "mb", "gb", "diag_mm", "sc0",
                "qp", "lev_mm", "lev", "pc", "kt_mm", "kt", "kv_mm", "s", "o_mm", "o_sq", "o_ms",
                "o_sd", "on", "ot_mm", "y", "y_hi", "y_lo", "down_mm", "down_add")}
            TOT_AT = [None, 0, 512, 768, 896, 960, 992, 1008]
            block = ctx.enter_context(nc.Block())

            def phases(run):
                def of(eng):
                    steps(0, lambda x, i: run(x, i, 0))
                    with eng.Fori(1, PAIRS) as n:
                        steps(n, lambda x, i: run(x, i, n))
                    steps(PAIRS, lambda x, i: run(x, i, PAIRS))
                return of

            def tiles(x):
                return x.rearrange("p (m n) -> p m n", n=P)

            def halves(x, n, tiled=False):
                if tiled:
                    return x.rearrange("p (m b h n) -> p m b h n", m=MT, h=2, n=n)
                return x.rearrange("p (b h n) -> p b h n", h=2, n=n)

            TILES = {
                "xa0": (c.PA, "g", 2, 0), "xa1": (c.PB, "mb", 2, 0),
                "q0": (c.PA, "conv", 2, 1), "f0": (c.PB, "conv", 2, 2),
                "v0": (c.PA, "q", 2, 1), "v1": (c.PB, "f", 2, 1),
                "r0": (c.PA, "v", 2, 1), "i0": (c.PB, "v", 2, 2),
                "ga0": (c.PA, "r", 2, 1), "ma0": (c.PB, "i", 2, 1),
                "r1": (c.PA, "ga", 2, 1), "i1": (c.PB, "ma", 2, 1),
                "g0": (c.PA, "r", 2, 2), "mb0": (c.PB, "i", 2, 2),
                "q1": (c.PA, "g", 2, 1), "f1": (c.PB, "mb", 2, 1),
                "ga1": (c.PA, "q", 2, 2), "ma1": (c.PB, "f", 2, 2),
                "g1": (c.PA, "ga", 2, 2), "mb1": (c.PB, "ma", 2, 2),
            }
            COLS = {"xa": XA_, "q": Q_, "f": F_, "ga": GA_, "ma": MA_, "g": G_, "mb": MB_}
            TOT7 = TOT[:, TOT_AT[LEVELS]:TOT_AT[LEVELS] + MT]

            @block.sync
            def _(sp):
                sp.dma_start(fin.row, a["final_norm_w"].partition_broadcast(P)).then_inc(fin.row_in, 16)
                sp.dma_start(norm.row, a["norm_mix_2"][0].partition_broadcast(P)).then_inc(norm.row_in, 16)

                def run(x, i, n):
                    if x[:-1] in COLS:
                        st.load(sp, n, at(n, x), W[:, :, ds(i * (2 * P) + (COLS[x[:-1]] + int(x[-1]) * P), P)], KT)
                    elif x in ("dn0", "dn1"):
                        st.load(sp, n, at(n, x), WO[:, ds(2 * i + int(x[-1]), 1), :].rearrange("p k n -> p (k n)"), 0)
                    elif x in ("v0", "v1"):
                        u = int(x[-1])
                        st.load(sp, n, at(n, x), W[:, 4 * u:4 * u + 4, ds(i * (2 * P) + V_, 2 * P)], 4)
                        if u == 0:
                            wait(sp, s["gates_mm"], 4 * i)
                            for w, src in enumerate((WR, WI)):
                                sp.dma_start(WRI[:, w, :, :], src[:, ds(i, 1), :, :].rearrange("p n j k -> p (n j) k"))\
                                  .then_inc(s["wri_in"], 16)
                phases(run)(sp)

            @block.gpsimd
            def _(pool):
                def run(x, i, n):
                    if x in POS:
                        st.divide(pool, n, at(n, x))
                phases(run)(pool)

            @block.tensor
            def _(pe):
                pe.sem_inc(st.used, 1)
                norm.tensor(pe)
                KT_, QT, MT_ = tiles(K), tiles(Q), tiles(c.MM)

                def gate(which, j, pair):
                    for half in range(2):
                        cols = slice(half * HALF, (half + 1) * HALF)
                        for jj in range(2):
                            mm = pe.matmul(pair[:, cols], WRI[:, which, jj, j * P:(j + 1) * P],
                                           XA[:, jj, cols], start=(jj == 0), stop=(jj == 1))
                    mm.then_inc(s["gates_mm"], 1)

                def free(name, i):
                    _, by, per, before = TILES[name]
                    wait(pe, s[by], per * i + before)

                def down_half(i, n, j, half):
                    hd = 2 * i + j
                    pos = at(n, f"dn{j}")
                    if half == 0:
                        pe.wait_ge(s["y_lo"], hd + 1)
                        pe.wait_ge(st.split, st.ready(n, pos))
                    for k in range(DOWN // 2 * half, DOWN // 2 * (half + 1)):
                        pe.wait_ge(s["down_add"], hd * DOWN + max(k, 1))
                        mm = down_tile(pe, c, k // 2, k % 2, [(yhi, ylo)], [st.slot(n, pos)], down_bank(c, k, 2))
                        mm.then_inc(*((s["down_mm"], 1) if k < DOWN - 1 else (st.used, 1)))

                def scores(hd, l):
                    if l == 0:
                        pe.wait_ge(s["qp"], hd + 1)
                    else:
                        pe.wait_ge(s["lev"], hd * LEVELS + l)
                        if l > 1:
                            pe.wait_ge(s["pc"], hd * LEVELS + l - 1)
                        else:
                            pe.wait_ge(s["sc0"], hd + 1)
                    bank = c.MM[:, (l % 2) * HALF:(l % 2 + 1) * HALF]
                    right = halves(Q, 1 << l, True)
                    for m in range(MT):
                        mm = pe.matmul(bank[:, m * (P // 2):(m + 1) * (P // 2)].rearrange(
                            "p (b n) -> p b n", n=1 << l), KT_[:, m, :], right[:, m, :, 1, :],
                            start=True, stop=True)
                    mm.then_inc(s["lev_mm"], 1)

                def outputs(i, j, q):
                    hd = 2 * i + j
                    VT = V[:, :, j * HG_DV:(j + 1) * HG_DV]
                    if q == 0:
                        pe.wait_ge(s["kt"], hd + 1)
                        pe.wait_ge(s["v"], 2 * i + 2)
                        pe.wait_ge(s["down_add"], hd * DOWN + 1)
                    for m in (2 * q, 2 * q + 1):
                        if m < MT - 1:
                            if m >= 2:
                                pe.wait_ge(s["s"], hd * (MT - 1) + m - 1)
                            pe.matmul(c.DD[:, (m % 2) * HALF:(m % 2) * HALF + HG_DV],
                                      tiles(KTT)[:, m, :], VT[:, m, :], start=True, stop=True)\
                                .then_inc(s["kv_mm"], 1)
                    for m in (2 * q, 2 * q + 1):
                        mm = pe.matmul(MT_[:, m, :], tiles(SC)[:, m, :], VT[:, m, :], start=True, stop=(m == 0))
                        if m:
                            pe.wait_ge(s["s"], hd * (MT - 1) + m)
                            mm = pe.matmul(MT_[:, m, :], QT[:, m, :], S[:, (m - 1) % 2, :],
                                           start=False, stop=True)
                        mm.then_inc(s["o_mm"], 1)

                def run(x, i, n):
                    name, _, half = x.partition(".")
                    if name in TILES and half:
                        if half == "0":
                            free(name, i)
                        columns_half(pe, c, st, n, at(n, name), TILES[name][0], int(half))
                    elif name == "v" and half:
                        q = int(half)
                        if q == 0:
                            pe.wait_ge(st.split, st.ready(n, at(n, "v1")))
                        if q % 2 == 0:
                            free(f"v{q // 2}", i)
                        for m in (2 * q, 2 * q + 1):
                            mm = rows_group(pe, c, row_parts(st, n, at(n, "v0")), (c.PA, c.PB)[q // 2], m, q // 2 * 4)
                        if q == 1:
                            mm.then_inc(s["v_mm"], 1)
                        if q == 3:
                            mm.then_inc(st.used, 2)
                    elif x in ("r0", "i0", "r1", "i1"):
                        if x == "r0":
                            pe.wait_ge(s["wri_in"], i * 32 + 32)
                            pe.wait_ge(s["conv"], 2 * i + 2)
                        free(x, i)
                        gate("ri".index(x[0]), int(x[1]), TILES[x][0])
                    elif name in ("dn0", "dn1") and half:
                        down_half(i, n, int(name[-1]), int(half))
                    elif "/" in x:
                        what, j = x.split("/")
                        hd = 2 * i + int(j)
                        if what == "D":
                            pe.wait_ge(s["kf"], hd + 1)
                            pe.wait_ge(s["q"], hd + 1)
                            wait(pe, s["y"], hd)
                            for m in range(MT):
                                mm = pe.matmul(MT_[:, m, :], KT_[:, m, :], QT[:, m, :], start=True, stop=True)
                            mm.then_inc(s["diag_mm"], 1)
                        elif what[0] == "L":
                            scores(hd, int(what[1:]))
                        elif what == "KT":
                            pe.wait_ge(s["lev"], (hd + 1) * LEVELS)
                            pe.wait_ge(s["pc"], (hd + 1) * LEVELS)
                            for m in range(MT):
                                mm = pe.transpose(MT_[:, m, :], KT_[:, m, :], c.ident)
                            mm.then_inc(s["kt_mm"], 1)
                        elif what == "OT":
                            pe.wait_ge(s["on"], hd + 1)
                            for m in range(MT):
                                mm = pe.transpose(MT_[:, m, :], tiles(ON)[:, m, :], c.ident)
                            mm.then_inc(s["ot_mm"], 1)
                        elif what[0] == "O":
                            outputs(i, int(j), int(what[1:]))
                phases(run)(pe)

            @block.scalar
            def _(act):
                fin.scalar(act)
                norm.scalar(act)

                def run(x, i, n):
                    kind, j = x[:-1], (int(x[-1]) if x[-1].isdigit() else 0)
                    hd = 2 * i + j

                    def par(col):
                        return c.par[:, ds(2 * i + (col + j), 1)]

                    if "." in x:
                        return
                    pair = TILES[x][0] if x in TILES else None
                    if x in POS:
                        if x != "v0":
                            if x not in ("dn0", "dn1"):
                                act.wait_ge(st.used, st.done(n, at(n, x)))
                    if kind == "xa":
                        wait(act, s["lru_u"], 2 * i)
                        act.activation(XA[:, j, :], pair, ACT.Identity, bias=par(C_CB), scale=par(C_CW + 24))\
                           .then_inc(s["xa_base"], 1)
                    elif kind == "q":
                        wait(act, s["o_mm"], hd * MT)
                        act.activation(Q, pair, ACT.Silu).then_inc(s["q"], 1)
                    elif kind == "f":
                        wait(act, s["ot_mm"], hd)
                        act.activation(F, pair, ACT.Sigmoid)
                        act.activation(K, pair, ACT.Sigmoid, scale=-1.0).then_inc(s["f"], 1)
                    elif kind == "v":
                        if j == 0:
                            act.wait_ge(s["v_mm"], i + 1)
                        act.copy(V[:, 4 * j:4 * j + 4, :], pair.rearrange("p (m v) -> p m v", v=2 * HG_DV))\
                           .then_inc(s["v"], 1)
                    elif kind == "r":
                        act.wait_ge(s["gates_mm"], 4 * i + 2 * j + 1)
                        wait(act, s["h"], hd)
                        act.activation(T1, pair, ACT.Sigmoid, bias=par(C_BR)).then_inc(s["r"], 1)
                    elif kind == "i":
                        act.wait_ge(s["gates_mm"], 4 * i + 2 * j + 2)
                        act.activation(T2, pair, ACT.Sigmoid, bias=par(C_BI)).then_inc(s["i"], 1)
                    elif kind == "lruA":
                        act.drain()
                        wait(act, s["gh"], hd)
                        act.activation(T3, T1, ACT.Tanh, scale=c.decay[:, 1, ds(2 * i + j, 1)])
                        act.drain()
                        act.activation(T1, T1, ACT.Exp, scale=c.decay[:, 0, ds(2 * i + j, 1)])\
                            .then_inc(s["lru_a"], 1)
                    elif kind == "lruB":
                        act.wait_ge(s["lru_m"], hd + 1)
                        act.activation(T3, T3, ACT.Sqrt).then_inc(s["lru_sd"], 1)
                    elif kind == "ga":
                        wait(act, s["y"], hd)
                        act.activation(GM, pair, ACT.Gelu_apprx_tanh).then_inc(s["ga"], 1)
                    elif kind == "ma":
                        wait(act, s["gb"], hd)
                        act.activation(TM, pair, ACT.Sigmoid).then_inc(s["ma"], 1)
                    elif kind == "g":
                        wait(act, s["y"], hd)
                        act.activation(GB, pair, ACT.Silu).then_inc(s["g"], 1)
                    elif kind == "mb":
                        act.wait_ge(s["gh"], hd + 1)
                        act.activation(TM, pair, ACT.Sigmoid).then_inc(s["mb"], 1)
                    elif kind == "SQ/":
                        act.wait_ge(s["o_mm"], (hd + 1) * MT)
                        act.activation(SC, c.MM, ACT.Square).then_inc(s["o_sq"], 1)
                        act.wait_ge(s["o_ms"], hd + 1)
                        act.activation(osd, oms, ACT.Sqrt).then_inc(s["o_sd"], 1)
                    elif kind == "Y/":
                        act.wait_ge(s["y"], hd + 1)
                        act.copy(yhi, SC).then_inc(s["y_hi"], 1)
                phases(run)(act)

            @block.vector
            def _(dve):
                fin.vector(dve)
                norm.vector(dve)
                dve.sem_inc(s["down_add"], 1)

                def run(x, i, n):
                    name, _, half = x.partition(".")
                    kind, j = x[:-1], (int(x[-1]) if x[-1].isdigit() else 0)
                    hd = 2 * i + j

                    def par(col):
                        return c.par[:, ds(2 * i + (col + j), 1)]

                    if name in ("dn0", "dn1") and half:
                        j = int(name[-1])
                        hd = 2 * i + j
                        for k in range(DOWN // 2 * int(half), DOWN // 2 * (int(half) + 1)):
                            if k < DOWN - 1:
                                dve.wait_ge(s["down_mm"], hd * (DOWN - 1) + k + 1)
                            else:
                                dve.wait_ge(st.used, st.done(n, at(n, name)))
                            cols = slice(k % 2 * HALF, (k % 2 + 1) * HALF)
                            dve.tensor_tensor(c.X[:, k // 2, cols], c.X[:, k // 2, cols], down_bank(c, k, 2),
                                              ALU.add).then_inc(s["down_add"], 1)
                    elif half:
                        return
                    elif kind == "xa":
                        dve.wait_ge(s["xa_base"], hd + 1)
                        for tap in (2, 1, 0):
                            lag = 3 - tap
                            mm = dve.scalar_tensor_tensor(
                                out=XA[:, j, lag:SEQ], in0=TILES[x][0][:, 0:SEQ - lag], scalar=par(C_CW + 8 * tap),
                                in1=XA[:, j, lag:SEQ], op0=ALU.mult, op1=ALU.add)
                            if tap:
                                dve.drain()
                        mm.then_inc(s["conv"], 1)
                    elif kind == "f":
                        lb, rest = (c.lb[:, q, ds(2 * i + j, 1)] for q in range(2))
                        dve.wait_ge(s["f"], hd + 1)
                        dve.tensor_scalar(F, F, rest, lb, ALU.mult, ALU.add)
                        dve.tensor_scalar(K, K, rest, None, ALU.mult)
                        dve.drain()
                        dve.tensor_scalar(F, F, F_MIN, None, ALU.max).then_inc(s["kf"], 1)
                    elif kind == "lruA":
                        dve.wait_ge(s["lru_a"], hd + 1)
                        dve.tensor_tensor(T4, T1, T1, ALU.mult)
                        dve.drain()
                        dve.scalar_tensor_tensor(out=T3, in0=T4, scalar=1.0, in1=T3, op0=ALU.add, op1=ALU.mult)
                        dve.drain()
                        dve.tensor_scalar(T3, T3, 0.0, None, ALU.max).then_inc(s["lru_m"], 1)
                        dve.wait_ge(s["i"], hd + 1)
                        dve.tensor_tensor(T2, T2, XA[:, j, :], ALU.mult).then_inc(s["lru_u"], 1)
                    elif kind == "lruC":
                        dve.wait_ge(s["lru_u"], hd + 1)
                        dve.wait_ge(s["lru_sd"], hd + 1)
                        dve.tensor_tensor(T2, T2, T3, ALU.mult)
                        dve.drain()
                        dve.tensor_tensor_scan(T3, T1, T2, 0.0, ALU.mult, ALU.add).then_inc(s["h"], 1)
                    elif kind == "gh":
                        dve.wait_ge(s["ma"], hd + 1)
                        dve.tensor_tensor(GM, GM, TM, ALU.mult)
                        dve.drain()
                        dve.wait_ge(s["h"], hd + 1)
                        dve.tensor_tensor(GM, GM, T3, ALU.mult).then_inc(s["gh"], 1)
                    elif kind == "gb":
                        dve.wait_ge(s["mb"], hd + 1)
                        dve.scalar_tensor_tensor(out=GB, in0=GB, scalar=c.par[:, C_HGN:C_HGN + 1], in1=TM,
                                                 op0=ALU.mult, op1=ALU.mult).then_inc(s["gb"], 1)
                    elif kind == "D/":
                        dve.wait_ge(s["diag_mm"], hd + 1)
                        dve.tensor_tensor(tiles(SC), tiles(c.MM), c.ident.unsqueeze(1).broadcast_to([P, MT, P]),
                                          ALU.mult).then_inc(s["sc0"], 1)
                        dve.tensor_tensor(Q, Q, F, ALU.mult).then_inc(s["qp"], 1)
                    elif kind[0] == "L":
                        level(hd, int(kind[1:-1]))
                    elif kind == "KT/":
                        dve.wait_ge(s["kt_mm"], hd + 1)
                        dve.tensor_copy(KTT, c.MM).then_inc(s["kt"], 1)
                    elif kind == "OT/":
                        return
                    elif kind[0] == "O":
                        for m in (2 * int(kind[1:-1]), 2 * int(kind[1:-1]) + 1):
                            if m < MT - 1:
                                state(hd, m)
                    elif kind == "SQ/":
                        dve.wait_ge(s["o_sq"], hd + 1)
                        dve.tensor_reduce(oss, tiles(SC), AX, ALU.add)
                        dve.drain()
                        dve.tensor_scalar(oms, oss, 1.0 / HG_DV, EPS, ALU.mult, ALU.add).then_inc(s["o_ms"], 1)
                        dve.wait_ge(s["o_sd"], hd + 1)
                        dve.reciprocal(ors, osd)
                        dve.drain()
                        dve.tensor_tensor(tiles(ON), tiles(c.MM), ors.unsqueeze(2).broadcast_to([P, MT, HG_DV]),
                                          ALU.mult).then_inc(s["on"], 1)
                    elif kind == "Y/":
                        dve.drain()
                        dve.wait_ge(s["ot_mm"], hd + 1)
                        dve.tensor_tensor(SC, c.MM, GB, ALU.mult)
                        dve.drain()
                        dve.tensor_tensor(SC, SC, GM, ALU.add).then_inc(s["y"], 1)
                        dve.wait_ge(s["y_hi"], hd + 1)
                        dve.tensor_tensor(ylo, SC, yhi.bitcast(F32), ALU.subtract).then_inc(s["y_lo"], 1)

                def level(hd, l):
                    nb, w = SEQ // (2 << l), 1 << l
                    tot = F if l == 0 else TOT[:, TOT_AT[l]:TOT_AT[l] + 2 * nb]
                    left, right = (tot.rearrange("p (b h) -> p b h", h=2)[:, :, q] for q in range(2))
                    dve.drain()
                    dve.wait_ge(s["lev_mm"], hd * LEVELS + l + 1)
                    dve.tensor_tensor(halves(Q, w)[:, :, 1, :], halves(Q, w)[:, :, 1, :],
                                      left.unsqueeze(2).broadcast_to([P, nb, w]), ALU.mult)
                    dve.tensor_tensor(halves(K, w)[:, :, 0, :], halves(K, w)[:, :, 0, :],
                                      right.unsqueeze(2).broadcast_to([P, nb, w]), ALU.mult)
                    dve.tensor_tensor(TOT[:, TOT_AT[l + 1]:TOT_AT[l + 1] + nb], left, right, ALU.mult)\
                       .then_inc(s["lev"], 1)
                    bank = c.MM[:, (l % 2) * HALF:(l % 2 + 1) * HALF]
                    dve.copy_predicated(
                        halves(SC, w, True)[:, :, :, 1, :],
                        c.masks[:, l, :].rearrange("p (b n) -> p b n", n=w).unsqueeze(1).broadcast_to(
                            [P, MT, P // (2 * w), w]),
                        bank.rearrange("p (m b n) -> p m b n", m=MT, n=w)).then_inc(s["pc"], 1)

                def state(hd, m):
                    dve.wait_ge(s["kv_mm"], hd * (MT - 1) + m + 1)
                    wait(dve, s["o_mm"], hd * MT + m)
                    ps = c.DD[:, (m % 2) * HALF:(m % 2) * HALF + HG_DV]
                    if m == 0:
                        dve.tensor_copy(S[:, 0, :], ps).then_inc(s["s"], 1)
                    else:
                        dve.wait_ge(s["s"], hd * (MT - 1) + m)
                        dve.scalar_tensor_tensor(out=S[:, m % 2, :], in0=S[:, (m - 1) % 2, :],
                                                 scalar=TOT7[:, m:m + 1], in1=ps, op0=ALU.mult,
                                                 op1=ALU.add).then_inc(s["s"], 1)
                phases(run)(dve)

    def finish(self):
        nc, c, a = self.nc, self.core, self.a
        with ExitStack() as ctx:
            junk = ctx.enter_context(nc.sbuf_tensor("out_junk", [P, D], F32))[:]
            row = ctx.enter_context(nc.sbuf_tensor("out_row", [P, D], F32))[:]
            norm = RowNorm(self.sem, "out", c, junk, row)
            stored = self.sem("stored")
            block = ctx.enter_context(nc.Block())

            @block.sync
            def _(sp):
                sp.dma_start(row, a["norm_final_2"].partition_broadcast(P)).then_inc(norm.row_in, 16)
                for m in range(MT):
                    sp.wait_ge(norm.scaled, m + 1)
                    sp.dma_start(a["out"][0, m * P:(m + 1) * P, :], c.X[:, m, :]).then_inc(stored, 16)
                sp.wait_ge(stored, 16 * MT)

            @block.scalar
            def _(act):
                norm.scalar(act)

            @block.vector
            def _(dve):
                norm.vector(dve)


def build(nc, a):
    with ExitStack() as ctx:
        p = Program(nc, ctx, a)
        p.parameters()
        p.end_stage()
        p.gla()
        p.end_stage()
        p.ffn("f1", a["ffn_w_up"][0], a["ffn_w_down"][0], a["ffn_norm_w"][0], FT // 2, True)
        p.end_stage()
        p.hybrid()
        p.end_stage()
        p.ffn("f2", a["w_up_2"][0], a["w_down_2"][0], a["norm_mlp_2"][0], D_FF // (2 * P), False)
        p.end_stage()
        p.finish()


_INS = ["x", "mix_norm_w", "ffn_norm_w", "final_norm_w", "gla_w_in", "gla_w_gate2", "gla_b_gate",
        "gla_norm_w", "gla_w_out", "ffn_w_up", "ffn_conv_w", "ffn_conv_b", "ffn_w_down",
        "lb_logits_2", "norm_mix_2", "w_in_2", "conv_w_2", "conv_b_2", "w_r_2", "b_r_2", "w_i_2",
        "b_i_2", "lam_2", "hg_norm_2", "w_out_2", "norm_mlp_2", "w_up_2", "w_down_2", "norm_final_2"]


def kernel(**inputs):
    import numpy as _np
    import concourse.bacc as _bacc
    from concourse import mybir as _mybir
    from concourse.bass_utils import run_bass_kernel_spmd as _run

    nc = _bacc.Bacc("TRN2", target_bir_lowering=False, num_devices=1)
    arrays, aps = {}, {}
    for name in _INS:
        arrays[f"in_{name}"] = _np.ascontiguousarray(inputs[name])
    arrays["in_ident"] = _np.eye(P, dtype=_np.float32)
    masks = _np.zeros((P, LEVELS, P // 2), _np.float32)
    for l in range(LEVELS):
        n = 1 << l
        for t in range(P // 2):
            at = (t // n) * 2 * n
            masks[at:at + n, l, t] = 1
    arrays["in_masks"] = masks
    for name, x in arrays.items():
        aps[name[3:]] = nc.dram_tensor(name, x.shape, _mybir.dt.from_np(x.dtype), kind="ExternalInput").ap()
    aps["out"] = nc.dram_tensor("out", (1, SEQ, D), _mybir.dt.float32, kind="ExternalOutput").ap()
    build(nc, aps)
    r = _run(nc, [arrays], core_ids=[0])
    return r.results[0]["out"]
```

```python
from contextlib import ExitStack

import concourse.bass as bass
from concourse import mybir

ALU = mybir.AluOpType
ACT = mybir.ActivationFunctionType
AX = mybir.AxisListType.X
F32 = mybir.dt.float32
F32R = mybir.dt.float32r
BF16 = mybir.dt.bfloat16
U8 = mybir.dt.uint8
ds = bass.ds

P = 128
SEQ = 1024
D = 1024
MT = SEQ // P
DOWN = 2 * MT
KT = D // P
HALF = 512
UNIT = 1024
EPS = 1e-6

GLA_HEADS, DK, DV, RANK, TAU, CHUNK = 4, 128, 256, 16, 16.0, 64
NCH = SEQ // CHUNK
GLA_IN = 2 * GLA_HEADS * DK + 2 * GLA_HEADS * DV + RANK
FFN_DIM = 2816
FT = FFN_DIM // P
HG_HEADS, HG_DV, LEVELS = 8, 128, 7
RG_C = 8.0
F_MIN = 1e-30
D_FF = 4096

C_FCW, C_FCB = 0, 3 * 2 * FT
C_BG = C_FCB + 2 * FT
C_GNW = C_BG + 4
C_CW = C_GNW + 8
C_CB = C_CW + 32
C_BR = C_CB + 8
C_BI = C_BR + 8
C_LAM = C_BI + 8
C_HGN = C_LAM + 8
C_LB = C_HGN + 1
C_END = C_LB + 8
ROWS = 4 * FT


def wait(eng, sem, value):
    if isinstance(value, int) and value <= 0:
        return
    eng.wait_ge(sem, value)


class Core:
    pass


class Stream:

    def __init__(self, sem, name, core, slots, first, per, total, early):
        self.slots, self.first, self.per, self.core = slots, first, per, core
        self.total = total
        self.early = early
        self.raw_in = [sem(f"{name}_raw_in{n}") for n in range(2)]
        self.hi_done = sem(f"{name}_hi_done")
        self.split = sem(f"{name}_split")
        self.used = sem(f"{name}_used")

    def number(self, it, pos):
        if isinstance(it, int) and it == 0:
            return pos, pos
        return self.first + pos, (it - 1) * self.per + self.first + pos

    def done(self, it, pos):
        return self.number(it, pos)[1] + 2

    def ready(self, it, pos):
        return self.number(it, pos)[1] + 1

    def slot(self, it, pos):
        n = self.number(it, pos)[0] % self.slots
        c = self.core
        return (c.whi[:, n, :], c.wlo[:, n, :]) if n < 3 else (c.whi4, c.wlo4)

    def load(self, sp, it, pos, source, dims):
        s, g = self.number(it, pos)
        if self.early and isinstance(g, int) and g < 2:
            return
        wait(sp, self.split, g - 1)
        dst = self.core.raw[:, s % 2, :]
        if dims:
            dst = dst.rearrange("p (k n) -> p k n", k=dims)
        sp.dma_start(dst, source).then_inc(self.raw_in[s % 2], 16)

    def divide(self, pool, it, pos):
        s, g = self.number(it, pos)
        if self.early and isinstance(g, int) and g == 0:
            return
        self.halve(pool, it, pos, s, g)

    def early_load(self, sp, before):
        sp.wait_ge(before.split, before.total)
        for n, source in enumerate(self.early):
            sp.dma_start(self.core.raw[:, n, :].rearrange("p (k n) -> p k n", k=KT), source)\
              .then_inc(self.raw_in[n], 16)

    def early_divide(self, pool, before, downs):
        pool.wait_ge(before.used, before.total - downs + 1)
        self.halve(pool, 0, 0, 0, 0)

    def halve(self, pool, it, pos, s, g):
        hi, lo = self.slot(it, pos)
        raw = self.core.raw[:, s % 2, :]
        if isinstance(g, int):
            arrived = 16 * (g // 2 + 1)
        else:
            arrived = (it - 1) * (8 * self.per) + 16 * (s // 2 + 1)
        pool.wait_ge(self.raw_in[s % 2], arrived)
        if not (isinstance(g, int) and g < self.slots):
            pool.wait_ge(self.used, g - self.slots + 2)
        pool.tensor_tensor(hi, raw, self.core.zero[:, 0:1].broadcast_to([P, UNIT]), ALU.add)\
            .then_inc(self.hi_done, 1)
        pool.wait_ge(self.hi_done, g + 1)
        pool.tensor_tensor(lo, raw, hi.bitcast(F32), ALU.subtract).then_inc(self.split, 1)


def product(pe, out, a, b, first, last):
    (ah, al), (bh, bl) = a, b
    pe.matmul(out, ah, bh, start=first, stop=False)
    pe.matmul(out, ah, bl, start=False, stop=False)
    return pe.matmul(out, al, bh, start=False, stop=last)


def columns_half(pe, core, st, it, pos, pair, half):
    if half == 0:
        pe.wait_ge(st.split, st.ready(it, pos))
    hi, lo = (x.rearrange("p (k n) -> p k n", k=KT) for x in st.slot(it, pos))
    cols = slice(half * HALF, (half + 1) * HALF)
    for k in range(KT):
        mm = product(pe, pair[:, cols], (hi[:, k, :], lo[:, k, :]),
                     (core.hhi[:, k, cols], core.hlo[:, k, cols]), k == 0, k == KT - 1)
    if half:
        mm.then_inc(st.used, 1)


def columns_tile(pe, core, st, it, pos, pair):
    columns_half(pe, core, st, it, pos, pair, 0)
    columns_half(pe, core, st, it, pos, pair, 1)


def rows_group(pe, core, parts, pair, m, first):
    rows = slice(m * P, (m + 1) * P)
    for k in range(KT):
        wh, wl = parts[k // 4]
        mm = product(pe, pair[:, (m - first) * 2 * P:(m - first + 1) * 2 * P],
                     (core.hhi[:, k, rows], core.hlo[:, k, rows]),
                     (wh[:, k % 4, :], wl[:, k % 4, :]), k == 0, k == KT - 1)
    return mm


def row_parts(st, it, pos):
    return [[x.rearrange("p (k n) -> p k n", k=4) for x in st.slot(it, pos + u)] for u in range(2)]


def down_tile(pe, core, m, half, parts, weights, bank):
    n = len(parts)
    rows, cols = slice(m * P, (m + 1) * P), slice(half * HALF, (half + 1) * HALF)
    for k, ((ah, al), (wh, wl)) in enumerate(zip(parts, weights)):
        mm = product(pe, bank, (ah[:, rows], al[:, rows]), (wh[:, cols], wl[:, cols]),
                     k == 0, k == n - 1)
    return mm


class Norm:

    def __init__(self, sem, name, core, xn, junk, row, pairs, ready):
        self.core, self.xn, self.junk, self.row, self.ready = core, xn, junk, row, ready
        self.pairs = pairs
        self.row_in, self.squared, self.vars, self.roots, self.scaled, self.turned, self.hi, self.lo = (
            sem(f"{name}_{s}") for s in ("row_in", "squared", "var", "root", "scaled", "turned", "hi", "lo"))

    def pair(self, m):
        return self.pairs[m % 2]

    def square(self, act, m):
        act.wait_ge(*self.ready(m))
        wait(act, self.squared, m)
        act.activation(self.junk, self.core.X[:, m, :], ACT.Square, accum_out=self.core.ss[:, m:m + 1])\
            .then_inc(self.squared, 1)

    def var(self, dve, m):
        c = self.core
        dve.wait_ge(self.squared, m + 1)
        dve.tensor_scalar(c.ms[:, m:m + 1], c.ss[:, m:m + 1], 1.0 / D, EPS, ALU.mult, ALU.add)\
            .then_inc(self.vars, 1)

    def root(self, act, m):
        act.wait_ge(self.vars, m + 1)
        act.activation(self.core.sd[:, m:m + 1], self.core.ms[:, m:m + 1], ACT.Sqrt).then_inc(self.roots, 1)

    def scale(self, dve, m):
        c = self.core
        dve.wait_ge(self.roots, m + 1)
        dve.reciprocal(c.rs[:, m:m + 1], c.sd[:, m:m + 1])
        if m == 0:
            dve.wait_ge(self.row_in, 16)
        dve.drain()
        self.scaled_tile(dve, m)

    def scaled_tile(self, dve, m):
        c = self.core
        wait(dve, self.turned, m - 1)
        dve.scalar_tensor_tensor(out=self.xn[:, m % 2, :], in0=c.X[:, m, :], scalar=c.rs[:, m:m + 1],
                                 in1=self.row, op0=ALU.mult, op1=ALU.mult).then_inc(self.scaled, 1)

    def turn(self, pe, m):
        pe.wait_ge(self.scaled, m + 1)
        wait(pe, self.lo, m - 1)
        for k in range(KT):
            mm = pe.transpose(self.pair(m)[:, k * P:(k + 1) * P],
                              self.xn[:, m % 2, k * P:(k + 1) * P], self.core.ident[:, :])
        mm.then_inc(self.turned, 1)

    def high(self, act, m):
        act.wait_ge(self.turned, m + 1)
        act.copy(self.core.hhi[:, :, m * P:(m + 1) * P],
                 self.pair(m).rearrange("p (k n) -> p k n", k=KT)).then_inc(self.hi, 1)

    def low(self, dve, m):
        c = self.core
        dve.wait_ge(self.hi, m + 1)
        rows = slice(m * P, (m + 1) * P)
        dve.tensor_tensor(c.hlo[:, :, rows], self.pair(m).rearrange("p (k n) -> p k n", k=KT),
                          c.hhi[:, :, rows].bitcast(F32), ALU.subtract).then_inc(self.lo, 1)


class RowNorm(Norm):

    def __init__(self, sem, name, core, junk, row, ready):
        self.core, self.junk, self.row, self.ready = core, junk, row, ready
        self.row_in, self.squared, self.vars, self.roots, self.scaled = (
            sem(f"{name}_{s}") for s in ("row_in", "squared", "var", "root", "scaled"))

    def scaled_tile(self, dve, m):
        c = self.core
        dve.scalar_tensor_tensor(out=c.X[:, m, :], in0=c.X[:, m, :], scalar=c.rs[:, m:m + 1],
                                 in1=self.row, op0=ALU.mult, op1=ALU.mult).then_inc(self.scaled, 1)


class Lags:

    def __init__(self, fin, norm):
        self.fin, self.norm = fin, norm
        back = 2 if fin and norm else 0
        self.act = [(fin, "square", 0), (fin, "root", 1)] if fin else []
        self.dve = [(fin, "var", 1), (fin, "scale", 2)] if fin else []
        if norm:
            self.act += [(norm, "square", back), (norm, "root", back + 1), (norm, "high", back + 4)]
            self.dve += [(norm, "var", back + 1), (norm, "scale", back + 2), (norm, "low", back + 4)]
        self.turn_lag = back + 3
        self.last = MT + back + 4 if norm else MT + 2

    def scalar(self, act):
        for k in range(self.last):
            for norm, step, lag in self.act:
                m = k - lag
                if 0 <= m < MT:
                    if step == "square":
                        norm.square(act, m)
                    elif step == "root":
                        norm.root(act, m)
                    else:
                        norm.high(act, m)

    def vector(self, dve, arrive):
        for k in range(self.last):
            if k < MT:
                arrive(k)
            for norm, step, lag in self.dve:
                m = k - lag
                if 0 <= m < MT:
                    if step == "var":
                        norm.var(dve, m)
                    elif step == "scale":
                        norm.scale(dve, m)
                    else:
                        norm.low(dve, m)

    def tensor(self, pe, arrive):
        for k in range(MT + self.turn_lag if self.norm else MT):
            if k < MT:
                arrive(k)
            if self.norm and k >= self.turn_lag:
                self.norm.turn(pe, k - self.turn_lag)


def down_product(pe, c, st, it, positions, parts, down_mm, down_add, before, banks=2, tiles=range(MT)):
    if tiles[0] == 0:
        pe.wait_ge(st.split, st.ready(it, positions[-1]))
    weights = [st.slot(it, pos) for pos in positions]
    for m in tiles:
        for half in range(2):
            n = 2 * m + half
            pe.wait_ge(down_add, before * DOWN + max(n - banks + 2, 1))
            mm = down_tile(pe, c, m, half, parts, weights, down_bank(c, n, banks))
            mm.then_inc(*((down_mm, 1) if n < DOWN - 1 else (st.used, len(positions))))


def down_bank(c, n, banks):
    return (c.DD, c.MM)[n % banks // 2][:, (n % 2) * HALF:(n % 2 + 1) * HALF]


def add_down(dve, c, st, down_mm, down_add, it, pos, before, banks=2, tiles=range(MT)):
    for m in tiles:
        for half in range(2):
            n = 2 * m + half
            if n < DOWN - 1:
                dve.wait_ge(down_mm, before * (DOWN - 1) + n + 1)
            else:
                dve.wait_ge(st.used, st.done(it, pos))
            cols = slice(half * HALF, (half + 1) * HALF)
            dve.tensor_tensor(c.X[:, m, cols], c.X[:, m, cols], down_bank(c, n, banks), ALU.add)\
               .then_inc(down_add, 1)


class Program:
    def __init__(self, nc, ctx, a):
        self.nc, self.ctx, self.a = nc, ctx, a
        self.stage_sems, self.next_sems = [], []
        c = self.core = Core()
        c.X = self.sb("X", [P, MT, D])
        c.hhi = self.sb("h_hi", [P, KT, SEQ], F32R)
        c.hlo = self.sb("h_lo", [P, KT, SEQ], F32R)
        c.raw = self.sb("w_raw", [P, 2, UNIT])
        c.whi = self.sb("w_hi", [P, 3, UNIT], F32R)
        c.wlo = self.sb("w_lo", [P, 3, UNIT], F32R)
        c.zero = self.sb("zero", [P, 1])
        c.ident = self.sb("ident", [P, P])
        c.masks = self.sb("masks", [P, LEVELS, P // 2], U8)
        c.par = self.sb("params", [P, C_END])
        c.decay = self.sb("lru_decay", [P, 2, 8])
        c.lb = self.sb("lower_bound", [P, 2, 8])
        c.ss, c.ms, c.sd, c.rs = (self.sb(n, [P, MT]) for n in ("ss", "ms", "sd", "rs"))
        c.PA = self.ps("PA", [P, SEQ])
        c.PB = self.ps("PB", [P, SEQ])
        c.DD = self.ps("DD", [P, SEQ])
        c.MM = self.ps("MM", [P, SEQ])
        self.x_in = [ctx.enter_context(nc.semaphore(f"x_in{m}")) for m in range(MT)]

    def sb(self, name, shape, dt=F32):
        return self.ctx.enter_context(self.nc.sbuf_tensor(name, shape, dt))[:]

    def ps(self, name, shape):
        return self.ctx.enter_context(self.nc.psum_tensor(name, shape, F32))[:]

    def sem(self, name):
        handle = self.nc.alloc_semaphore(name)
        self.stage_sems.append(handle)
        return handle

    def next_sem(self, name):
        handle = self.nc.alloc_semaphore(name)
        self.next_sems.append(handle)
        return handle

    def end_stage(self):
        self.nc.clear_and_free_semaphores(self.stage_sems)
        self.nc.all_engine_barrier()
        self.stage_sems, self.next_sems = self.next_sems, []

    def fourth_slot(self, ctx, name):
        c = self.core
        c.whi4 = ctx.enter_context(self.nc.sbuf_tensor(f"{name}_w_hi", [P, UNIT], F32R))[:]
        c.wlo4 = ctx.enter_context(self.nc.sbuf_tensor(f"{name}_w_lo", [P, UNIT], F32R))[:]

    def parameters(self):
        nc, c, a = self.nc, self.core, self.a
        with ExitStack() as ctx:
            rows = ctx.enter_context(nc.sbuf_tensor("param_rows", [P, 3, P], F32))[:]
            t = ctx.enter_context(nc.sbuf_tensor("param_temps", [P, 6, 8], F32))[:]
            maskf = ctx.enter_context(nc.sbuf_tensor("masks_in", [P, LEVELS, P // 2], F32))[:]
            s_rows, s_id, s_par, s_turn, s_zero = (self.sem(n) for n in (
                "rows_in", "ident_in", "params_ready", "params_turned", "rows_zeroed"))
            s_abs, s_exp, s_lb = self.sem("lam_abs"), self.sem("lam_exp"), self.sem("lb_exp")
            s_e = self.sem("lb_shifted")
            last = C_END - 2 * ROWS
            block = ctx.enter_context(nc.Block())

            @block.sync
            def _(sp):
                sp.dma_start(c.ident, a["ident"]).then_inc(s_id, 16)
                sp.dma_start(maskf, a["masks"]).then_inc(s_id, 16)
                taps = a["ffn_conv_w"][0].rearrange("t (f p) -> (t f) p", p=P)
                sp.dma_start(rows[0:ROWS, 0, :], taps[0:ROWS, :]).then_inc(s_rows, 16)
                sp.dma_start(rows[0:2 * FT, 1, :], taps[ROWS:3 * 2 * FT, :]).then_inc(s_rows, 16)
                sp.dma_start(rows[2 * FT:ROWS, 1, :],
                             a["ffn_conv_b"][0].rearrange("(f p) -> f p", p=P)).then_inc(s_rows, 16)
                n = 0
                for src in (
                    a["gla_b_gate"][0].rearrange("(f p) -> f p", p=P),
                    a["gla_norm_w"][0].rearrange("(f p) -> f p", p=P),
                    a["conv_w_2"][0].rearrange("t (f p) -> (t f) p", p=P),
                    a["conv_b_2"][0].rearrange("(f p) -> f p", p=P),
                    a["b_r_2"][0].rearrange("(f p) -> f p", p=P),
                    a["b_i_2"][0].rearrange("(f p) -> f p", p=P),
                    a["lam_2"][0].rearrange("(f p) -> f p", p=P),
                    a["hg_norm_2"],
                    a["lb_logits_2"][0].rearrange("(f p) -> f p", p=P),
                ):
                    k = src.shape[0]
                    sp.dma_start(rows[n:n + k, 2, :], src).then_inc(s_rows, 16)
                    n += k
                for m in range(MT):
                    sp.dma_start(c.X[:, m, :], a["x"][0, m * P:(m + 1) * P, :]).then_inc(self.x_in[m], 16)

            @block.tensor
            def _(pe):
                pe.wait_ge(s_id, 32)
                pe.wait_ge(s_rows, 16 * 12)
                for g in range(3):
                    k = ROWS if g < 2 else last
                    mm = pe.transpose(c.MM[:, g * ROWS:g * ROWS + k], rows[0:k, g, :], c.ident[0:k, 0:k])
                mm.then_inc(s_turn, 1)

            @block.scalar
            def _(act):
                act.wait_ge(s_abs, 1)
                act.activation(t[:, 1, :], t[:, 0, :], ACT.Exp, scale=-1.0).then_inc(s_exp, 1)
                act.wait_ge(s_e, 1)
                act.activation(t[:, 5, :], t[:, 4, :], ACT.Exp).then_inc(s_lb, 1)

            @block.vector
            def _(dve):
                def then(ins):
                    dve.drain()
                    return ins

                dve.memset(c.zero, 0.0)
                dve.wait_ge(s_id, 32)
                dve.tensor_copy(c.masks, maskf)
                dve.wait_ge(s_turn, 1)
                then(dve.tensor_copy(c.par, c.MM[:, 0:C_END]))
                lam, lbl = c.par[:, C_LAM:C_LAM + 8], c.par[:, C_LB:C_LB + 8]
                dve.tensor_scalar(t[:, 2, :], lam, -1.0, 0.0, ALU.mult, ALU.max)
                then(dve.tensor_scalar(t[:, 3, :], lam, 0.0, None, ALU.max))
                dve.tensor_tensor(t[:, 0, :], t[:, 2, :], t[:, 3, :], ALU.add).then_inc(s_abs, 1)
                dve.tensor_tensor(t[:, 4, :], lbl, lbl, ALU.subtract).then_inc(s_e, 1)
                dve.wait_ge(s_exp, 1)
                then(dve.tensor_scalar(t[:, 3, :], t[:, 1, :], 2.0, None, ALU.add))
                then(dve.reciprocal(t[:, 3, :], t[:, 3, :]))
                then(dve.tensor_tensor(t[:, 1, :], t[:, 1, :], t[:, 3, :], ALU.mult))
                then(dve.tensor_tensor(t[:, 3, :], t[:, 1, :], t[:, 1, :], ALU.mult))
                then(dve.tensor_scalar(t[:, 0, :], t[:, 3, :], 1.0 / 17, 1.0 / 15, ALU.mult, ALU.add))
                for d in (13, 11, 9, 7, 5, 3, 1):
                    then(dve.tensor_tensor(t[:, 0, :], t[:, 0, :], t[:, 3, :], ALU.mult))
                    then(dve.tensor_scalar(t[:, 0, :], t[:, 0, :], 1.0 / d, None, ALU.add))
                then(dve.tensor_tensor(t[:, 0, :], t[:, 0, :], t[:, 1, :], ALU.mult))
                then(dve.scalar_tensor_tensor(out=t[:, 0, :], in0=t[:, 0, :], scalar=2.0,
                                              in1=t[:, 2, :], op0=ALU.mult, op1=ALU.add))
                dve.tensor_scalar(c.decay[:, 0, :], t[:, 0, :], -RG_C, None, ALU.mult)
                dve.tensor_scalar(c.decay[:, 1, :], t[:, 0, :], RG_C, None, ALU.mult)
                dve.wait_ge(s_lb, 1)
                then(dve.reciprocal(t[:, 4, :], t[:, 5, :]))
                then(dve.tensor_tensor(t[:, 4, :], t[:, 4, :], t[:, 5, :], ALU.mult))
                then(dve.tensor_tensor(t[:, 5, :], t[:, 4, :], t[:, 4, :], ALU.subtract))
                then(dve.tensor_scalar(c.lb[:, 0, :], t[:, 5, :], 0.0, 1.0, ALU.max, ALU.min))
                dve.tensor_scalar(c.lb[:, 1, :], c.lb[:, 0, :], -1.0, 1.0, ALU.mult, ALU.add)\
                    .then_inc(s_par, 1)
                dve.wait_ge(s_par, 1)

    def gla(self, following):
        nc, c, a = self.nc, self.core, self.a
        W = a["gla_w_in"][0].rearrange("(k p) n -> p k n", p=P)
        WO = a["gla_w_out"][0].rearrange("(k p) n -> p k n", p=P)
        H = GLA_HEADS
        QC, KC, VC, RC = 0, H * DK, 2 * H * DK, 2 * H * DK + H * DV
        with ExitStack() as ctx:
            def sb(name, shape, dt=F32):
                return ctx.enter_context(nc.sbuf_tensor(name, shape, dt))[:]

            self.fourth_slot(ctx, "gla")
            T1, T2, T3, Q = (sb(f"gla_{n}", [P, SEQ]) for n in ("t1", "t2", "t3", "q"))
            GLR = sb("gla_glr", [P, SEQ])
            V, R, Y = (sb(f"gla_{n}", [P, MT, DV]) for n in ("v", "r", "y"))
            KDT = sb("gla_kdT", [P, MT, DK])
            yhi, ylo = (sb(f"gla_y_{n}", [P, 2, SEQ], F32R) for n in ("hi", "lo"))
            keep = sb("gla_keep", [P, SEQ], BF16)
            G2 = sb("gla_gate2", [P, DK])
            S = sb("gla_state", [P, 2, DV])
            DEC = sb("gla_dec", [P, NCH])
            so, vo, qo, ro = (sb(f"gla_o_{n}", [P, MT]) for n in ("ss", "ms", "sd", "rs"))
            graw = Y.rearrange("p m v -> p (m v)")[:, 0:UNIT].rearrange("p (k n) -> p k n", k=KT)
            ghi, glo = (y[:, 0, :].rearrange("p (k n) -> p k n", k=KT) for y in (yhi, ylo))

            POS = {n: k for k, n in enumerate(("k", "v0", "v1", "dn0", "dn1", "q", "r0", "r1"))}

            def at(h, name):
                if isinstance(h, int):
                    if h == 0 and POS[name] > POS["dn1"]:
                        return POS[name] - 2
                    if h == H:
                        return POS[name] - POS["dn0"]
                return POS[name]

            st = Stream(self.sem, "gla", c, 4, 6, 8, 8 * H, None)
            ahead = following(self.next_sem)
            s = {n: self.sem(f"gla_{n}") for n in (
                "graw_in", "g_hi", "g_lo", "glr_mm", "glr", "g2_zero", "g2_in",
                "gate_mm", "absd", "gate_read", "logd", "rel", "decay", "kd", "v_mm", "r_mm", "v", "q",
                "r", "kdt_mm", "kdt", "st_mm", "s", "o_mm", "o_sq", "o_ms", "o_sd", "o_n", "y", "yt_mm",
                "y_hi", "y_lo", "down_mm", "down_add")}
            scratch = V.rearrange("p (b m) v -> p b (m v)", b=2)
            norm = Norm(self.sem, "gla_norm", c, scratch, T1, Q, (c.DD, c.MM), lambda m: (self.x_in[m], 16))
            head = Lags(None, norm)
            after = Norm(self.sem, "gla_next", c, scratch, T1, Q, (c.PA, c.PB),
                         lambda m: (s["down_add"], (H - 1) * DOWN + 2 * m + 3))
            tail = Lags(None, after)
            block = ctx.enter_context(nc.Block())
            ends = T3.rearrange("p (c t) -> p c t", t=CHUNK)[:, :, CHUNK - 1]

            ORDER = ("YR* gate k.0 k.1 YT0* v.0 YT1* v.1 v.2 v.3 dn* q.0 q.1 KT r.0 C0 r.1 C1 r.2 C2 r.3 C3 "
                     "r.4 C4 r.5 C5 r.6 C6 r.7 C7 C8").split()

            def phases(run):
                def steps(h):
                    for x in ORDER:
                        if x.endswith("*"):
                            if not (isinstance(h, int) and h == 0):
                                run(x[:-1], h - 1, h)
                        elif not (isinstance(h, int) and h == H):
                            run(x, h, h)

                def of(eng):
                    steps(0)
                    with eng.Fori(1, H) as h:
                        steps(h)
                    steps(H)
                return of

            @block.sync
            def _(sp):
                sp.dma_start(norm.row, a["mix_norm_w"][0].partition_broadcast(P)).then_inc(norm.row_in, 16)
                sp.dma_start(graw, W[:, :, GLA_IN - P:GLA_IN]).then_inc(s["graw_in"], 16)

                def run(x, h, n):
                    if x == "gate":
                        if isinstance(h, int):
                            sp.wait_ge(s["g2_zero"], 1)
                        wait(sp, s["gate_mm"], h)
                        sp.dma_start(G2[P - RANK:P, :], a["gla_w_gate2"][0][:, ds(h * DK, DK)])\
                            .then_inc(s["g2_in"], 16)
                    elif x == "k.0":
                        st.load(sp, n, at(n, "k"), W[:, :, ds(h * DK + KC, DK)], KT)
                    elif x == "dn":
                        for k in range(2):
                            st.load(sp, n, at(n, f"dn{k}"), WO[:, ds(h * 2 + k, 1), :].rearrange("p k n -> p (k n)"), 0)
                    elif x in ("v.0", "r.0"):
                        for k in range(2):
                            st.load(sp, n, at(n, f"{x[0]}{k}"),
                                    W[:, 4 * k:4 * k + 4, ds(h * DV + {"v": VC, "r": RC}[x[0]], DV)], 4)
                    elif x == "q.0":
                        st.load(sp, n, at(n, "q"), W[:, :, ds(h * DK + QC, DK)], KT)
                phases(run)(sp)
                sp.wait_ge(s["q"], H)
                sp.wait_ge(s["o_mm"], NCH * H)
                sp.dma_start(after.row, a["ffn_norm_w"][0].partition_broadcast(P)).then_inc(after.row_in, 16)
                ahead.early_load(sp, st)

            @block.gpsimd
            def _(pool):
                pool.wait_ge(s["graw_in"], 16)
                pool.tensor_tensor(ghi, graw, c.zero[:, 0:1].unsqueeze(2).broadcast_to([P, KT, P]),
                                   ALU.add).then_inc(s["g_hi"], 1)
                pool.wait_ge(s["g_hi"], 1)
                pool.tensor_tensor(glo, graw, ghi.bitcast(F32), ALU.subtract).then_inc(s["g_lo"], 1)

                def run(x, h, n):
                    for name in {"k.0": ("k",), "dn": ("dn0", "dn1"), "v.0": ("v0", "v1"), "q.0": ("q",),
                                 "r.0": ("r0", "r1")}.get(x, ()):
                        st.divide(pool, n, at(n, name))
                phases(run)(pool)
                ahead.early_divide(pool, st, 2)

            def down_parts():
                return [(yhi[:, k, :], ylo[:, k, :]) for k in range(2)]

            @block.tensor
            def _(pe):
                pe.sem_inc(st.used, 1)
                head.tensor(pe, lambda m: None)
                pe.wait_ge(norm.lo, MT)
                pe.wait_ge(s["g_lo"], 1)
                for half in range(2):
                    cols = slice(half * HALF, (half + 1) * HALF)
                    for k in range(KT):
                        mm = product(pe, c.MM[:, cols], (ghi[:, k, :], glo[:, k, :]),
                                     (c.hhi[:, k, cols], c.hlo[:, k, cols]), k == 0, k == KT - 1)
                mm.then_inc(s["glr_mm"], 1)
                pe.wait_ge(s["glr"], 1)

                def update(h, n):
                    if n >= 2:
                        pe.wait_ge(s["s"], h * NCH + n - 1)
                    rows = slice(CHUNK * (n % 2), CHUNK * (n % 2) + CHUNK)
                    pe.matmul(c.DD[:, (n % 2) * HALF:(n % 2) * HALF + DV], KDT[rows, n // 2, :],
                              V[rows, n // 2, :], start=True, stop=True).then_inc(s["st_mm"], 1)

                def read(h, n):
                    pe.wait_ge(s["s"], h * NCH + n + 1)
                    m = n // 2
                    if m >= 2:
                        pe.wait_ge(s["o_n"], h * MT + m - 1)
                    rows = slice(CHUNK * (n % 2), CHUNK * (n % 2) + CHUNK)
                    pe.matmul(c.MM[rows, (m % 2) * HALF:(m % 2) * HALF + DV],
                              Q[:, n * CHUNK:(n + 1) * CHUNK], S[:, n % 2, :],
                              start=True, stop=True).then_inc(s["o_mm"], 1)

                def run(x, h, n):
                    name, _, part = x.partition(".")
                    if x == "gate":
                        pe.wait_ge(s["g2_in"], 16 * h + 16)
                        wait(pe, s["s"], NCH * h)
                        for half in range(2):
                            cols = slice(half * HALF, (half + 1) * HALF)
                            mm = pe.matmul(c.DD[:, cols], G2, GLR[:, cols], start=True, stop=True)
                        mm.then_inc(s["gate_mm"], 1)
                    elif name in ("k", "q"):
                        if x == "k.0":
                            wait(pe, s["r"], 2 * h - 1)
                        if x == "q.0":
                            pe.wait_ge(s["v"], 2 * h + 1)
                        columns_half(pe, c, st, n, at(n, name), c.PA if name == "k" else c.PB, int(part))
                    elif name in ("v", "r") and part:
                        q = int(part)
                        pos = at(n, name + "0")
                        if q == 0:
                            pe.wait_ge(st.split, st.ready(n, pos + 1))
                        parts = row_parts(st, n, pos)
                        ms = (2 * q, 2 * q + 1) if name == "v" else (q,)
                        for m in ms:
                            if m % 4 == 0:
                                wait(pe, *{"v0": (s["r"], 2 * h), "v4": (s["kd"], h + 1),
                                           "r0": (s["v"], 2 * h + 2), "r4": (s["q"], h + 1)}[f"{name}{m}"])
                            pair = (c.PB, c.PA)[m // 4] if name == "v" else (c.PA, c.PB)[m // 4]
                            mm = rows_group(pe, c, parts, pair, m, m // 4 * 4)
                            if m == 3:
                                mm.then_inc(s[name + "_mm"], 1)
                            if m == MT - 1:
                                mm.then_inc(st.used, 2)
                    elif x == "KT":
                        pe.wait_ge(s["kd"], h + 1)
                        wait(pe, s["y_lo"], 2 * h)
                        for m in range(MT):
                            mm = pe.transpose(c.MM[:, m * P:(m + 1) * P], T1[:, m * P:(m + 1) * P], c.ident)
                        mm.then_inc(s["kdt_mm"], 1)
                    elif x[0] == "C":
                        m = int(x[1:])
                        if m == 0:
                            pe.wait_ge(s["kdt"], h + 1)
                            pe.wait_ge(s["v"], 2 * h + 2)
                            pe.wait_ge(s["q"], h + 1)
                            pe.wait_ge(s["gate_read"], h + 1)
                            pe.wait_ge(s["down_add"], h * DOWN + 1)
                        else:
                            read(h, 2 * m - 2)
                            read(h, 2 * m - 1)
                        if m < MT:
                            update(h, 2 * m)
                            update(h, 2 * m + 1)
                    elif x in ("YT0", "YT1"):
                        k = int(x[2])
                        pe.wait_ge(s["y"], 2 * h + 2)
                        wait(pe, s["y_lo"], 2 * h + k)
                        for m in range(MT):
                            mm = pe.transpose(c.MM[:, m * P:(m + 1) * P], Y[:, m, k * P:(k + 1) * P], c.ident)
                        mm.then_inc(s["yt_mm"], 1)
                    elif x == "dn":
                        pe.wait_ge(s["y_lo"], 2 * h + 2)
                        last = isinstance(n, int)
                        if not last:
                            pe.wait_ge(s["gate_read"], h + 2)

                        def some(tiles):
                            down_product(pe, c, st, n, (at(n, "dn0"), at(n, "dn1")), down_parts(),
                                         s["down_mm"], s["down_add"], h, 2, tiles)
                        if last:
                            tail.tensor(pe, lambda m: some((m,)))
                        else:
                            some(range(MT))
                phases(run)(pe)

            @block.scalar
            def _(act):
                head.scalar(act)
                act.wait_ge(s["glr_mm"], 1)
                act.copy(GLR, c.MM).then_inc(s["glr"], 1)

                def squares(h, m):
                    act.wait_ge(s["o_mm"], h * NCH + 2 * m + 2)
                    o = c.MM[:, (m % 2) * HALF:(m % 2) * HALF + DV]
                    act.activation(T3[:, 0:DV], o, ACT.Square, accum_out=so[:, m:m + 1]).then_inc(s["o_sq"], 1)
                    act.wait_ge(s["o_ms"], h * MT + m + 1)
                    act.activation(qo[:, m:m + 1], vo[:, m:m + 1], ACT.Sqrt).then_inc(s["o_sd"], 1)

                def run(x, h, n):
                    if x == "gate":
                        act.wait_ge(s["gate_mm"], h + 1)
                        act.activation(T1, c.DD, ACT.Abs, bias=c.par[:, ds(h + C_BG, 1)]).then_inc(s["absd"], 1)
                        act.drain()
                        act.activation(T1, T1, ACT.Exp, scale=-1.0)
                        act.drain()
                        act.activation(T1, T1, ACT.Ln, bias=1.0).then_inc(s["logd"], 1)
                        act.wait_ge(s["rel"], h + 1)
                        act.activation(T2, T2, ACT.Exp, scale=1.0 / TAU)
                        act.activation(DEC, ends, ACT.Exp, scale=1.0 / TAU).then_inc(s["decay"], 1)
                    elif x in ("v.1", "v.3"):
                        k = int(x[2]) // 2
                        act.wait_ge(*((s["v_mm"], h + 1) if k == 0 else (st.used, st.done(n, at(n, "v1")))))
                        act.copy(V[:, 4 * k:4 * k + 4, :], (c.PB, c.PA)[k].rearrange("p (m v) -> p m v", v=DV))\
                           .then_inc(s["v"], 1)
                    elif x == "q.1":
                        act.wait_ge(st.used, st.done(n, at(n, "q")))
                        act.activation(Q, c.PB, ACT.Copy, scale=DK ** -0.5).then_inc(s["q"], 1)
                    elif x in ("r.3", "r.7"):
                        k = int(x[2]) // 4
                        act.wait_ge(*((s["r_mm"], h + 1) if k == 0 else (st.used, st.done(n, at(n, "r1")))))
                        act.activation(R[:, 4 * k:4 * k + 4, :], (c.PA, c.PB)[k].rearrange("p (m v) -> p m v", v=DV),
                                       ACT.Silu).then_inc(s["r"], 1)
                    elif x[0] == "C" and x != "C0":
                        squares(h, int(x[1:]) - 1)
                    elif x in ("YT0", "YT1"):
                        k = int(x[2])
                        act.wait_ge(s["yt_mm"], 2 * h + k + 1)
                        act.activation(yhi[:, k, :], c.MM, ACT.Identity, scale=c.par[:, ds(2 * h + (C_GNW + k), 1)])\
                            .then_inc(s["y_hi"], 1)
                phases(run)(act)
                tail.scalar(act)

            @block.vector
            def _(dve):
                dve.memset(G2, 0.0).then_inc(s["g2_zero"], 1)
                dve.memset(keep, 1.0)
                dve.drain()
                dve.memset(keep.rearrange("p (c t) -> p c t", t=CHUNK)[:, :, 0:1], 0.0)
                dve.sem_inc(s["down_add"], 1)
                head.vector(dve, lambda m: None)

                def state(h, n):
                    dve.wait_ge(s["st_mm"], h * NCH + n + 1)
                    wait(dve, s["o_mm"], h * NCH + n - 1)
                    ps = c.DD[:, (n % 2) * HALF:(n % 2) * HALF + DV]
                    if n == 0:
                        dve.tensor_copy(S[:, 0, :], ps).then_inc(s["s"], 1)
                    else:
                        dve.wait_ge(s["s"], h * NCH + n)
                        dve.scalar_tensor_tensor(out=S[:, n % 2, :], in0=S[:, (n - 1) % 2, :],
                                                 scalar=DEC[:, n:n + 1], in1=ps, op0=ALU.mult,
                                                 op1=ALU.add).then_inc(s["s"], 1)

                def output(h, m):
                    dve.wait_ge(s["o_sd"], h * MT + m + 1)
                    dve.reciprocal(ro[:, m:m + 1], qo[:, m:m + 1])
                    dve.drain()
                    o = c.MM[:, (m % 2) * HALF:(m % 2) * HALF + DV]
                    dve.tensor_scalar(Y[:, m, :], o, ro[:, m:m + 1], None, ALU.mult).then_inc(s["o_n"], 1)

                def run(x, h, n):
                    if x == "gate":
                        dve.wait_ge(s["absd"], h + 1)
                        dve.tensor_scalar(T2, c.DD, c.par[:, ds(h + C_BG, 1)], 0.0, ALU.add, ALU.min)\
                           .then_inc(s["gate_read"], 1)
                        dve.drain()
                        dve.wait_ge(s["logd"], h + 1)
                        dve.tensor_tensor(T2, T2, T1, ALU.subtract)
                        dve.drain()
                        dve.tensor_tensor_scan(T3, keep, T2, 0.0, ALU.mult, ALU.add)
                        dve.drain()
                        chunks = [y.rearrange("p (c t) -> p c t", t=CHUNK) for y in (T2, T3)]
                        dve.tensor_tensor(chunks[0], ends.unsqueeze(2).broadcast_to([P, NCH, CHUNK]), chunks[1],
                                          ALU.subtract).then_inc(s["rel"], 1)
                    elif x == "k.1":
                        dve.wait_ge(s["decay"], h + 1)
                        dve.wait_ge(st.used, st.done(n, at(n, "k")))
                        dve.tensor_tensor(T1, c.PA, T2, ALU.mult).then_inc(s["kd"], 1)
                    elif x == "KT":
                        dve.wait_ge(s["kdt_mm"], h + 1)
                        dve.tensor_copy(KDT.rearrange("p m k -> p (m k)"), c.MM).then_inc(s["kdt"], 1)
                    elif x[0] == "C":
                        m = int(x[1:])
                        if m < MT:
                            state(h, 2 * m)
                            state(h, 2 * m + 1)
                        if m >= 2:
                            output(h, m - 2)
                        if m >= 1:
                            dve.wait_ge(s["o_sq"], h * MT + m)
                            dve.tensor_scalar(vo[:, m - 1:m], so[:, m - 1:m], 1.0 / DV, EPS, ALU.mult,
                                              ALU.add).then_inc(s["o_ms"], 1)
                        if m == MT:
                            output(h, MT - 1)
                    elif x == "YR":
                        dve.wait_ge(s["o_n"], h * MT + MT)
                        for k in range(2):
                            dve.wait_ge(s["r"], 2 * h + k + 1)
                            dve.tensor_tensor(Y[:, 4 * k:4 * k + 4, :], Y[:, 4 * k:4 * k + 4, :],
                                              R[:, 4 * k:4 * k + 4, :], ALU.mult).then_inc(s["y"], 1)
                    elif x in ("YT0", "YT1"):
                        k = int(x[2])
                        dve.wait_ge(s["y_hi"], 2 * h + k + 1)
                        dve.scalar_tensor_tensor(out=ylo[:, k, :], in0=c.MM,
                                                 scalar=c.par[:, ds(2 * h + (C_GNW + k), 1)],
                                                 in1=yhi[:, k, :].bitcast(F32), op0=ALU.mult,
                                                 op1=ALU.subtract).then_inc(s["y_lo"], 1)
                    elif x == "dn":
                        def some(tiles):
                            add_down(dve, c, st, s["down_mm"], s["down_add"], n, at(n, "dn1"), h, 2, tiles)
                        if isinstance(n, int):
                            tail.vector(dve, lambda m: some((m,)))
                        else:
                            some(range(MT))
                phases(run)(dve)

    @staticmethod
    def ffn_stream(sem, name, core, W_up, chunks, gated):
        WU = W_up.rearrange("(k p) n -> p k n", p=P)
        n_up = 4 if gated else 2
        second = FFN_DIM if gated else P
        return Stream(sem, name, core, 3 if gated else 4, n_up, n_up + 2, (n_up + 2) * chunks,
                      [WU[:, :, 0:P], WU[:, :, second:second + P]])

    def ffn(self, name, st, W_up, W_down, chunks, gated, following, rows):
        nc, c = self.nc, self.core
        WU = W_up.rearrange("(k p) n -> p k n", p=P)
        WD = W_down.rearrange("(k p) n -> p k n", p=P)
        n_up = 4 if gated else 2
        with ExitStack() as ctx:
            def sb(n, shape, dt=F32):
                return ctx.enter_context(nc.sbuf_tensor(f"{name}_{n}", shape, dt))[:]

            if not gated:
                self.fourth_slot(ctx, name)
            xn = sb("xn", [P, 2, D])
            rowts = [sb(f"row{k}", [P, D]) for k in range(len(rows))]
            UG, UV = sb("u_gate", [P, SEQ]), sb("u_val", [P, SEQ])
            A = sb("a", [P, 2, SEQ])
            ahi, alo = sb("a_hi", [P, 2, SEQ], F32R), sb("a_lo", [P, 2, SEQ], F32R)
            ahead = following(self.next_sem) if following else None
            s = {n: self.sem(f"{name}_{n}") for n in (
                "base", "conv", "silu", "prod", "a_hi", "a_lo",
                "down_mm", "down_add")}
            fin = RowNorm(self.sem, f"{name}_fin", c, UG, rowts[0],
                          lambda m: (s["down_add"], (chunks - 1) * DOWN + 2 * m + 3))
            norm = Norm(self.sem, f"{name}_next", c, xn, UV, rowts[1], (c.PA, c.PB),
                        lambda m: (fin.scaled, m + 1)) if following else None
            tail = Lags(fin, norm)
            stored = self.sem(f"{name}_stored")
            read = s["conv"] if gated else s["base"]
            pair = (c.PA, c.PB)
            block = ctx.enter_context(nc.Block())

            def phases(eng, up, down):
                up(0)
                with eng.Fori(1, chunks) as i:
                    up(i)
                    down(i)
                down(chunks)

            @block.sync
            def _(sp):
                for x, tile, row in zip((fin, norm), rowts, rows):
                    sp.dma_start(tile, row.partition_broadcast(P)).then_inc(x.row_in, 16)

                def up(i):
                    for t in range(n_up):
                        off = (t // 2) * P + (t % 2) * FFN_DIM if gated else t * P
                        st.load(sp, i, t, WU[:, :, ds(i * (2 * P) + off, P)], KT)

                def down(i):
                    base = n_up if not (isinstance(i, int) and i == chunks) else 0
                    for k in range(2):
                        st.load(sp, i, base + k, WD[:, ds((i - 1) * 2 + k, 1), :].rearrange("p k n -> p (k n)"), 0)
                phases(sp, up, down)
                if ahead:
                    ahead.early_load(sp, st)
                else:
                    for m in range(MT):
                        sp.wait_ge(fin.scaled, m + 1)
                        sp.dma_start(self.a["out"][0, m * P:(m + 1) * P, :], c.X[:, m, :]).then_inc(stored, 16)
                    sp.wait_ge(stored, 16 * MT)

            @block.gpsimd
            def _(pool):
                def up(i):
                    for t in range(n_up):
                        st.divide(pool, i, t)

                def down(i):
                    base = n_up if not (isinstance(i, int) and i == chunks) else 0
                    for k in range(2):
                        st.divide(pool, i, base + k)
                phases(pool, up, down)
                if ahead:
                    ahead.early_divide(pool, st, 2)

            @block.tensor
            def _(pe):
                pe.sem_inc(st.used, 1)

                def up(i):
                    for t in range(n_up):
                        wait(pe, read, i * n_up + t - 1)
                        columns_tile(pe, c, st, i, t, pair[t % 2])

                def down(i):
                    base = n_up if not (isinstance(i, int) and i == chunks) else 0
                    pe.wait_ge(s["a_lo"], i * 2)

                    def some(tiles):
                        down_product(pe, c, st, i, (base, base + 1),
                                     [(ahi[:, k, :], alo[:, k, :]) for k in range(2)],
                                     s["down_mm"], s["down_add"], i - 1, 4, tiles)
                    if isinstance(i, int):
                        tail.tensor(pe, lambda m: some((m,)))
                    else:
                        some(range(MT))
                phases(pe, up, down)

            @block.scalar
            def _(act):
                def up(i):
                    for t in range(n_up):
                        act.wait_ge(st.used, st.done(i, t))
                        if gated:
                            f = (t // 2) + (t % 2) * FT
                            U = UV if t % 2 else UG
                            wait(act, s["prod"], 2 * i + t // 2)
                            act.activation(U, pair[t % 2], ACT.Identity, bias=c.par[:, ds(2 * i + (C_FCB + f), 1)],
                                           scale=c.par[:, ds(2 * i + (C_FCW + 4 * FT + f), 1)]).then_inc(s["base"], 1)
                            if t % 2 == 0:
                                act.wait_ge(s["conv"], 4 * i + t + 1)
                                act.activation(UG, UG, ACT.Silu).then_inc(s["silu"], 1)
                        else:
                            wait(act, s["prod"], 2 * i + t - 1)
                            act.activation((UG, UV)[t], pair[t], ACT.Relu).then_inc(s["base"], 1)
                    for k in range(2):
                        act.wait_ge(s["prod"], 2 * i + k + 1)
                        if not (isinstance(i, int) and i == 0):
                            act.wait_ge(st.used, st.done(i, n_up + 1))
                        act.copy(ahi[:, k, :], A[:, k, :]).then_inc(s["a_hi"], 1)
                phases(act, up, lambda i: None)
                tail.scalar(act)

            @block.vector
            def _(dve):
                dve.sem_inc(s["down_add"], 1)

                def low(i):
                    for k in range(2):
                        dve.wait_ge(s["a_hi"], 2 * i + k + 1)
                        dve.tensor_tensor(alo[:, k, :], A[:, k, :], ahi[:, k, :].bitcast(F32),
                                          ALU.subtract).then_inc(s["a_lo"], 1)

                def up(i):
                    for t in range(n_up):
                        dve.wait_ge(s["base"], i * n_up + t + 1)
                        if gated:
                            f = (t // 2) + (t % 2) * FT
                            U = UV if t % 2 else UG
                            for tap in (1, 0):
                                lag = 2 - tap
                                dve.scalar_tensor_tensor(
                                    out=U[:, lag:SEQ], in0=pair[t % 2][:, 0:SEQ - lag],
                                    scalar=c.par[:, ds(2 * i + (C_FCW + tap * 2 * FT + f), 1)],
                                    in1=U[:, lag:SEQ], op0=ALU.mult, op1=ALU.add)
                                if tap:
                                    dve.drain()
                            dve.drain().then_inc(s["conv"], 1)
                            if t % 2:
                                dve.wait_ge(s["silu"], 2 * i + t // 2 + 1)
                                if not isinstance(i, int):
                                    dve.wait_ge(s["a_lo"], 2 * i)
                                dve.tensor_tensor(A[:, t // 2, :], UG, UV, ALU.mult).then_inc(s["prod"], 1)
                        else:
                            U = (UG, UV)[t]
                            if not isinstance(i, int):
                                dve.wait_ge(s["a_lo"], 2 * i)
                            dve.tensor_tensor(A[:, t, :], U, U, ALU.mult).then_inc(s["prod"], 1)

                def down(i):
                    base = n_up if not (isinstance(i, int) and i == chunks) else 0

                    def some(tiles):
                        add_down(dve, c, st, s["down_mm"], s["down_add"], i, base + 1, i - 1, 4, tiles)
                    if isinstance(i, int):
                        tail.vector(dve, lambda m: some((m,)))
                    else:
                        some(range(MT))

                up(0)
                low(0)
                with dve.Fori(1, chunks) as i:
                    up(i)
                    down(i)
                    low(i)
                down(chunks)

    @staticmethod
    def hybrid_stream(sem, core, W_in):
        W = W_in.rearrange("(k p) n -> p k n", p=P)
        return Stream(sem, "hy", core, 3, 17, 18, 18 * (HG_HEADS // 2), [W[:, :, 0:P], W[:, :, P:2 * P]])

    def hybrid(self, st, following):
        nc, c, a = self.nc, self.core, self.a
        W = a["w_in_2"][0].rearrange("(k p) n -> p k n", p=P)
        WO = a["w_out_2"][0].rearrange("(k p) n -> p k n", p=P)
        WR = a["w_r_2"][0].rearrange("n (j p) k -> p n j k", p=P)
        WI = a["w_i_2"][0].rearrange("n (j p) k -> p n j k", p=P)
        XA_, GA_, Q_, F_, V_, G_, MA_, MB_ = (n * D for n in range(8))
        POS = {n: k for k, n in enumerate((
            "xa0", "xa1", "f0", "q0", "dn1", "v0", "v1", "ga0", "ma0", "g0", "mb0",
            "f1", "q1", "dn0", "ga1", "ma1", "g1", "mb1"))}
        PAIRS = HG_HEADS // 2

        def at(i, name):
            if isinstance(i, int):
                if i == 0 and POS[name] > POS["dn1"]:
                    return POS[name] - 1
                if i == PAIRS:
                    return 0
            return POS[name]

        TAIL = ("xa0.0 O0/1 xa0.1 O1/1 xa0 xa1.0 O2/1 xa1.1 O3/1 SQ/1 xa1 f0.0 OT/1 f0.1 Y/1 f0 q0.0 q0.1 q0 "
                "dn1.0 dn1.1 dn1")
        ORDER = (TAIL + " D/0 v.0 L0/0 v.1 v0 L1/0 v.2 L2/0 v.3 v1 L3/0 r0 L4/0 i0 L5/0 lruA0 ga0.0 L6/0 ga0.1 ga0 KT/0 "
                 "lruB0 ma0.0 O0/0 ma0.1 ma0 O1/0 lruC0 gh0 r1 O2/0 i1 O3/0 lruA1 g0.0 SQ/0 g0.1 g0 lruB1 OT/0 mb0.0 mb0.1 "
                 "mb0 gb0 Y/0 f1.0 lruC1 f1.1 f1 q1.0 q1.1 q1 dn0.0 dn0.1 dn0 D/1 ga1.0 L0/1 ga1.1 ga1 L1/1 "
                 "ma1.0 L2/1 ma1.1 ma1 gh1 L3/1 g1.0 L4/1 g1.1 g1 L5/1 mb1.0 L6/1 mb1.1 KT/1 mb1 gb1").split()
        OF_LAST = {x for x in TAIL.split() if x.endswith("/1") or x.startswith("dn1")}

        def steps(i, run):
            for x in ORDER:
                if x in OF_LAST and ORDER.index(x) < len(TAIL.split()):
                    if not (isinstance(i, int) and i == 0):
                        run(x, i - 1)
                elif not (isinstance(i, int) and i == PAIRS):
                    run(x, i)

        with ExitStack() as ctx:
            def sb(name, shape, dt=F32):
                return ctx.enter_context(nc.sbuf_tensor(f"hy_{name}", shape, dt))[:]

            XA = sb("xa", [P, 2, SEQ])
            GM, Q, F, K, GB, TM = (sb(n, [P, SEQ]) for n in ("gm", "q", "f", "k", "gb", "tm"))
            V = sb("v", [P, MT, 2 * HG_DV])
            T1, T2, T3, T4 = (sb(n, [P, SEQ]) for n in ("t1", "t2", "t3", "t4"))
            TOT, SC = sb("totals", [P, SEQ]), sb("scores", [P, SEQ])
            KTT, ON = K, F
            yhi, ylo = sb("y_hi", [P, SEQ], F32R), sb("y_lo", [P, SEQ], F32R)
            WRI = sb("w_ri", [P, 2, 2, 2 * P])
            S = sb("state", [P, 2, HG_DV])
            oss, oms, osd, ors = (sb(n, [P, MT]) for n in ("o_ss", "o_ms", "o_sd", "o_rs"))
            s = {n: self.sem(f"hy_{n}") for n in (
                "wri_in", "xa_base", "conv", "q", "f", "kf", "v_mm", "v", "gates_mm", "r", "i",
                "lru_a", "lru_m", "lru_sd", "lru_u", "h", "ga", "ma", "gh", "g", "mb", "gb", "diag_mm", "sc0",
                "qp", "lev_mm", "lev", "pc", "kt_mm", "kt", "kv_mm", "s", "o_mm", "o_sq", "o_ms",
                "o_sd", "on", "ot_mm", "y", "y_hi", "y_lo", "down_mm", "down_add")}
            ahead = following(self.next_sem)
            tail = Lags(None, Norm(self.sem, "hy_next", c, V.rearrange("p (b m) v -> p b (m v)", b=2), T1, T2,
                                   (c.PA, c.PB), lambda m: (s["down_add"], (HG_HEADS - 1) * DOWN + 2 * m + 3)))
            TOT_AT = [None, 0, 512, 768, 896, 960, 992, 1008]
            block = ctx.enter_context(nc.Block())

            def phases(run):
                def of(eng):
                    steps(0, lambda x, i: run(x, i, 0))
                    with eng.Fori(1, PAIRS) as n:
                        steps(n, lambda x, i: run(x, i, n))
                    steps(PAIRS, lambda x, i: run(x, i, PAIRS))
                return of

            def tiles(x):
                return x.rearrange("p (m n) -> p m n", n=P)

            def halves(x, n, tiled=False):
                if tiled:
                    return x.rearrange("p (m b h n) -> p m b h n", m=MT, h=2, n=n)
                return x.rearrange("p (b h n) -> p b h n", h=2, n=n)

            TILES = {
                "xa0": (c.PA, "g", 2, 0), "xa1": (c.PB, "mb", 2, 0),
                "f0": (c.PA, "conv", 2, 1), "q0": (c.PB, "conv", 2, 2),
                "v0": (c.PA, "f", 2, 1), "v1": (c.PB, "q", 2, 1),
                "r0": (c.PA, "v", 2, 1), "i0": (c.PB, "v", 2, 2),
                "ga0": (c.PA, "r", 2, 1), "ma0": (c.PB, "i", 2, 1),
                "r1": (c.PA, "ga", 2, 1), "i1": (c.PB, "ma", 2, 1),
                "g0": (c.PA, "r", 2, 2), "mb0": (c.PB, "i", 2, 2),
                "f1": (c.PA, "g", 2, 1), "q1": (c.PB, "mb", 2, 1),
                "ga1": (c.PA, "f", 2, 2), "ma1": (c.PB, "q", 2, 2),
                "g1": (c.PA, "ga", 2, 2), "mb1": (c.PB, "ma", 2, 2),
            }
            COLS = {"xa": XA_, "q": Q_, "f": F_, "ga": GA_, "ma": MA_, "g": G_, "mb": MB_}
            TOT7 = TOT[:, TOT_AT[LEVELS]:TOT_AT[LEVELS] + MT]

            @block.sync
            def _(sp):
                def run(x, i, n):
                    if x[:-1] in COLS:
                        st.load(sp, n, at(n, x), W[:, :, ds(i * (2 * P) + (COLS[x[:-1]] + int(x[-1]) * P), P)], KT)
                    elif x in ("dn0", "dn1"):
                        st.load(sp, n, at(n, x), WO[:, ds(2 * i + int(x[-1]), 1), :].rearrange("p k n -> p (k n)"), 0)
                    elif x in ("v0", "v1"):
                        u = int(x[-1])
                        st.load(sp, n, at(n, x), W[:, 4 * u:4 * u + 4, ds(i * (2 * P) + V_, 2 * P)], 4)
                        if u == 0:
                            wait(sp, s["gates_mm"], 4 * i)
                            for w, src in enumerate((WR, WI)):
                                sp.dma_start(WRI[:, w, :, :], src[:, ds(i, 1), :, :].rearrange("p n j k -> p (n j) k"))\
                                  .then_inc(s["wri_in"], 16)
                phases(run)(sp)
                sp.wait_ge(s["h"], HG_HEADS)
                sp.dma_start(tail.norm.row, a["norm_mlp_2"][0].partition_broadcast(P))\
                  .then_inc(tail.norm.row_in, 16)
                ahead.early_load(sp, st)

            @block.gpsimd
            def _(pool):
                def run(x, i, n):
                    if x in POS:
                        st.divide(pool, n, at(n, x))
                phases(run)(pool)
                ahead.early_divide(pool, st, 1)

            @block.tensor
            def _(pe):
                pe.sem_inc(st.used, 1)
                KT_, QT, MT_ = tiles(K), tiles(Q), tiles(c.MM)

                def gate(which, j, pair):
                    for half in range(2):
                        cols = slice(half * HALF, (half + 1) * HALF)
                        for jj in range(2):
                            mm = pe.matmul(pair[:, cols], WRI[:, which, jj, j * P:(j + 1) * P],
                                           XA[:, jj, cols], start=(jj == 0), stop=(jj == 1))
                    mm.then_inc(s["gates_mm"], 1)

                def free(name, i):
                    _, by, per, before = TILES[name]
                    wait(pe, s[by], per * i + before)

                def down_half(i, n, j, half):
                    if half == 0:
                        pe.wait_ge(s["y_lo"], 2 * i + j + 1)

                    def some(tiles):
                        down_product(pe, c, st, n, (at(n, f"dn{j}"),), [(yhi, ylo)], s["down_mm"], s["down_add"],
                                     2 * i + j, 4, tiles)
                    if isinstance(n, int) and n == PAIRS:
                        if half:
                            tail.tensor(pe, lambda m: some((m,)))
                    else:
                        some(range(MT // 2 * half, MT // 2 * (half + 1)))

                def scores(hd, l):
                    if l == 0:
                        pe.wait_ge(s["qp"], hd + 1)
                    else:
                        pe.wait_ge(s["lev"], hd * LEVELS + l)
                        if l > 1:
                            pe.wait_ge(s["pc"], hd * LEVELS + l - 1)
                        else:
                            pe.wait_ge(s["sc0"], hd + 1)
                    bank = c.MM[:, (l % 2) * HALF:(l % 2 + 1) * HALF]
                    right = halves(Q, 1 << l, True)
                    for m in range(MT):
                        mm = pe.matmul(bank[:, m * (P // 2):(m + 1) * (P // 2)].rearrange(
                            "p (b n) -> p b n", n=1 << l), KT_[:, m, :], right[:, m, :, 1, :],
                            start=True, stop=True)
                    mm.then_inc(s["lev_mm"], 1)

                def outputs(i, j, q):
                    hd = 2 * i + j
                    VT = V[:, :, j * HG_DV:(j + 1) * HG_DV]
                    if q == 0:
                        pe.wait_ge(s["kt"], hd + 1)
                        pe.wait_ge(s["v"], 2 * i + 2)
                        pe.wait_ge(s["down_add"], hd * DOWN + 1)
                    for m in (2 * q, 2 * q + 1):
                        if m < MT - 1:
                            if m >= 2:
                                pe.wait_ge(s["s"], hd * (MT - 1) + m - 1)
                            pe.matmul(c.DD[:, (m % 2) * HALF:(m % 2) * HALF + HG_DV],
                                      tiles(KTT)[:, m, :], VT[:, m, :], start=True, stop=True)\
                                .then_inc(s["kv_mm"], 1)
                    for m in (2 * q, 2 * q + 1):
                        mm = pe.matmul(MT_[:, m, :], tiles(SC)[:, m, :], VT[:, m, :], start=True, stop=(m == 0))
                        if m:
                            pe.wait_ge(s["s"], hd * (MT - 1) + m)
                            mm = pe.matmul(MT_[:, m, :], QT[:, m, :], S[:, (m - 1) % 2, :],
                                           start=False, stop=True)
                        mm.then_inc(s["o_mm"], 1)

                def run(x, i, n):
                    name, _, half = x.partition(".")
                    if name in TILES and half:
                        if half == "0":
                            free(name, i)
                        columns_half(pe, c, st, n, at(n, name), TILES[name][0], int(half))
                    elif name == "v" and half:
                        q = int(half)
                        if q == 0:
                            pe.wait_ge(st.split, st.ready(n, at(n, "v1")))
                        if q % 2 == 0:
                            free(f"v{q // 2}", i)
                        for m in (2 * q, 2 * q + 1):
                            mm = rows_group(pe, c, row_parts(st, n, at(n, "v0")), (c.PA, c.PB)[q // 2], m, q // 2 * 4)
                        if q == 1:
                            mm.then_inc(s["v_mm"], 1)
                        if q == 3:
                            mm.then_inc(st.used, 2)
                    elif x in ("r0", "i0", "r1", "i1"):
                        if x == "r0":
                            pe.wait_ge(s["wri_in"], i * 32 + 32)
                            pe.wait_ge(s["conv"], 2 * i + 2)
                        free(x, i)
                        gate("ri".index(x[0]), int(x[1]), TILES[x][0])
                    elif name in ("dn0", "dn1") and half:
                        down_half(i, n, int(name[-1]), int(half))
                    elif "/" in x:
                        what, j = x.split("/")
                        hd = 2 * i + int(j)
                        if what == "D":
                            pe.wait_ge(s["kf"], hd + 1)
                            pe.wait_ge(s["q"], hd + 1)
                            pe.wait_ge(s["down_add"], hd * DOWN + 1)
                            for m in range(MT):
                                mm = pe.matmul(MT_[:, m, :], KT_[:, m, :], QT[:, m, :], start=True, stop=True)
                            mm.then_inc(s["diag_mm"], 1)
                        elif what[0] == "L":
                            scores(hd, int(what[1:]))
                        elif what == "KT":
                            pe.wait_ge(s["lev"], (hd + 1) * LEVELS)
                            pe.wait_ge(s["pc"], (hd + 1) * LEVELS)
                            for m in range(MT):
                                mm = pe.transpose(MT_[:, m, :], KT_[:, m, :], c.ident)
                            mm.then_inc(s["kt_mm"], 1)
                        elif what == "OT":
                            pe.wait_ge(s["on"], hd + 1)
                            for m in range(MT):
                                mm = pe.transpose(MT_[:, m, :], tiles(ON)[:, m, :], c.ident)
                            mm.then_inc(s["ot_mm"], 1)
                        elif what[0] == "O":
                            outputs(i, int(j), int(what[1:]))
                phases(run)(pe)

            @block.scalar
            def _(act):

                def run(x, i, n):
                    kind, j = x[:-1], (int(x[-1]) if x[-1].isdigit() else 0)
                    hd = 2 * i + j

                    def par(col):
                        return c.par[:, ds(2 * i + (col + j), 1)]

                    if "." in x:
                        return
                    pair = TILES[x][0] if x in TILES else None
                    if x in POS:
                        if x != "v0":
                            if x not in ("dn0", "dn1"):
                                act.wait_ge(st.used, st.done(n, at(n, x)))
                    if kind == "xa":
                        wait(act, s["lru_u"], 2 * i)
                        act.activation(XA[:, j, :], pair, ACT.Identity, bias=par(C_CB), scale=par(C_CW + 24))\
                           .then_inc(s["xa_base"], 1)
                    elif kind == "q":
                        wait(act, s["o_mm"], hd * MT)
                        act.activation(Q, pair, ACT.Silu).then_inc(s["q"], 1)
                    elif kind == "f":
                        wait(act, s["ot_mm"], hd)
                        act.activation(F, pair, ACT.Sigmoid)
                        act.activation(K, pair, ACT.Sigmoid, scale=-1.0).then_inc(s["f"], 1)
                    elif kind == "v":
                        if j == 0:
                            act.wait_ge(s["v_mm"], i + 1)
                        act.copy(V[:, 4 * j:4 * j + 4, :], pair.rearrange("p (m v) -> p m v", v=2 * HG_DV))\
                           .then_inc(s["v"], 1)
                    elif kind == "r":
                        act.wait_ge(s["gates_mm"], 4 * i + 2 * j + 1)
                        wait(act, s["h"], hd)
                        act.activation(T1, pair, ACT.Sigmoid, bias=par(C_BR)).then_inc(s["r"], 1)
                    elif kind == "i":
                        act.wait_ge(s["gates_mm"], 4 * i + 2 * j + 2)
                        act.activation(T2, pair, ACT.Sigmoid, bias=par(C_BI)).then_inc(s["i"], 1)
                    elif kind == "lruA":
                        act.drain()
                        wait(act, s["gh"], hd)
                        act.activation(T3, T1, ACT.Tanh, scale=c.decay[:, 1, ds(2 * i + j, 1)])
                        act.drain()
                        act.activation(T1, T1, ACT.Exp, scale=c.decay[:, 0, ds(2 * i + j, 1)])\
                            .then_inc(s["lru_a"], 1)
                    elif kind == "lruB":
                        act.wait_ge(s["lru_m"], hd + 1)
                        act.activation(T3, T3, ACT.Sqrt).then_inc(s["lru_sd"], 1)
                    elif kind == "ga":
                        wait(act, s["y"], hd)
                        act.activation(GM, pair, ACT.Gelu_apprx_tanh).then_inc(s["ga"], 1)
                    elif kind == "ma":
                        wait(act, s["gb"], hd)
                        act.activation(TM, pair, ACT.Sigmoid).then_inc(s["ma"], 1)
                    elif kind == "g":
                        wait(act, s["y"], hd)
                        act.activation(GB, pair, ACT.Silu).then_inc(s["g"], 1)
                    elif kind == "mb":
                        act.wait_ge(s["gh"], hd + 1)
                        act.activation(TM, pair, ACT.Sigmoid).then_inc(s["mb"], 1)
                    elif kind == "SQ/":
                        act.wait_ge(s["o_mm"], (hd + 1) * MT)
                        act.activation(SC, c.MM, ACT.Square).then_inc(s["o_sq"], 1)
                        act.wait_ge(s["o_ms"], hd + 1)
                        act.activation(osd, oms, ACT.Sqrt).then_inc(s["o_sd"], 1)
                    elif kind == "Y/":
                        act.wait_ge(s["y"], hd + 1)
                        act.copy(yhi, SC).then_inc(s["y_hi"], 1)
                phases(run)(act)
                tail.scalar(act)

            @block.vector
            def _(dve):
                dve.sem_inc(s["down_add"], 1)

                def run(x, i, n):
                    name, _, half = x.partition(".")
                    kind, j = x[:-1], (int(x[-1]) if x[-1].isdigit() else 0)
                    hd = 2 * i + j

                    def par(col):
                        return c.par[:, ds(2 * i + (col + j), 1)]

                    if name in ("dn0", "dn1") and half:
                        def some(tiles):
                            add_down(dve, c, st, s["down_mm"], s["down_add"], n, at(n, name), 2 * i + int(name[-1]),
                                     4, tiles)
                        if isinstance(n, int) and n == PAIRS:
                            if int(half):
                                tail.vector(dve, lambda m: some((m,)))
                        else:
                            some(range(MT // 2 * int(half), MT // 2 * (int(half) + 1)))
                    elif half:
                        return
                    elif kind == "xa":
                        dve.wait_ge(s["xa_base"], hd + 1)
                        for tap in (2, 1, 0):
                            lag = 3 - tap
                            mm = dve.scalar_tensor_tensor(
                                out=XA[:, j, lag:SEQ], in0=TILES[x][0][:, 0:SEQ - lag], scalar=par(C_CW + 8 * tap),
                                in1=XA[:, j, lag:SEQ], op0=ALU.mult, op1=ALU.add)
                            if tap:
                                dve.drain()
                        mm.then_inc(s["conv"], 1)
                    elif kind == "f":
                        lb, rest = (c.lb[:, q, ds(2 * i + j, 1)] for q in range(2))
                        dve.wait_ge(s["f"], hd + 1)
                        dve.tensor_scalar(F, F, rest, lb, ALU.mult, ALU.add)
                        dve.tensor_scalar(K, K, rest, None, ALU.mult)
                        dve.drain()
                        dve.tensor_scalar(F, F, F_MIN, None, ALU.max).then_inc(s["kf"], 1)
                    elif kind == "lruA":
                        dve.wait_ge(s["lru_a"], hd + 1)
                        dve.tensor_tensor(T4, T1, T1, ALU.mult)
                        dve.drain()
                        dve.scalar_tensor_tensor(out=T3, in0=T4, scalar=1.0, in1=T3, op0=ALU.add, op1=ALU.mult)
                        dve.drain()
                        dve.tensor_scalar(T3, T3, 0.0, None, ALU.max).then_inc(s["lru_m"], 1)
                        dve.wait_ge(s["i"], hd + 1)
                        dve.tensor_tensor(T2, T2, XA[:, j, :], ALU.mult).then_inc(s["lru_u"], 1)
                    elif kind == "lruC":
                        dve.wait_ge(s["lru_u"], hd + 1)
                        dve.wait_ge(s["lru_sd"], hd + 1)
                        dve.tensor_tensor(T2, T2, T3, ALU.mult)
                        dve.drain()
                        dve.tensor_tensor_scan(T3, T1, T2, 0.0, ALU.mult, ALU.add).then_inc(s["h"], 1)
                    elif kind == "gh":
                        dve.wait_ge(s["ma"], hd + 1)
                        dve.tensor_tensor(GM, GM, TM, ALU.mult)
                        dve.drain()
                        dve.wait_ge(s["h"], hd + 1)
                        dve.tensor_tensor(GM, GM, T3, ALU.mult).then_inc(s["gh"], 1)
                    elif kind == "gb":
                        dve.wait_ge(s["mb"], hd + 1)
                        dve.scalar_tensor_tensor(out=GB, in0=GB, scalar=c.par[:, C_HGN:C_HGN + 1], in1=TM,
                                                 op0=ALU.mult, op1=ALU.mult).then_inc(s["gb"], 1)
                    elif kind == "D/":
                        dve.wait_ge(s["diag_mm"], hd + 1)
                        dve.tensor_tensor(tiles(SC), tiles(c.MM), c.ident.unsqueeze(1).broadcast_to([P, MT, P]),
                                          ALU.mult).then_inc(s["sc0"], 1)
                        dve.tensor_tensor(Q, Q, F, ALU.mult).then_inc(s["qp"], 1)
                    elif kind[0] == "L":
                        level(hd, int(kind[1:-1]))
                    elif kind == "KT/":
                        dve.wait_ge(s["kt_mm"], hd + 1)
                        dve.tensor_copy(KTT, c.MM).then_inc(s["kt"], 1)
                    elif kind == "OT/":
                        return
                    elif kind[0] == "O":
                        for m in (2 * int(kind[1:-1]), 2 * int(kind[1:-1]) + 1):
                            if m < MT - 1:
                                state(hd, m)
                    elif kind == "SQ/":
                        dve.wait_ge(s["o_sq"], hd + 1)
                        dve.tensor_reduce(oss, tiles(SC), AX, ALU.add)
                        dve.drain()
                        dve.tensor_scalar(oms, oss, 1.0 / HG_DV, EPS, ALU.mult, ALU.add).then_inc(s["o_ms"], 1)
                        dve.wait_ge(s["o_sd"], hd + 1)
                        dve.reciprocal(ors, osd)
                        dve.drain()
                        dve.tensor_tensor(tiles(ON), tiles(c.MM), ors.unsqueeze(2).broadcast_to([P, MT, HG_DV]),
                                          ALU.mult).then_inc(s["on"], 1)
                    elif kind == "Y/":
                        dve.drain()
                        dve.wait_ge(s["ot_mm"], hd + 1)
                        dve.tensor_tensor(SC, c.MM, GB, ALU.mult)
                        dve.drain()
                        dve.tensor_tensor(SC, SC, GM, ALU.add).then_inc(s["y"], 1)
                        dve.wait_ge(s["y_hi"], hd + 1)
                        dve.tensor_tensor(ylo, SC, yhi.bitcast(F32), ALU.subtract).then_inc(s["y_lo"], 1)

                def level(hd, l):
                    nb, w = SEQ // (2 << l), 1 << l
                    tot = F if l == 0 else TOT[:, TOT_AT[l]:TOT_AT[l] + 2 * nb]
                    left, right = (tot.rearrange("p (b h) -> p b h", h=2)[:, :, q] for q in range(2))
                    dve.drain()
                    dve.wait_ge(s["lev_mm"], hd * LEVELS + l + 1)
                    dve.tensor_tensor(halves(Q, w)[:, :, 1, :], halves(Q, w)[:, :, 1, :],
                                      left.unsqueeze(2).broadcast_to([P, nb, w]), ALU.mult)
                    dve.tensor_tensor(halves(K, w)[:, :, 0, :], halves(K, w)[:, :, 0, :],
                                      right.unsqueeze(2).broadcast_to([P, nb, w]), ALU.mult)
                    dve.tensor_tensor(TOT[:, TOT_AT[l + 1]:TOT_AT[l + 1] + nb], left, right, ALU.mult)\
                       .then_inc(s["lev"], 1)
                    bank = c.MM[:, (l % 2) * HALF:(l % 2 + 1) * HALF]
                    dve.copy_predicated(
                        halves(SC, w, True)[:, :, :, 1, :],
                        c.masks[:, l, :].rearrange("p (b n) -> p b n", n=w).unsqueeze(1).broadcast_to(
                            [P, MT, P // (2 * w), w]),
                        bank.rearrange("p (m b n) -> p m b n", m=MT, n=w)).then_inc(s["pc"], 1)

                def state(hd, m):
                    dve.wait_ge(s["kv_mm"], hd * (MT - 1) + m + 1)
                    wait(dve, s["o_mm"], hd * MT + m)
                    ps = c.DD[:, (m % 2) * HALF:(m % 2) * HALF + HG_DV]
                    if m == 0:
                        dve.tensor_copy(S[:, 0, :], ps).then_inc(s["s"], 1)
                    else:
                        dve.wait_ge(s["s"], hd * (MT - 1) + m)
                        dve.scalar_tensor_tensor(out=S[:, m % 2, :], in0=S[:, (m - 1) % 2, :],
                                                 scalar=TOT7[:, m:m + 1], in1=ps, op0=ALU.mult,
                                                 op1=ALU.add).then_inc(s["s"], 1)
                phases(run)(dve)


def build(nc, a):
    with ExitStack() as ctx:
        p = Program(nc, ctx, a)
        f1 = ("f1", p.core, a["ffn_w_up"][0], FT // 2, True)
        f2 = ("f2", p.core, a["w_up_2"][0], D_FF // (2 * P), False)
        streams = {}

        def stream_of(name, make):
            def of(sem):
                streams[name] = make(sem)
                return streams[name]
            return of

        p.parameters()
        p.end_stage()
        p.gla(stream_of("f1", lambda sem: p.ffn_stream(sem, *f1)))
        p.end_stage()
        p.ffn("f1", streams["f1"], a["ffn_w_up"][0], a["ffn_w_down"][0], FT // 2, True,
              stream_of("hy", lambda sem: p.hybrid_stream(sem, p.core, a["w_in_2"][0])),
              [a["final_norm_w"], a["norm_mix_2"][0]])
        p.end_stage()
        p.hybrid(streams["hy"], stream_of("f2", lambda sem: p.ffn_stream(sem, *f2)))
        p.end_stage()
        p.ffn("f2", streams["f2"], a["w_up_2"][0], a["w_down_2"][0], D_FF // (2 * P), False, None,
              [a["norm_final_2"]])
        p.end_stage()


_INS = ["x", "mix_norm_w", "ffn_norm_w", "final_norm_w", "gla_w_in", "gla_w_gate2", "gla_b_gate",
        "gla_norm_w", "gla_w_out", "ffn_w_up", "ffn_conv_w", "ffn_conv_b", "ffn_w_down",
        "lb_logits_2", "norm_mix_2", "w_in_2", "conv_w_2", "conv_b_2", "w_r_2", "b_r_2", "w_i_2",
        "b_i_2", "lam_2", "hg_norm_2", "w_out_2", "norm_mlp_2", "w_up_2", "w_down_2", "norm_final_2"]


def kernel(**inputs):
    import numpy as _np
    import concourse.bacc as _bacc
    from concourse import mybir as _mybir
    from concourse.bass_utils import run_bass_kernel_spmd as _run

    nc = _bacc.Bacc("TRN2", target_bir_lowering=False, num_devices=1)
    arrays, aps = {}, {}
    for name in _INS:
        arrays[f"in_{name}"] = _np.ascontiguousarray(inputs[name])
    arrays["in_ident"] = _np.eye(P, dtype=_np.float32)
    masks = _np.zeros((P, LEVELS, P // 2), _np.float32)
    for l in range(LEVELS):
        n = 1 << l
        for t in range(P // 2):
            at = (t // n) * 2 * n
            masks[at:at + n, l, t] = 1
    arrays["in_masks"] = masks
    for name, x in arrays.items():
        aps[name[3:]] = nc.dram_tensor(name, x.shape, _mybir.dt.from_np(x.dtype), kind="ExternalInput").ap()
    aps["out"] = nc.dram_tensor("out", (1, SEQ, D), _mybir.dt.float32, kind="ExternalOutput").ap()
    build(nc, aps)
    r = _run(nc, [arrays], core_ids=[0])
    return r.results[0]["out"]
```
